# Optimizing a Trainium2 kernel written in Bass

```python
import math
import jax, jax.numpy as jnp
from jax import lax
import numpy as np

D_MODEL = 1024
BATCH = 1
SEQ = 256
DEPTH = 1

ATT_HEADS = 8
ATT_HEAD_DIM = 64
ATT_WIDTH = ATT_HEADS * ATT_HEAD_DIM
MOBA_BLOCK = 256
MOBA_TOPK = 3
MOBA_QBLOCK = 16
ROPE_THETA = 10000.0
HGRN_HEADS = 4
HGRN_KEY_DIM = 128
HGRN_VAL_DIM = 128
HGRN_FDIM = HGRN_HEADS * HGRN_KEY_DIM
HGRN_VDIM = HGRN_HEADS * HGRN_VAL_DIM
HGRN_CHUNK = 64
N_EXPERTS = 32
TOP_K = 4
D_EXPERT = 1024
SWIGLU_LIMIT = 7.0
SWIGLU_ALPHA = 1.702
MOE_BLOCK = 128
RMS_EPS = 1e-6
NEG = -1e30

IN_WIDTHS = [ATT_WIDTH, ATT_WIDTH, ATT_WIDTH,
             HGRN_FDIM, HGRN_FDIM, HGRN_VDIM, HGRN_VDIM,
             D_MODEL, D_MODEL]
D_IN = sum(IN_WIDTHS)
IN_SPLITS = list(np.cumsum(IN_WIDTHS)[:-1].tolist())

kernel_name = 'hybrid_moba_hgrn2_moe_block'

def rmsnorm(x, w):
    xf = x.astype(jnp.float32)
    y = xf * lax.rsqrt(jnp.mean(xf * xf, axis=-1, keepdims=True) + RMS_EPS)
    return (y * w.astype(jnp.float32)).astype(x.dtype)

def apply_rope(t, pos):
    dh = t.shape[-1]
    half = dh // 2
    inv = ROPE_THETA ** (-(jnp.arange(half, dtype=jnp.float32) * 2.0 / dh))
    ang = pos.astype(jnp.float32)[:, None] * inv[None, :]
    cos, sin = jnp.cos(ang), jnp.sin(ang)
    tf = t.astype(jnp.float32)
    t1, t2 = tf[..., :half], tf[..., half:]
    out = jnp.concatenate([t1 * cos - t2 * sin, t2 * cos + t1 * sin], axis=-1)
    return out.astype(t.dtype)

def moba_attention(q, k, v):
    B, H, S, Dh = q.shape
    nb = -(-S // MOBA_BLOCK)
    pad = nb * MOBA_BLOCK - S
    kp = jnp.pad(k, ((0, 0), (0, 0), (0, pad), (0, 0)))
    vp = jnp.pad(v, ((0, 0), (0, 0), (0, pad), (0, 0)))
    kb = kp.reshape(B, H, nb, MOBA_BLOCK, Dh)
    vb = vp.reshape(B, H, nb, MOBA_BLOCK, Dh)
    cnt = jnp.minimum(S - jnp.arange(nb) * MOBA_BLOCK, MOBA_BLOCK).astype(jnp.float32)
    kmean = kb.astype(jnp.float32).sum(axis=3) / cnt[None, None, :, None]
    k_sel = min(MOBA_TOPK, nb)
    scale = Dh ** -0.5
    bi = jnp.arange(B)[:, None, None, None]
    hi = jnp.arange(H)[None, :, None, None]

    def one_qblock(qi):
        q0 = qi * MOBA_QBLOCK
        qblk = lax.dynamic_slice_in_dim(q, q0, MOBA_QBLOCK, axis=2).astype(jnp.float32)
        cur = q0 // MOBA_BLOCK
        qpos = q0 + jnp.arange(MOBA_QBLOCK)
        gate = jnp.einsum('bhqd,bhnd->bhqn', qblk, kmean)
        gate = jnp.where(jnp.arange(nb)[None, None, None, :] < cur, gate, NEG)
        _, sel = lax.top_k(gate, k_sel)
        sel_ok = sel < cur
        ks = kb[bi, hi, sel]
        vs = vb[bi, hi, sel]
        s_sel = jnp.einsum('bhqd,bhqjkd->bhqjk', qblk, ks) * scale
        s_sel = jnp.where(sel_ok[..., None], s_sel, NEG).reshape(B, H, MOBA_QBLOCK, k_sel * MOBA_BLOCK)
        ko = lax.dynamic_slice_in_dim(kp, cur * MOBA_BLOCK, MOBA_BLOCK, axis=2)
        vo = lax.dynamic_slice_in_dim(vp, cur * MOBA_BLOCK, MOBA_BLOCK, axis=2)
        kpos = cur * MOBA_BLOCK + jnp.arange(MOBA_BLOCK)
        s_own = jnp.einsum('bhqd,bhkd->bhqk', qblk, ko) * scale
        s_own = jnp.where(kpos[None, :] <= qpos[:, None], s_own, NEG)
        p = jax.nn.softmax(jnp.concatenate([s_sel, s_own], axis=-1), axis=-1)
        p_sel = p[..., :k_sel * MOBA_BLOCK].reshape(B, H, MOBA_QBLOCK, k_sel, MOBA_BLOCK)
        p_own = p[..., k_sel * MOBA_BLOCK:]
        out = (jnp.einsum('bhqjk,bhqjkd->bhqd', p_sel, vs)
               + jnp.einsum('bhqk,bhkd->bhqd', p_own, vo))
        return out.astype(q.dtype)

    outs = lax.map(one_qblock, jnp.arange(S // MOBA_QBLOCK))
    return outs.transpose(1, 2, 0, 3, 4).reshape(B, H, S, Dh)

def hgrn2(q_in, f_in, i_in, g_in, lb, norm_w):
    B, S, _ = q_in.shape
    H, dk, dv, C = HGRN_HEADS, HGRN_KEY_DIM, HGRN_VAL_DIM, HGRN_CHUNK
    nc = S // C
    qf = jax.nn.silu(q_in.astype(jnp.float32))
    f = lb.astype(jnp.float32) + (1.0 - lb.astype(jnp.float32)) * jax.nn.sigmoid(f_in.astype(jnp.float32))
    logf = jnp.log(f)
    kf = 1.0 - f
    iv = i_in.astype(jnp.float32)

    def to_chunks(t, d):
        return t.reshape(B, nc, C, H, d).transpose(1, 0, 3, 2, 4)

    causal = jnp.tril(jnp.ones((C, C), dtype=bool))

    def step(state, xs):
        qc, kc, ic, lc = xs
        b = jnp.cumsum(lc, axis=2)
        diff = b[:, :, :, None, :] - b[:, :, None, :, :]
        decay = jnp.exp(jnp.where(causal[None, None, :, :, None], diff, -jnp.inf))
        attn = jnp.einsum('bhtd,bhsd,bhtsd->bhts', qc, kc, decay)
        o = (jnp.einsum('bhts,bhsv->bhtv', attn, ic)
             + jnp.einsum('bhtd,bhdv->bhtv', qc * jnp.exp(b), state))
        b_last = b[:, :, -1:, :]
        state = (jnp.exp(b_last[:, :, 0, :])[..., None] * state
                 + jnp.einsum('bhsd,bhsv->bhdv', kc * jnp.exp(b_last - b), ic))
        return state, o

    s0 = jnp.zeros((B, H, dk, dv), jnp.float32)
    _, o = lax.scan(step, s0, (to_chunks(qf, dk), to_chunks(kf, dk), to_chunks(iv, dv), to_chunks(logf, dk)))
    o = o.transpose(1, 0, 3, 2, 4).reshape(B, S, H, dv)
    o = o * lax.rsqrt(jnp.mean(o * o, axis=-1, keepdims=True) + RMS_EPS)
    o = o * norm_w.astype(jnp.float32).reshape(H, dv)
    o = o.reshape(B, S, H * dv) * jax.nn.silu(g_in.astype(jnp.float32))
    return o.astype(q_in.dtype)

def moe_ffn(h, router_w, router_b, w_gate_up, b_gate_up, w_down, b_down):
    B, S, D = h.shape
    T = B * S
    A = T * TOP_K
    hf = h.reshape(T, D)
    logits = (hf @ router_w).astype(jnp.float32) + router_b.astype(jnp.float32)
    top_v, top_e = lax.top_k(logits, TOP_K)
    top_w = jax.nn.softmax(top_v, axis=-1)
    e_flat = top_e.reshape(A)
    w_flat = top_w.reshape(A)
    tok_flat = jnp.repeat(jnp.arange(T, dtype=jnp.int32), TOP_K)
    order = jnp.argsort(e_flat)
    e_sorted = e_flat[order]
    counts = jnp.bincount(e_flat, length=N_EXPERTS)
    start = jnp.cumsum(counts) - counts
    padded = (counts + MOE_BLOCK - 1) // MOE_BLOCK * MOE_BLOCK
    pend = jnp.cumsum(padded)
    pstart = pend - padded
    dest = pstart[e_sorted] + (jnp.arange(A) - start[e_sorted])
    P = A + N_EXPERTS * MOE_BLOCK
    nblk = P // MOE_BLOCK
    row_tok = jnp.zeros((P,), jnp.int32).at[dest].set(tok_flat[order])
    row_w = jnp.zeros((P,), jnp.float32).at[dest].set(w_flat[order])
    blk_e = jnp.minimum(jnp.sum((jnp.arange(nblk) * MOE_BLOCK)[:, None] >= pend[None, :], axis=1), N_EXPERTS - 1)
    xg = hf[row_tok].reshape(nblk, MOE_BLOCK, D)

    def expert_block(args):
        xb, e = args
        gu = xb @ w_gate_up[e] + b_gate_up[e]
        gate = jnp.minimum(gu[:, 0::2], SWIGLU_LIMIT)
        up = jnp.clip(gu[:, 1::2], -SWIGLU_LIMIT, SWIGLU_LIMIT)
        glu = gate * jax.nn.sigmoid(gate * SWIGLU_ALPHA)
        return ((up + 1.0) * glu) @ w_down[e] + b_down[e]

    yg = lax.map(expert_block, (xg, blk_e)).reshape(P, D)
    out = jnp.zeros((T, D), jnp.float32).at[row_tok].add(yg.astype(jnp.float32) * row_w[:, None])
    return out.astype(h.dtype).reshape(B, S, D)

def setup_inputs(seed: int = 0) -> dict:
    key = jax.random.key(seed)
    ks = jax.random.split(key, 16)
    f32 = jnp.float32
    nrm = lambda k, shape, s: jax.random.normal(k, shape, f32) * s
    return {
        'x': jax.random.normal(ks[0], (BATCH, SEQ, D_MODEL), f32),
        'norm1_w': 1.0 + nrm(ks[1], (DEPTH, D_MODEL), 0.02),
        'w_in': nrm(ks[2], (DEPTH, D_MODEL, D_IN), D_MODEL ** -0.5),
        'moba_up': nrm(ks[3], (DEPTH, ATT_WIDTH, D_MODEL), ATT_WIDTH ** -0.5),
        'hgrn_lb_logits': nrm(ks[4], (DEPTH + 1, HGRN_FDIM), 0.1),
        'hgrn_norm_w': 1.0 + nrm(ks[5], (DEPTH, HGRN_VDIM), 0.02),
        'hgrn_up': nrm(ks[6], (DEPTH, HGRN_VDIM, D_MODEL), HGRN_VDIM ** -0.5),
        'w_out': nrm(ks[7], (DEPTH, D_MODEL, D_MODEL), D_MODEL ** -0.5),
        'norm2_w': 1.0 + nrm(ks[8], (DEPTH, D_MODEL), 0.02),
        'router_w': nrm(ks[9], (DEPTH, D_MODEL, N_EXPERTS), D_MODEL ** -0.5),
        'router_b': nrm(ks[10], (DEPTH, N_EXPERTS), 0.01),
        'w_gate_up': nrm(ks[11], (DEPTH, N_EXPERTS, D_MODEL, 2 * D_EXPERT), D_MODEL ** -0.5),
        'b_gate_up': nrm(ks[12], (DEPTH, N_EXPERTS, 2 * D_EXPERT), 0.01),
        'w_down': nrm(ks[13], (DEPTH, N_EXPERTS, D_EXPERT, D_MODEL), D_EXPERT ** -0.5),
        'b_down': nrm(ks[14], (DEPTH, N_EXPERTS, D_MODEL), 0.01),
        'final_norm_w': 1.0 + nrm(ks[15], (D_MODEL,), 0.02),
    }

def reference(x, norm1_w, w_in, moba_up, hgrn_lb_logits, hgrn_norm_w, hgrn_up, w_out,
              norm2_w, router_w, router_b, w_gate_up, b_gate_up, w_down, b_down, final_norm_w):
    B, S, D = x.shape
    pos = jnp.arange(S, dtype=jnp.int32)
    lb_table = jnp.cumsum(jax.nn.softmax(hgrn_lb_logits.astype(jnp.float32), axis=0), axis=0)

    def heads(t):
        return t.reshape(B, S, ATT_HEADS, ATT_HEAD_DIM).transpose(0, 2, 1, 3)

    for l in range(DEPTH):
        h = rmsnorm(x, norm1_w[l])
        proj = h @ w_in[l]
        q_a, k_a, v_a, q_b, f_b, i_b, g_b, gate_a, gate_b = jnp.split(proj, IN_SPLITS, axis=-1)
        q_a = apply_rope(heads(q_a), pos)
        k_a = apply_rope(heads(k_a), pos)
        y_a = moba_attention(q_a, k_a, heads(v_a)).transpose(0, 2, 1, 3).reshape(B, S, ATT_WIDTH)
        y_b = hgrn2(q_b, f_b, i_b, g_b, lb_table[l], hgrn_norm_w[l])
        mixed = (jax.nn.sigmoid(gate_a) * (y_a @ moba_up[l])
                 + jax.nn.sigmoid(gate_b) * (y_b @ hgrn_up[l]))
        x = x + mixed @ w_out[l]
        h2 = rmsnorm(x, norm2_w[l])
        x = x + moe_ffn(h2, router_w[l], router_b[l], w_gate_up[l], b_gate_up[l], w_down[l], b_down[l])
    return rmsnorm(x, final_norm_w)


_drawn_inputs = setup_inputs


def setup_inputs(seed=0):
    import zlib

    import numpy as np

    out = dict(_drawn_inputs(seed))
    spreads = {}
    factors = {'hgrn_lb_logits': 3.13,
     'hgrn_norm_w': 2.697,
     'b_gate_up': 8.0,
     'b_down': 8.0,
     'final_norm_w': 2.867}
    for name, (base, spread) in spreads.items():
        noise = np.random.default_rng([zlib.crc32(name.encode()), seed]).standard_normal(out[name].shape)
        drawn = base * np.exp(spread * noise) if base else spread * noise
        out[name] = __import__('jax').numpy.asarray(drawn.astype(out[name].dtype))
    for name, factor in factors.items():
        out[name] = (out[name] * factor).astype(out[name].dtype)
    return out
```

```python
import concourse.bass as bass
from concourse import mybir
from contextlib import ExitStack

F32 = mybir.dt.float32
I32 = mybir.dt.int32
ALU = mybir.AluOpType
ACT = mybir.ActivationFunctionType
AX = mybir.AxisListType

P = 128
T = 256
TT = T // P
D = 1024
KD = D // P
HEADS, DH = 8, 64
GH, GK = 4, 128
CHUNK = 64
E = 32
TOPK = 4
CAP = 64
ROUNDS = T // CAP
DE = 1024
LIMIT, ALPHA = 7.0, 1.702
EPS = 1e-6
NEG = -1e30
BANKS = 8
SCALE = DH ** -0.5
GROUP = 512
RING = 3
QA, KA, VA, QB, FB, IB, GB, GA0, GA1, GB0, GB1 = range(11)
LEVELS = [6, 5, 4, 3, 2, 1, 0]
NMASK = 8
DIAG = 7

LOADS = [FB, QB, QA, KA, VA, IB, GB, GA0, GA1, GB0, GB1, "mu", "hu", "wo0", "wo1"]


def bank_units():
    u = [("rows", "dve")] + [(f"xT{j}", "dve") for j in range(4)]
    u += [("f0", "act"), ("f1", "act"), ("q0", "dve"), ("q1", "dve")]
    u += [("qa0", "act"), ("qa1", "act"), ("ka0", "act"), ("ka1", "act")]
    lev = [("D0", "dve"), ("D1", "dve"), ("X", "dve")]
    for lv in LEVELS:
        lev += [(f"L{lv}0", "dve"), (f"L{lv}1", "dve")]
    u += lev[:5] + [("va0", "act")] + lev[5:9] + [("va1", "act")] + lev[9:13] + [("ib0", "act")]
    u += lev[13:] + [("ib1", "act")]
    u += [("qT0", "act"), ("qT1", "act"), ("kT0", "act"), ("kT1", "act")]
    fill = ["g0", "g1", "ga0", "ga1", "ga2", "ga3", "gb0", "gb1", "gb2", "gb3"]
    for h in range(HEADS):
        u += [(f"sc{h}", "dve"), (fill[h], "act")]
        if h >= 1:
            u += [(f"pT{h - 1}", "act")]
    u += [("o0", "act"), ("o1", "act"), (fill[8], "act"), ("pT7", "act"), ("ms0", "act"), ("ms1", "act")]
    u += [(fill[9], "act"), ("ya0", "act"), ("ya1", "act")]
    u += [(f"mu{j}", "dve") for j in range(4)] + [(f"hu{j}", "dve") for j in range(4)]
    u += [(f"wo{tt}{n}", "dve") for n in range(2) for tt in range(2)]
    u += [(f"h2T{j}", "dve") for j in range(4)] + [("rt", "dve"), ("pos", "dve"), ("wT", "dve")]
    return u


UNITS = bank_units()
AT_UNIT = {name: n for n, (name, _) in enumerate(UNITS)}


def drained(name):
    n = AT_UNIT[name]
    who = UNITS[n][1]
    return who, sum(1 for _, w in UNITS[:n + 1] if w == who)


class Steps:

    def __init__(self, eng, own):
        self.eng, self.own, self.count, self.last = eng, own, {}, None

    def did(self, ins, sem=None, by=1):
        sem = self.own if sem is None else sem
        key = sem.name
        self.count[key] = self.count.get(key, 0) + by
        ins.then_inc(sem, by)
        self.last = (sem, self.count[key])

    def settle(self):
        self.eng.wait_ge(*self.last)


def hybrid_block(nc, A, out):
    ctx = ExitStack()
    with ctx:
        def sb(name, shape, dt=F32):
            return ctx.enter_context(nc.sbuf_tensor(name, shape, dt))

        def sem(name):
            return ctx.enter_context(nc.semaphore(name))

        X = sb("X", [P, TT, D])
        XN = sb("XN", [P, TT, D])
        HT = sb("HT", [P, KD, T])
        CST = sb("CST", [P, 1152])
        MSK = sb("MSK", [P, NMASK, P], I32)
        ROWS = sb("ROWS", [32, P])
        COLS = sb("COLS", [P, 32])
        SMALL = sb("SMALL", [P, 640])
        ident, ucum = CST[:, 0:128], CST[:, 128:256]
        iota = CST[:, 256:384]
        amask = CST[:, 384:768]
        rcos = CST[:, 768:832].rearrange("p (t c) -> p t c", t=TT)
        rsin = CST[:, 832:896].rearrange("p (t c) -> p t c", t=TT)
        ohtab = CST[0:E, 896:896 + E + 1]
        ones = CST[:, 1024:1152]

        QKT = sb("QKT", [P, 2, 4, T])
        qT, kT = QKT[:, 0], QKT[:, 1]
        yaT = QKT[:, 0]
        VI = sb("VI", [P, 2, TT, 512])
        va, ib = VI[:, 0], VI[:, 1]
        mixT = VI[:].rearrange("p a t n -> p (a t n)").rearrange("p (k t) -> p k t", k=KD)
        SM = sb("SM", [P, 2, 384])

        WR = sb("WR", [P, RING, 4096])
        wr8 = [WR[:, s, :].rearrange("p (k n) -> p k n", k=KD) for s in range(RING)]
        wr4 = [WR[:, s, :].rearrange("p (k n) -> p k n", k=4) for s in range(RING)]

        S = sb("S", [P, 6, 4096])
        SF = S[:].rearrange("p s n -> p (s n)")

        def page(n, c=1):
            return SF[:, 1024 * n:1024 * (n + c)]

        qraw, kraw, rt1, rt2 = page(0), page(1), page(2), page(3)
        qs, kf, bcum, sgq = page(4), page(5), page(6), page(7)
        DD = [page(8), page(9)]
        KQ = [page(10), page(11)]
        KX = page(12)
        logf = page(13)
        AT = page(14).rearrange("p (b h t) -> p b h t", b=2, h=GH)
        CT = page(15)[:, 0:512].rearrange("p (h t) -> p h t", h=GH)
        PT = page(4, 3).rearrange("p (h c) -> p h c", h=HEADS)
        gT, oT, sq, rms = page(16), page(17), page(18), page(19)
        gaT, gbT = page(20, 2), page(22, 2)
        reset = sb("reset", [P, 1024])

        def h3(ap):
            return ap.rearrange("p (h t) -> p h t", h=GH)

        n1w, n2w = COLS[:, 0:8], COLS[:, 8:16]
        lbrow0, lbrow1, hnw = COLS[:, 16:20], COLS[:, 20:24], COLS[:, 24:28]
        ss, rstd, eps = SMALL[:, 0:2], SMALL[:, 2:4], SMALL[:, 4:5]
        rroot = SMALL[:, 5:7]
        lb, oml, lbd = SMALL[:, 8:12], SMALL[:, 12:16], SMALL[:, 16:20]
        dec = SMALL[:, 20:28]
        mx = SMALL[:, 28:30]
        nmx, rsum, rinv = SMALL[:, 32:48], SMALL[:, 48:64], SMALL[:, 64:80]
        top8 = SMALL[:, 80:96].rearrange("p (t c) -> p t c", t=TT)
        cgt, need, nm4, wsum, wrec = (SMALL[:, 96 + 2 * j:98 + 2 * j] for j in range(5))
        CM = SMALL[:, 110:111]
        lg = SMALL[:, 128:192].rearrange("p (t c) -> p t c", t=TT)
        gt = SMALL[:, 192:256].rearrange("p (t c) -> p t c", t=TT)
        eq = SMALL[:, 256:320].rearrange("p (t c) -> p t c", t=TT)
        cum = SMALL[:, 320:384].rearrange("p (t c) -> p t c", t=TT)
        mask = SMALL[:, 384:448].rearrange("p (t c) -> p t c", t=TT)
        posm = SMALL[:, 448:514].rearrange("p (t c) -> p t c", t=TT)
        wts = SMALL[:, 514:580].rearrange("p (t c) -> p t c", t=TT)
        CMI = sb("CMI", [1, 1], I32)

        M = WR[:].rearrange("p s n -> p (s n)")
        at = [0]

        def cut(n):
            at[0] += n
            return M[:, at[0] - n:at[0]]

        RW = cut(KD * E).rearrange("p (k e) -> p k e", k=KD)
        RB = cut(E)
        GU_B = cut(2 * DE)[0:E, :]
        DN_B = cut(D)[0:E, :]
        FW = cut(D)
        wT = cut(T)[0:E, :]
        hTe = [cut(KD * CAP).rearrange("p (k s) -> p k s", k=KD) for _ in range(2)]
        onehot = [cut(CAP)[0:E, :] for _ in range(2)]
        sel = cut(TT * CAP).rearrange("p (t s) -> p t s", t=TT)
        selw = cut(TT * P).rearrange("p (t s) -> p t s", t=TT)
        selT = [cut(T) for _ in range(2)]
        gate, up, sg = cut(512), cut(512), cut(512)
        act, actT, Y = cut(512), cut(512).rearrange("p (c s) -> p c s", c=4), cut(512)
        assert at[0] <= RING * 4096

        PS = [ctx.enter_context(nc.psum_tensor(f"PS{b}", [P, 512], F32)) for b in range(BANKS)]
        acc = [[PS[2 * t + n] for n in range(2)] for t in range(TT)]
        gu = [PS[4], PS[5]]
        gath, multi = PS[6], PS[7]

        def bank(name):
            return PS[AT_UNIT[name] % BANKS]

        x_loaded, small_loaded, rope_loaded = sem("x_loaded"), sem("small_loaded"), sem("rope_loaded")
        w_loaded = [sem(f"w_loaded{s}") for s in range(RING)]
        moe_small_loaded = sem("moe_small_loaded")
        bank_filled = sem("bank_filled")
        drained_by = {"act": sem("drained_by_act"), "dve": sem("drained_by_dve")}
        act_step, dve_step, pool_step = sem("act_step"), sem("dve_step"), sem("pool_step")
        pool_ready = sem("pool_ready")
        ss_ready, root_ready, xn_ready = sem("ss_ready"), sem("root_ready"), sem("xn_ready")
        f_ready, logf_ready, sgq_ready = sem("f_ready"), sem("logf_ready"), sem("sgq_ready")
        dec_in_ready, dec_ready = sem("dec_in_ready"), sem("dec_ready")
        lb_in_ready, lb_ready = sem("lb_in_ready"), sem("lb_ready")
        diff_ready, decay_ready, kq_ready, kx_ready, qk_ready = (
            sem(n) for n in ("diff_ready", "decay_ready", "kq_ready", "kx_ready", "qk_ready"))
        q_roped, k_roped = sem("q_roped"), sem("k_roped")
        dx_ready, dx_exp, mix_step = sem("dx_ready"), sem("dx_exp"), sem("mix_step")
        round_moved, fin_step = sem("round_moved"), sem("fin_step")
        smax_ready, exp_ready, prob_ready = sem("smax_ready"), sem("exp_ready"), sem("prob_ready")
        osq_ready, rms_ready, sig_ready, yb_ready, mix_ready = (
            sem(n) for n in ("osq_ready", "rms_ready", "sig_ready", "yb_ready", "mix_ready"))
        ss2_ready, root2_ready, xn2_ready = sem("ss2_ready"), sem("root2_ready"), sem("xn2_ready")
        lgmax_ready, lgexp_ready, mask_ready, wts_ready, rounds_ready = (
            sem(n) for n in ("lgmax_ready", "lgexp_ready", "mask_ready", "wts_ready", "rounds_ready"))
        ss3_ready, root3_ready, out_ready, out_stored = (
            sem(n) for n in ("ss3_ready", "root3_ready", "out_ready", "out_stored"))
        slot_loaded = [sem(f"slot_loaded{s}") for s in range(6)]
        slot_used = {0: sem("slot0_used"), 2: sem("slot2_used"), 4: sem("slot4_used")}
        sel_ready, selT_filled, selT_drained = sem("sel_ready"), sem("selT_filled"), sem("selT_drained")
        gath_filled, hTe_ready = sem("gath_filled"), sem("hTe_ready")
        gu_filled, gu_drained = sem("gu_filled"), sem("gu_drained")
        gate_ready, sigm_ready, act_ready = sem("gate_ready"), sem("sigm_ready"), sem("act_ready")
        up_ready = sem("up_ready")
        actT_filled, actT_ready = sem("actT_filled"), sem("actT_ready")
        y_filled, y_ready, moe_done = sem("y_filled"), sem("y_ready"), sem("moe_done")

        def filled(eng, name):
            eng.wait_ge(bank_filled, AT_UNIT[name] + 1)

        def wait_drained(eng, name):
            who, n = drained(name)
            eng.wait_ge(drained_by[who], n)

        wi = A["w_in"].rearrange("l (k p) n -> p (l k) n", p=P)
        load_src = {"mu": A["moba_up"].rearrange("l (k p) n -> p (l k) n", p=P),
                    "hu": A["hgrn_up"].rearrange("l (k p) n -> p (l k) n", p=P)}
        wo = A["w_out"].rearrange("l (k p) n -> p (l k) n", p=P)
        load_src["wo0"], load_src["wo1"] = wo[:, :, 0:512], wo[:, :, 512:1024]
        for g in range(11):
            load_src[g] = wi[:, :, g * GROUP:(g + 1) * GROUP]
        last_unit = {FB: "f1", QB: "q1", QA: "qa1", KA: "ka1", VA: "va1", IB: "ib1", GB: "g1", GA0: "ga1",
                     GA1: "ga3", GB0: "gb1", GB1: "gb3", "mu": "mu3", "hu": "hu3", "wo0": "wo10", "wo1": "wo11"}

        wgu = A["w_gate_up"].rearrange("l e (k p) (g b n) -> (l e) b p k g n", p=P, g=2, b=2)
        wdn = A["w_down"].rearrange("l e (k p) n -> (l e) p k n", p=P)
        gu_slot = [S[:, s, :].rearrange("p (k g n) -> p k g n", k=4, g=2) for s in range(4)]
        dn_slot = [S[:, 4 + s, :].rearrange("p (k n) -> p k n", k=4) for s in range(2)]

        block = ctx.enter_context(nc.Block())

        @block.sync
        def _(sp):
            for n, what in enumerate(LOADS):
                if n >= RING:
                    filled(sp, last_unit[LOADS[n - RING]])
                s = n % RING
                dst = wr4[s] if what in ("mu", "hu") else wr8[s]
                sp.dma_start(dst, load_src[what]).then_inc(w_loaded[s], 16)

            def load_gu(e, s):
                for g in range(2):
                    src = wgu[e, s // 2, :, 4 * (s % 2):4 * (s % 2) + 4, g, :]
                    if len(src.shape) == 4:
                        src = src[0]
                    sp.dma_start(gu_slot[s][:, :, g, :], src).then_inc(slot_loaded[s], 16)

            def load_dn(e, s):
                src = wdn[e, :, 4 * s:4 * s + 4, :]
                if len(src.shape) == 4:
                    src = src[0]
                sp.dma_start(dn_slot[s], src).then_inc(slot_loaded[4 + s], 16)

            filled(sp, "kT1")
            load_gu(0, 0)
            filled(sp, "ya1")
            load_gu(0, 1)
            load_gu(0, 2)
            load_gu(0, 3)
            filled(sp, "hu3")
            sp.wait_ge(mix_ready, 1)
            load_dn(0, 0)
            load_dn(0, 1)

            def load_expert(i, e):
                sp.wait_ge(slot_used[0], i)
                load_gu(e, 0)
                sp.wait_ge(gu_filled, 2 * i - 1)
                load_gu(e, 1)
                sp.wait_ge(slot_used[2], i)
                load_gu(e, 2)
                sp.wait_ge(gu_filled, 2 * i)
                load_gu(e, 3)
                sp.wait_ge(slot_used[4], i)
                load_dn(e, 0)
                sp.wait_ge(y_filled, i)
                load_dn(e, 1)

            with sp.Fori(1, E) as e:
                load_expert(e, e)
            sp.wait_ge(rounds_ready, 1)
            most = sp.value_load(CMI[0:1, 0:1], min_val=0, max_val=T)
            with sp.Fori(1, ROUNDS) as r:
                with sp.If(most > r * CAP):
                    with sp.Fori(0, E) as e:
                        load_expert(r * E + e, e)

        @block.gpsimd
        def _(pool):
            st = Steps(pool, pool_step)
            st.did(nc.gpsimd.memset(reset[:], 1.0))
            st.settle()
            nc.gpsimd.memset(reset[:].rearrange("p (c t) -> p c t", t=CHUNK)[:, :, 0:1], 0.0).then_inc(pool_ready, 1)
            nc.gpsimd.memset(page(14), 0.0).then_inc(pool_ready, 1)

            pool.wait_ge(rope_loaded, 16)
            for raw, units, done in ((qraw, "qa", q_roped), (kraw, "ka", k_roped)):
                for tt in range(TT):
                    wait_drained(pool, f"{units}{tt}")
                    r4 = raw[:, 512 * tt:512 * tt + 512].rearrange("p (h f c) -> p h f c", h=HEADS, f=2)
                    t1 = rt1[:, 512 * tt:512 * tt + 512].rearrange("p (h f c) -> p h f c", h=HEADS, f=2)
                    t2 = rt2[:, 512 * tt:512 * tt + 512].rearrange("p (h f c) -> p h f c", h=HEADS, f=2)
                    cs = rcos[:, tt, :].unsqueeze(1).to_broadcast([P, HEADS, 32])
                    sn = rsin[:, tt, :].unsqueeze(1).to_broadcast([P, HEADS, 32])
                    st.settle()
                    for f in range(2):
                        nc.gpsimd.tensor_tensor(t1[:, :, f, :], r4[:, :, f, :], cs, ALU.mult)
                        ins = nc.gpsimd.tensor_tensor(t2[:, :, f, :], r4[:, :, 1 - f, :], sn, ALU.mult)
                    st.did(ins)
                    st.settle()
                    nc.gpsimd.tensor_tensor(r4[:, :, 0, :], t1[:, :, 0, :], t2[:, :, 0, :], ALU.subtract)
                    st.did(nc.gpsimd.tensor_tensor(r4[:, :, 1, :], t1[:, :, 1, :], t2[:, :, 1, :], ALU.add), done)

        @block.scalar
        def _(se):
            st = Steps(se, act_step)
            for tt in range(TT):
                se.dma_start(X[:, tt, :], A["x"][0, tt * P:(tt + 1) * P, :]).then_inc(x_loaded, 16)
            se.dma_start(CST[:], A["cst"]).then_inc(rope_loaded, 16)
            for r0, n, name in ((0, 8, "norm1_w"), (8, 8, "norm2_w"), (16, 8, "hgrn_lb_logits"), (24, 4, "hgrn_norm_w")):
                se.dma_start(ROWS[r0:r0 + n, :], A[name].rearrange("a (r c) -> (a r) c", c=P)).then_inc(small_loaded, 16)
            se.dma_start(MSK[:], A["lmask"].rearrange("p (m t) -> p m t", t=P)).then_inc(small_loaded, 16)

            def root(dst, src, scale):
                return nc.scalar.activation(dst, src, ACT.Sqrt, bias=eps, scale=scale)

            for tt in range(TT):
                se.wait_ge(x_loaded, 32)
                st.did(nc.scalar.activation(XN[:, tt, :], X[:, tt, :], ACT.Square, accum_out=ss[:, tt:tt + 1]))
            st.settle()
            se.wait_ge(ss_ready, 1)
            st.did(root(rroot, ss, 1.0 / D), root_ready)

            se.wait_ge(lb_in_ready, 1)
            st.did(nc.scalar.activation(lbd, lbd, ACT.Exp), lb_ready)

            def copy_out(name, dst, src=None):
                filled(se, name)
                st.did(nc.scalar.copy(dst, bank(name)[:] if src is None else src), drained_by["act"])

            filled(se, "f0")
            st.did(nc.scalar.activation(kf[:, 0:512], bank("f0")[:], ACT.Sigmoid), drained_by["act"])
            filled(se, "f1")
            st.did(nc.scalar.activation(kf[:, 512:1024], bank("f1")[:], ACT.Sigmoid), drained_by["act"])
            for j in range(2):
                filled(se, f"q{j}")
                st.did(nc.scalar.activation(sgq[:, 512 * j:512 * j + 512], bank(f"q{j}")[:], ACT.Sigmoid), sgq_ready)
            se.wait_ge(f_ready, 1)
            st.did(nc.scalar.activation(logf[:], bcum[:], ACT.Ln), logf_ready)

            def decays(n):
                lv = LEVELS[n]
                h = 1 << lv
                d4 = DD[n % 2].rearrange("p (b f t) -> p b f t", f=2, t=h)
                se.wait_ge(diff_ready, n + 1)
                nc.scalar.activation(d4[:, :, 0, :], d4[:, :, 0, :], ACT.Exp, scale=-1.0)
                st.did(nc.scalar.activation(d4[:, :, 1, :], d4[:, :, 1, :], ACT.Exp), decay_ready)

            se.wait_ge(dec_in_ready, 1)
            bl = h3(bcum)[:, :, CHUNK - 1:T:CHUNK]
            st.did(nc.scalar.activation(dec.rearrange("p (c h) -> p h c", c=2), bl[:, :, 1:3], ACT.Exp), dec_ready)
            decays(0)
            se.wait_ge(dx_ready, 1)
            dx = h3(KX)[:, :, CHUNK:3 * CHUNK]
            st.did(nc.scalar.activation(dx, dx, ACT.Exp), dx_exp)
            decays(1)
            copy_out("qa0", qraw[:, 0:512])
            copy_out("qa1", qraw[:, 512:1024])
            copy_out("ka0", kraw[:, 0:512])
            copy_out("ka1", kraw[:, 512:1024])
            decays(2)
            copy_out("va0", va[:, 0, :])
            decays(3)
            decays(4)
            copy_out("va1", va[:, 1, :])
            decays(5)
            decays(6)
            copy_out("ib0", ib[:, 0, :])
            copy_out("ib1", ib[:, 1, :])
            for name, dst in (("qT0", qT), ("qT1", qT), ("kT0", kT), ("kT1", kT)):
                j = int(name[2])
                copy_out(name, dst[:, 2 * j:2 * j + 2, :].rearrange("p a t -> p (a t)"))

            gates = [("g0", gT, 0), ("g1", gT, 1)] + [(f"ga{j}", gaT, j) for j in range(4)] + \
                [(f"gb{j}", gbT, j) for j in range(4)]

            def gate_out(n):
                name, dst, j = gates[n]
                copy_out(name, dst[:, 512 * j:512 * j + 512])

            def exps(h):
                se.wait_ge(smax_ready, h + 1)
                s = SM[:, h % 2, :]
                nc.scalar.activation(s[:, 0:128], s[:, 0:128], ACT.Exp, bias=nmx[:, 2 * h:2 * h + 1], scale=SCALE,
                                     accum_out=rsum[:, 2 * h:2 * h + 1])
                st.did(nc.scalar.activation(s[:, 128:384], s[:, 128:384], ACT.Exp, bias=nmx[:, 2 * h + 1:2 * h + 2],
                                            scale=SCALE, accum_out=rsum[:, 2 * h + 1:2 * h + 2]), exp_ready)

            for h in range(HEADS):
                exps(h)
                gate_out(h)
                if h >= 1:
                    copy_out(f"pT{h - 1}", PT[:, h - 1, :], bank(f"pT{h - 1}")[:, 0:384])
            for j in range(2):
                filled(se, f"o{j}")
                nc.scalar.activation(sq[:, 512 * j:512 * j + 512], bank(f"o{j}")[:], ACT.Square).then_inc(osq_ready, 1)
                st.did(nc.scalar.copy(oT[:, 512 * j:512 * j + 512], bank(f"o{j}")[:]), drained_by["act"])
            gate_out(8)
            copy_out("pT7", PT[:, 7, :], bank("pT7")[:, 0:384])
            for j in range(2):
                filled(se, f"ms{j}")
                st.did(root(rms[:, 512 * j:512 * j + 512], bank(f"ms{j}")[:], 1.0 / GK), drained_by["act"])
            wait_drained(se, "ms1")
            filled(se, "ms1")
            st.did(nc.scalar.activation(sq[:], gT[:], ACT.Sigmoid), sig_ready)
            gate_out(9)
            st.settle()
            st.did(nc.scalar.activation(gaT[:], gaT[:], ACT.Sigmoid), sig_ready)
            st.did(nc.scalar.activation(gbT[:], gbT[:], ACT.Sigmoid), sig_ready)
            for j in range(2):
                copy_out(f"ya{j}", yaT[:, 2 * j:2 * j + 2, :].rearrange("p a t -> p (a t)"))

            filled(se, "wo11")
            for dst, src in ((RW, A["router_w"].rearrange("l (k p) e -> p (l k) e", p=P)),
                             (RB, A["router_b"].to_broadcast([P, E])),
                             (GU_B, A["b_gate_up"][0]), (DN_B, A["b_down"][0]),
                             (FW, A["final_norm_w"].unsqueeze(0).to_broadcast([P, D]))):
                se.dma_start(dst, src).then_inc(moe_small_loaded, 16)

            se.wait_ge(ss2_ready, 1)
            for tt in range(TT):
                st.did(nc.scalar.activation(XN[:, tt, :], X[:, tt, :], ACT.Square, accum_out=ss[:, tt:tt + 1]))
            st.settle()
            st.did(root(rroot, ss, 1.0 / D), root2_ready)
            se.wait_ge(lgmax_ready, 1)
            for tt in range(TT):
                st.did(nc.scalar.activation(cum[:, tt, :], lg[:, tt, :], ACT.Exp, bias=nm4[:, tt:tt + 1]), lgexp_ready)

            def drain_selT(i, b):
                se.wait_ge(selT_filled, i + 1)
                nc.scalar.copy(selT[b], multi[:, 0:T]).then_inc(selT_drained, 1)

            def expert(i, b):
                for half in range(2):
                    se.wait_ge(gate_ready, 2 * i + half + 1)
                    c = slice(256 * half, 256 * half + 256)
                    nc.scalar.activation(sg[:, c], gate[:, c], ACT.Sigmoid, scale=ALPHA).then_inc(sigm_ready, 1)
                drain_selT(i + 1, 1 - b)
                se.wait_ge(y_filled, i + 1)
                nc.scalar.copy(Y, multi[:]).then_inc(y_ready, 1)

            st.settle()
            nc.scalar.copy(nm4, nm4).then_inc(y_ready, 1)
            drain_selT(0, 0)
            with se.Fori(0, E // 2) as pair:
                expert(pair * 2, 0)
                expert(pair * 2 + 1, 1)
            se.wait_ge(rounds_ready, 1)
            most = se.value_load(CMI[0:1, 0:1], min_val=0, max_val=T)
            with se.Fori(1, ROUNDS) as r:
                with se.If(most > r * CAP):
                    with se.Fori(0, E // 2) as pair:
                        expert(r * E + pair * 2, 0)
                        expert(r * E + pair * 2 + 1, 1)

            for tt in range(TT):
                se.wait_ge(ss3_ready, tt + 1)
                nc.scalar.activation(XN[:, tt, :], X[:, tt, :], ACT.Square,
                                     accum_out=ss[:, tt:tt + 1]).then_inc(act_step, 1)
                se.wait_ge(act_step, st.count[act_step.name] + tt + 1)
                root(rroot[:, tt:tt + 1], ss[:, tt:tt + 1], 1.0 / D).then_inc(root3_ready, 1)
            for tt in range(TT):
                se.wait_ge(out_ready, tt + 1)
                se.dma_start(out[0, tt * P:(tt + 1) * P, :], XN[:, tt, :]).then_inc(out_stored, 16)
            se.wait_ge(out_stored, 16 * TT)

        @block.vector
        def _(ve):
            st = Steps(ve, dve_step)
            v = nc.vector

            def drain(name, ins):
                st.did(ins, drained_by["dve"])

            st.did(v.memset(eps, EPS), ss_ready)
            filled(ve, "rows")
            drain("rows", v.tensor_copy(COLS[:, 0:28], bank("rows")[:, 0:28]))
            st.settle()
            lbm = SMALL[:, 600:604]
            e1 = SMALL[:, 604:608]
            st.did(v.tensor_tensor(lbm, lbrow0, lbrow1, ALU.max))
            st.settle()
            st.did(v.tensor_tensor(lbrow0, lbrow0, lbm, ALU.subtract))
            st.did(v.tensor_tensor(lbrow1, lbrow1, lbm, ALU.subtract))
            st.settle()
            st.did(v.tensor_tensor(lbd, lbrow1, lbrow0, ALU.subtract), lb_in_ready)

            ve.wait_ge(root_ready, 1)
            st.did(v.reciprocal(rstd, rroot))
            st.settle()
            for tt in range(TT):
                st.did(v.tensor_scalar(XN[:, tt, :], X[:, tt, :], rstd[:, tt:tt + 1], None, ALU.mult), xn_ready)

            def weighted_T(name, j, w):
                filled(ve, name)
                for a in range(2):
                    k = 2 * j + a
                    ins = v.tensor_scalar(HT[:, k, :], bank(name)[:, T * a:T * a + T], w[:, k:k + 1], None, ALU.mult)
                drain(name, ins)

            for j in range(4):
                weighted_T(f"xT{j}", j, n1w)
            ve.wait_ge(lb_ready, 1)
            st.did(v.tensor_scalar(lbm, lbd, 1.0, None, ALU.add))
            st.settle()
            st.did(v.reciprocal(lb, lbm))
            st.settle()
            st.did(v.tensor_scalar(oml, lb, -1.0, 1.0, ALU.mult, ALU.add))
            st.settle()

            wait_drained(ve, "f1")
            for h in range(GH):
                c = slice(T * h, T * h + T)
                st.did(v.tensor_scalar(bcum[:, c], kf[:, c], oml[:, h:h + 1], lb[:, h:h + 1], ALU.mult, ALU.add), f_ready if h == GH - 1 else None)
            st.settle()
            st.did(v.tensor_scalar(kf[:], bcum[:], -1.0, 1.0, ALU.mult, ALU.add))
            for j in range(2):
                ve.wait_ge(sgq_ready, j + 1)
                c = slice(512 * j, 512 * j + 512)
                drain(f"q{j}", v.tensor_tensor(qs[:, c], bank(f"q{j}")[:], sgq[:, c], ALU.mult))
            ve.wait_ge(drained_by["dve"], st.count[drained_by["dve"].name])
            st.did(v.tensor_scalar(SMALL[:, 608:609], eps, 1.0, None, ALU.mult), qk_ready)
            ve.wait_ge(logf_ready, 1)
            ve.wait_ge(pool_ready, 1)
            st.did(v.tensor_tensor_scan(bcum[:], reset[:], logf[:], 0.0, ALU.mult, ALU.add), dec_in_ready)
            st.settle()

            def differences(n):
                lv = LEVELS[n]
                h = 1 << lv
                if n >= 2:
                    ve.wait_ge(kq_ready, n - 1)
                if lv == 6:
                    d4 = DD[n % 2].rearrange("p (b f t) -> p b f t", f=2, t=h)
                    b4 = bcum.rearrange("p (b f t) -> p b f t", f=2, t=h)
                    v.tensor_tensor(d4[:, :, 0, :], b4[:, :, 0, :], b4[:, :, 0, h - 1:h].to_broadcast([P, 8, h]),
                                    ALU.subtract)
                    st.did(v.tensor_copy(d4[:, :, 1, :], b4[:, :, 1, :]), diff_ready)
                else:
                    n_b = 1024 // (2 * h)
                    d3 = DD[n % 2].rearrange("p (b t) -> p b t", t=2 * h)
                    b3 = bcum.rearrange("p (b t) -> p b t", t=2 * h)
                    st.did(v.tensor_tensor(d3, b3, b3[:, :, h - 1:h].to_broadcast([P, n_b, 2 * h]), ALU.subtract),
                           diff_ready)

            def factors(n):
                lv = LEVELS[n]
                h = 1 << lv
                ve.wait_ge(decay_ready, n + 1)
                if n >= 2:
                    filled(ve, f"L{LEVELS[n - 2]}1")
                kq4, d4, k4, q4 = (a.rearrange("p (b f t) -> p b f t", f=2, t=h)
                                   for a in (KQ[n % 2], DD[n % 2], kf, qs))
                v.tensor_tensor(kq4[:, :, 0, :], k4[:, :, 0, :], d4[:, :, 0, :], ALU.mult)
                st.did(v.tensor_tensor(kq4[:, :, 1, :], q4[:, :, 1, :], d4[:, :, 1, :], ALU.mult), kq_ready)

            def cross_factors():
                kx, kq, b3, k3, q3 = (h3(a) for a in (KX, KQ[0], bcum, kf, qs))
                dx = h3(KX)
                C = CHUNK
                st.settle()
                v.tensor_tensor(dx[:, :, C:2 * C], b3[:, :, 2 * C - 1:2 * C].to_broadcast([P, GH, C]), b3[:, :, C:2 * C],
                                ALU.subtract)
                st.did(v.tensor_copy(dx[:, :, 2 * C:3 * C], b3[:, :, 2 * C:3 * C]), dx_ready)
                ve.wait_ge(dx_exp, 1)
                v.tensor_tensor(kx[:, :, C:2 * C], k3[:, :, C:2 * C], dx[:, :, C:2 * C], ALU.mult)
                v.tensor_tensor(kx[:, :, 2 * C:3 * C], q3[:, :, 2 * C:3 * C], dx[:, :, 2 * C:3 * C], ALU.mult)
                ve.wait_ge(dec_ready, 1)
                v.tensor_tensor(kx[:, :, 0:C], kq[:, :, 0:C], dec[:, 0:4].unsqueeze(2).to_broadcast([P, GH, C]), ALU.mult)
                st.did(v.tensor_tensor(kx[:, :, 3 * C:4 * C], kq[:, :, 3 * C:4 * C],
                                       dec[:, 4:8].unsqueeze(2).to_broadcast([P, GH, C]), ALU.mult), kx_ready)

            def take_level(name, m):
                for b in range(2):
                    filled(ve, f"{name}{b}")
                    drain(f"{name}{b}", v.copy_predicated(
                        AT[:, b], MSK[:, m, :].unsqueeze(1).to_broadcast([P, GH, P]),
                        bank(f"{name}{b}")[:].rearrange("p (h t) -> p h t", h=GH)))
                    st.settle()

            differences(0)
            differences(1)
            factors(0)
            cross_factors()
            ve.wait_ge(small_loaded, 80)
            ve.wait_ge(pool_ready, 2)
            factors(1)
            take_level("D", DIAG)
            filled(ve, "X")
            drain("X", v.tensor_copy(CT.rearrange("p h t -> p (h t)"), bank("X")[:]))
            for n in range(len(LEVELS)):
                if n + 2 < len(LEVELS):
                    differences(n + 2)
                take_level(f"L{LEVELS[n]}", LEVELS[n])
                if n + 2 < len(LEVELS):
                    factors(n + 2)

            def softmax_max(h):
                filled(ve, f"sc{h}")
                if h >= 2:
                    filled(ve, f"pT{h - 2}")
                s = SM[:, h % 2, :]
                drain(f"sc{h}", v.tensor_tensor(s, bank(f"sc{h}")[:, 0:384], amask, ALU.add))
                st.settle()
                st.did(v.reduce_max(mx[:, 0:1], s[:, 0:128], AX.X))
                st.did(v.reduce_max(mx[:, 1:2], s[:, 128:384], AX.X))
                st.settle()
                st.did(v.tensor_scalar(nmx[:, 2 * h:2 * h + 2], mx, -SCALE, None, ALU.mult), smax_ready)

            def softmax_norm(h):
                ve.wait_ge(exp_ready, h + 1)
                s = SM[:, h % 2, :]
                st.did(v.reciprocal(rinv[:, 2 * h:2 * h + 2], rsum[:, 2 * h:2 * h + 2]))
                st.settle()
                v.tensor_scalar(s[:, 0:128], s[:, 0:128], rinv[:, 2 * h:2 * h + 1], None, ALU.mult)
                st.did(v.tensor_scalar(s[:, 128:384], s[:, 128:384], rinv[:, 2 * h + 1:2 * h + 2], None, ALU.mult),
                       prob_ready)

            for h in range(HEADS):
                softmax_max(h)
                softmax_norm(h)

            wait_drained(ve, "ms1")
            st.did(v.reciprocal(rms[:], rms[:]))
            st.settle()
            for h in range(GH):
                c = slice(T * h, T * h + T)
                st.did(v.scalar_tensor_tensor(out=oT[:, c], in0=oT[:, c], scalar=hnw[:, h:h + 1], in1=rms[:, c],
                                              op0=ALU.mult, op1=ALU.mult))
            ve.wait_ge(sig_ready, 1)
            st.did(v.tensor_tensor(sq[:], sq[:], gT[:], ALU.mult))
            st.settle()
            st.did(v.tensor_tensor(oT[:], oT[:], sq[:], ALU.mult), yb_ready)

            flat = mixT.rearrange("p k t -> p (k t)")
            ve.wait_ge(sig_ready, 3)
            for j in range(4):
                c = slice(512 * j, 512 * j + 512)
                filled(ve, f"mu{j}")
                drain(f"mu{j}", v.tensor_tensor(flat[:, c], bank(f"mu{j}")[:], gaT[:, c], ALU.mult))
            for j in range(4):
                c = slice(512 * j, 512 * j + 512)
                filled(ve, f"hu{j}")
                drain(f"hu{j}", v.tensor_tensor(gbT[:, c], bank(f"hu{j}")[:], gbT[:, c], ALU.mult))
                st.settle()
                st.did(v.tensor_tensor(flat[:, c], flat[:, c], gbT[:, c], ALU.add), mix_step)
            st.settle()
            st.did(v.tensor_scalar(SMALL[:, 609:610], eps, 1.0, None, ALU.mult), mix_ready)
            for n in range(2):
                for tt in range(TT):
                    name = f"wo{tt}{n}"
                    filled(ve, name)
                    xs = X[:, tt, 512 * n:512 * n + 512]
                    drain(name, v.tensor_tensor(xs, bank(name)[:], xs, ALU.add))
            st.settle()
            st.did(v.tensor_scalar(SMALL[:, 610:611], eps, 1.0, None, ALU.mult), ss2_ready)
            ve.wait_ge(root2_ready, 1)
            st.did(v.reciprocal(rstd, rroot))
            st.settle()
            for tt in range(TT):
                st.did(v.tensor_scalar(XN[:, tt, :], X[:, tt, :], rstd[:, tt:tt + 1], None, ALU.mult), xn2_ready)
            for j in range(4):
                weighted_T(f"h2T{j}", j, n2w)

            ve.wait_ge(moe_small_loaded, 80)
            filled(ve, "rt")
            drain("rt", v.tensor_tensor(lg, bank("rt")[:, 0:64].rearrange("p (t e) -> p t e", t=TT),
                                        RB.unsqueeze(1).to_broadcast([P, TT, E]), ALU.add))
            st.settle()
            for tt in range(TT):
                st.did(v.max(top8[:, tt, :], lg[:, tt, :]))
            st.settle()
            st.did(v.tensor_scalar(nm4, top8[:, :, 0], -1.0, None, ALU.mult), lgmax_ready)
            v4 = top8[:, :, TOPK - 1:TOPK].to_broadcast([P, TT, E])
            v.tensor_tensor(gt, lg, v4, ALU.is_gt)
            st.did(v.tensor_tensor(eq, lg, v4, ALU.is_equal))
            st.settle()
            st.did(v.reduce_sum(cgt, gt, AX.X))
            st.settle()
            st.did(v.tensor_scalar(need, cgt, -1.0, float(TOPK), ALU.mult, ALU.add))
            for tt in range(TT):
                st.did(v.tensor_tensor_scan(mask[:, tt, :], eq[:, tt, :], eq[:, tt, :], 0.0, ALU.add, ALU.bypass))
            st.settle()
            for tt in range(TT):
                st.did(v.scalar_tensor_tensor(out=eq[:, tt, :], in0=mask[:, tt, :], scalar=need[:, tt:tt + 1],
                                              in1=eq[:, tt, :], op0=ALU.is_le, op1=ALU.mult))
            st.settle()
            st.did(v.tensor_tensor(mask, gt, eq, ALU.add), mask_ready)
            st.settle()
            ve.wait_ge(lgexp_ready, TT)
            st.did(v.tensor_tensor(cum, cum, mask, ALU.mult))
            st.settle()
            st.did(v.reduce_sum(wsum, cum, AX.X))
            st.settle()
            st.did(v.reciprocal(wrec, wsum))
            st.settle()
            st.did(v.tensor_tensor(wts[:, :, 0:E], cum, wrec.unsqueeze(2).to_broadcast([P, TT, E]), ALU.mult), wts_ready)
            st.settle()
            filled(ve, "pos")
            pp = bank("pos")[:, 0:64].rearrange("p (t e) -> p t e", t=TT)
            st.did(v.scalar_tensor_tensor(out=posm[:, :, 0:E], in0=pp, scalar=1.0, in1=mask, op0=ALU.add, op1=ALU.mult))
            drain("pos", v.reduce_max(CM, bank("pos")[:, 64:96], AX.X))
            st.settle()
            st.did(v.tensor_copy(CMI[0:1, 0:1], CM[0:1, 0:1]), rounds_ready)
            st.did(v.tensor_scalar(posm[:, :, 0:E], posm[:, :, 0:E], -1.0, None, ALU.add))
            st.settle()
            st.did(v.tensor_scalar(posm[:, :, E:E + 1], posm[:, :, 0:1], -float(CAP), None, ALU.add))
            st.did(v.tensor_copy(wts[:, :, E:E + 1], wts[:, :, 0:1]))
            filled(ve, "wT")
            drain("wT", v.tensor_copy(wT, bank("wT")[0:E, 0:T]))
            st.settle()
            st.did(v.tensor_copy(SMALL[:, 611:612], eps), gu_drained)
            st.did(v.tensor_copy(SMALL[:, 612:613], eps), gu_drained)
            st.settle()

            def select(e, b, moved=None):
                v.tensor_copy(onehot[b], ohtab[:, bass.ds(e, 1)].to_broadcast([E, CAP]))
                if moved is not None:
                    ve.wait_ge(round_moved, moved)
                for tt in range(TT):
                    ps = posm[:, tt, bass.ds(e, 1)]
                    v.tensor_scalar(sel[:, tt, :], iota[:, 0:CAP], ps, None, ALU.is_equal)
                    ins = v.tensor_scalar(selw[:, tt, :], iota, ps, wts[:, tt, bass.ds(e, 1)], ALU.is_equal, ALU.mult)
                ins.then_inc(sel_ready, 1)

            def drain_gathered(i, b):
                ve.wait_ge(gath_filled, i + 1)
                v.tensor_tensor(hTe[b], gath[:].rearrange("p (k s) -> p k s", k=KD),
                                n2w.unsqueeze(2).to_broadcast([P, KD, CAP]), ALU.mult).then_inc(hTe_ready, 1)

            def expert(i, e, b, moved=None):
                for half in range(2):
                    c = slice(256 * half, 256 * half + 256)
                    ve.wait_ge(gu_filled, 2 * i + half + 1)
                    g2 = gu[half][:].rearrange("p (n f) -> p n f", f=2)
                    v.tensor_scalar(gate[:, c], g2[:, :, 0], LIMIT, None, ALU.min).then_inc(gate_ready, 1)
                    v.tensor_scalar(up[:, c], g2[:, :, 1], LIMIT, -LIMIT, ALU.min, ALU.max).then_inc(gu_drained, 1)
                    ve.wait_ge(gu_drained, 2 * i + half + 3)
                    v.scalar_tensor_tensor(out=up[:, c], in0=up[:, c], scalar=1.0, in1=gate[:, c],
                                           op0=ALU.add, op1=ALU.mult).then_inc(up_ready, 1)
                    ve.wait_ge(up_ready, 2 * i + half + 1)
                    ve.wait_ge(sigm_ready, 2 * i + half + 1)
                    v.tensor_tensor(act[:, c], up[:, c], sg[:, c], ALU.mult).then_inc(act_ready, 1)
                    if half == 0:
                        select(e + 1, 1 - b, moved)
                drain_gathered(i + 1, 1 - b)
                ve.wait_ge(actT_filled, i + 1)
                v.tensor_copy(actT, multi[:].rearrange("p (c s) -> p c s", c=4)).then_inc(actT_ready, 1)

            def next_round():
                v.tensor_scalar(posm, posm, -float(CAP), None, ALU.add).then_inc(round_moved, 1)

            ve.wait_ge(dve_step, st.count[dve_step.name])
            select(0, 0)
            drain_gathered(0, 0)
            with ve.Fori(0, E // 2) as pair:
                expert(pair * 2, pair * 2, 0)
                expert(pair * 2 + 1, pair * 2 + 1, 1)
            most = ve.value_load(CMI[0:1, 0:1], min_val=0, max_val=T)
            with ve.Fori(1, ROUNDS) as r:
                with ve.If(most > r * CAP):
                    next_round()
                    with ve.Fori(0, E // 2) as pair:
                        expert(r * E + pair * 2, pair * 2, 0, r)
                        expert(r * E + pair * 2 + 1, pair * 2 + 1, 1, r)

            ve.wait_ge(moe_done, 1)
            f = Steps(ve, fin_step)
            for tt in range(TT):
                for n in range(2):
                    xs = X[:, tt, 512 * n:512 * n + 512]
                    ins = v.tensor_tensor(xs, acc[tt][n][:], xs, ALU.add)
                    if n == 0:
                        f.did(ins)
                    else:
                        f.did(ins, ss3_ready)
            for tt in range(TT):
                ve.wait_ge(root3_ready, tt + 1)
                f.did(v.reciprocal(rstd[:, tt:tt + 1], rroot[:, tt:tt + 1]))
                f.settle()
                f.did(v.scalar_tensor_tensor(out=XN[:, tt, :], in0=X[:, tt, :], scalar=rstd[:, tt:tt + 1], in1=FW,
                                             op0=ALU.mult, op1=ALU.mult), out_ready)

        @block.tensor
        def _(pe):
            mm, tr = nc.tensor.matmul, nc.tensor.transpose
            n_unit = [0]

            def begin(name):
                assert UNITS[n_unit[0]][0] == name, (name, UNITS[n_unit[0]])
                if n_unit[0] >= BANKS:
                    wait_drained(pe, UNITS[n_unit[0] - BANKS][0])
                return bank(name)

            def end(ins):
                ins.then_inc(bank_filled, 1)
                n_unit[0] += 1

            def weights(what):
                n = LOADS.index(what)
                pe.wait_ge(w_loaded[n % RING], 16 * (n // RING + 1))
                return wr4[n % RING] if what in ("mu", "hu") else wr8[n % RING]

            def proj_T(name, what, j, src=HT, kn=KD):
                ps, w = begin(name), weights(what)
                for a in range(2):
                    for k in range(kn):
                        c = P * (2 * j + a)
                        ins = mm(ps[:, T * a:T * a + T], w[:, k, c:c + P], src[:, k, :], start=(k == 0), stop=(k == kn - 1))
                end(ins)

            def proj(name, what, tt, src=HT):
                ps, w = begin(name), weights(what)
                for k in range(KD):
                    ins = mm(ps[:], src[:, k, P * tt:P * tt + P], w[:, k, :], start=(k == 0), stop=(k == KD - 1))
                end(ins)

            def transposed(name, j):
                ps = begin(name)
                for a in range(2):
                    for tt in range(TT):
                        k = 2 * j + a
                        ins = tr(ps[:, T * a + P * tt:T * a + P * tt + P], XN[:, tt, P * k:P * k + P], ident)
                end(ins)

            pe.wait_ge(rope_loaded, 16)
            pe.wait_ge(small_loaded, 80)
            end(tr(begin("rows")[:, 0:28], ROWS[0:28, :], ident[0:28, 0:28]))
            pe.wait_ge(xn_ready, TT)
            for j in range(4):
                transposed(f"xT{j}", j)
            wait_drained(pe, "xT3")
            for name in ("f0", "f1"):
                proj_T(name, FB, int(name[1]))
            for name in ("q0", "q1"):
                proj_T(name, QB, int(name[1]))
            for tt in range(TT):
                proj(f"qa{tt}", QA, tt)
            for tt in range(TT):
                proj(f"ka{tt}", KA, tt)

            def level(name, lhs, rhs, b):
                ps = begin(name)
                for h in range(GH):
                    ins = mm(ps[:, P * h:P * h + P], h3(lhs)[:, h, P * b[0]:P * b[0] + P],
                             h3(rhs)[:, h, P * b[1]:P * b[1] + P], start=True, stop=True)
                end(ins)

            def levels(names):
                for name in names:
                    if name[0] == "D":
                        pe.wait_ge(qk_ready, 1)
                        level(name, kf, qs, (int(name[1]),) * 2)
                    elif name == "X":
                        pe.wait_ge(kx_ready, 1)
                        level(name, KX, KX, (0, 1))
                    else:
                        n = LEVELS.index(int(name[1]))
                        pe.wait_ge(kq_ready, n + 1)
                        level(name, KQ[n % 2], KQ[n % 2], (int(name[2]),) * 2)

            order = ["D0", "D1", "X"] + [f"L{lv}{b}" for lv in LEVELS for b in range(2)]
            levels(order[:5])
            proj("va0", VA, 0)
            levels(order[5:9])
            proj("va1", VA, 1)
            levels(order[9:13])
            proj("ib0", IB, 0)
            levels(order[13:])
            proj("ib1", IB, 1)

            for raw, u, roped in ((qraw, "qT", q_roped), (kraw, "kT", k_roped)):
                pe.wait_ge(roped, TT)
                for j in range(2):
                    ps = begin(f"{u}{j}")
                    for a in range(2):
                        for tt in range(TT):
                            c = 512 * tt + P * (2 * j + a)
                            ins = tr(ps[:, T * a + P * tt:T * a + P * tt + P], raw[:, c:c + P], ident)
                    end(ins)

            gates = [("g0", GB, 0), ("g1", GB, 1)] + [(f"ga{j}", GA0 + j // 2, j % 2) for j in range(4)] + \
                [(f"gb{j}", GB0 + j // 2, j % 2) for j in range(4)]

            def probs_T(h):
                ps = begin(f"pT{h}")
                pe.wait_ge(prob_ready, h + 1)
                for a in range(3):
                    ins = tr(ps[:, P * a:P * a + P], SM[:, h % 2, P * a:P * a + P], ident)
                end(ins)

            wait_drained(pe, "kT1")
            for h in range(HEADS):
                ps = begin(f"sc{h}")
                r = slice(64 * (h % 2), 64 * (h % 2) + 64)
                for c, q, k in ((0, 0, 0), (128, 1, 1), (256, 1, 0)):
                    ins = mm(ps[:, c:c + P], qT[r, h // 2, P * q:P * q + P], kT[r, h // 2, P * k:P * k + P],
                             start=True, stop=True)
                end(ins)
                proj_T(*gates[h])
                if h >= 1:
                    probs_T(h - 1)

            wait_drained(pe, "ib1")
            wait_drained(pe, "L01")
            wait_drained(pe, "X")
            for j in range(2):
                ps = begin(f"o{j}")
                for a in range(2):
                    h = 2 * j + a
                    c = slice(P * h, P * h + P)
                    mm(ps[:, T * a:T * a + P], ib[:, 0, c], AT[:, 0, h, :], start=True, stop=True)
                    mm(ps[:, T * a + P:T * a + T], ib[:, 1, c], AT[:, 1, h, :], start=True, stop=False)
                    ins = mm(ps[:, T * a + P:T * a + T], ib[:, 0, c], CT[:, h, :], start=False, stop=True)
                end(ins)
            proj_T(*gates[8])
            probs_T(7)
            for j in range(2):
                ps = begin(f"ms{j}")
                pe.wait_ge(osq_ready, j + 1)
                end(mm(ps[:], ones, sq[:, 512 * j:512 * j + 512], start=True, stop=True))
            proj_T(*gates[9])
            wait_drained(pe, "pT7")
            for j in range(2):
                ps = begin(f"ya{j}")
                for a in range(2):
                    for f in range(2):
                        h = 4 * j + 2 * a + f
                        o, c = slice(64 * f, 64 * f + 64), slice(64 * h, 64 * h + 64)
                        mm(ps[o, T * a:T * a + P], va[:, 0, c], PT[:, h, 0:128], start=True, stop=True)
                        mm(ps[o, T * a + P:T * a + T], va[:, 1, c], PT[:, h, 128:256], start=True, stop=False)
                        ins = mm(ps[o, T * a + P:T * a + T], va[:, 0, c], PT[:, h, 256:384], start=False, stop=True)
                end(ins)
            wait_drained(pe, "ya1")
            for j in range(4):
                proj_T(f"mu{j}", "mu", j, src=yaT, kn=4)
            pe.wait_ge(yb_ready, 1)
            for j in range(4):
                proj_T(f"hu{j}", "hu", j, src=h3(oT), kn=4)
            pe.wait_ge(mix_ready, 1)
            for n in range(2):
                for tt in range(TT):
                    proj(f"wo{tt}{n}", f"wo{n}", tt, src=mixT)
            pe.wait_ge(xn2_ready, TT)
            for j in range(4):
                transposed(f"h2T{j}", j)

            ps = begin("rt")
            wait_drained(pe, "h2T3")
            pe.wait_ge(moe_small_loaded, 80)
            for tt in range(TT):
                for k in range(KD):
                    ins = mm(ps[:, E * tt:E * tt + E], HT[:, k, P * tt:P * tt + P], RW[:, k, :], start=(k == 0), stop=(k == KD - 1))
            end(ins)
            ps = begin("pos")
            pe.wait_ge(mask_ready, 1)
            mm(ps[:, 0:E], ucum, mask[:, 0, :], start=True, stop=True)
            mm(ps[:, E:2 * E], ones, mask[:, 0, :], start=True, stop=False)
            mm(ps[:, E:2 * E], ucum, mask[:, 1, :], start=False, stop=True)
            mm(ps[:, 2 * E:3 * E], ones, mask[:, 0, :], start=True, stop=False)
            end(mm(ps[:, 2 * E:3 * E], ones, mask[:, 1, :], start=False, stop=True))
            ps = begin("wT")
            pe.wait_ge(wts_ready, 1)
            for tt in range(TT):
                ins = tr(ps[0:E, P * tt:P * tt + P], wts[:, tt, 0:E], ident)
            end(ins)

            wait_drained(pe, "wT")
            for tt in range(TT):
                for n in range(2):
                    mm(acc[tt][n][:], wT[:, P * tt:P * tt + P], DN_B[:, 512 * n:512 * n + 512], start=True, stop=True,
                       skip_group_check=True)

            def prepare(i, b, first=False):
                pe.wait_ge(sel_ready, i + 1)
                if not first:
                    pe.wait_ge(y_ready, i)
                for tt in range(TT):
                    ins = tr(multi[:, P * tt:P * tt + P], selw[:, tt, :], ident)
                ins.then_inc(selT_filled, 1)
                if not first:
                    pe.wait_ge(hTe_ready, i)
                for k in range(KD):
                    for tt in range(TT):
                        ins = mm(gath[:, CAP * k:CAP * k + CAP], XN[:, tt, P * k:P * k + P], sel[:, tt, :],
                                 start=(tt == 0), stop=(tt == TT - 1))
                ins.then_inc(gath_filled, 1)

            def expert(i, b):
                pe.wait_ge(hTe_ready, i + 1)
                for half in range(2):
                    pe.wait_ge(gu_drained, 2 * i + half + 1)
                    for g in range(2):
                        c = 1024 * g + 512 * half
                        mm(gu[half][64 * g:64 * g + 64, :], onehot[b], GU_B[:, c:c + 512], start=True, stop=False)
                    for kh in range(2):
                        s = 2 * half + kh
                        pe.wait_ge(slot_loaded[s], 32 * (i + 1))
                        for k in range(4):
                            for g in range(2):
                                ins = mm(gu[half][64 * g:64 * g + 64, :], hTe[b][:, 4 * kh + k, :],
                                         gu_slot[s][:, k, g, :], start=False, stop=(kh == 1 and k == 3))
                        ins.then_inc(gu_filled if kh else slot_used[s], 1)
                prepare(i + 1, 1 - b)
                pe.wait_ge(act_ready, 2 * i + 2)
                pe.wait_ge(selT_drained, i + 2)
                for c in range(4):
                    ins = tr(multi[:, P * c:P * c + P], act[:, P * c:P * c + P], ident)
                ins.then_inc(actT_filled, 1)
                pe.wait_ge(actT_ready, i + 1)
                for kh in range(2):
                    pe.wait_ge(slot_loaded[4 + kh], 16 * (i + 1))
                    for k in range(4):
                        for n in range(2):
                            ins = mm(multi[64 * n:64 * n + 64, :], actT[:, k, 64 * kh:64 * kh + 64],
                                     dn_slot[kh][:, k, 512 * n:512 * n + 512], start=(kh == 0 and k == 0),
                                     stop=(kh == 1 and k == 3))
                    ins.then_inc(y_filled if kh else slot_used[4], 1)
                pe.wait_ge(y_ready, i + 2)
                for tt in range(TT):
                    for n in range(2):
                        mm(acc[tt][n][:], selT[b][64 * n:64 * n + 64, P * tt:P * tt + P], Y[64 * n:64 * n + 64, :],
                           start=False, stop=True, skip_group_check=True)

            prepare(0, 0, first=True)
            with pe.Fori(0, E // 2) as pair:
                expert(pair * 2, 0)
                expert(pair * 2 + 1, 1)
            pe.wait_ge(rounds_ready, 1)
            most = pe.value_load(CMI[0:1, 0:1], min_val=0, max_val=T)
            with pe.Fori(1, ROUNDS) as r:
                with pe.If(most > r * CAP):
                    with pe.Fori(0, E // 2) as pair:
                        expert(r * E + pair * 2, 0)
                        expert(r * E + pair * 2 + 1, 1)
            mm(multi[0:64, 0:64], sel[:, 0, :], sel[:, 0, :], start=True, stop=True).then_inc(moe_done, 1)


_INS = ['x', 'norm1_w', 'w_in', 'moba_up', 'hgrn_lb_logits', 'hgrn_norm_w', 'hgrn_up', 'w_out', 'norm2_w', 'router_w',
        'router_b', 'w_gate_up', 'b_gate_up', 'w_down', 'b_down', 'final_norm_w']


def shape_constants():
    import numpy as np
    c = np.zeros((P, 1152), np.float32)
    r = np.arange(P)
    c[:, 0:128] = np.eye(P)
    c[:, 128:256] = r[:, None] < r[None, :]
    c[:, 256:384] = r[None, :] % CAP
    own = np.where(r[None, :] <= r[:, None], 0.0, NEG)
    c[:, 384:512] = own
    c[:, 512:640] = own
    inv = (np.float32(10000.0) ** (-(np.arange(32, dtype=np.float32) * np.float32(2.0) / np.float32(DH)))).astype(np.float32)
    ang = (np.arange(T, dtype=np.float32)[:, None] * inv[None, :]).astype(np.float32)
    for t in range(TT):
        c[:, 768 + 32 * t:800 + 32 * t] = np.cos(ang[P * t:P * t + P])
        c[:, 832 + 32 * t:864 + 32 * t] = np.sin(ang[P * t:P * t + P])
    c[0:E, 896:896 + E] = np.eye(E)
    c[0, 896 + E] = 1.0
    c[:, 1024:1152] = 1.0
    m = np.zeros((P, NMASK, P), np.int32)
    x = r[:, None] ^ r[None, :]
    for lv in range(7):
        m[:, lv] = ((x >> lv) == 1) & (r[:, None] < r[None, :])
    m[:, DIAG] = x == 0
    return c, m.reshape(P, NMASK * P)


def kernel(**inputs):
    import numpy as _np
    import concourse.bacc as _bacc
    from concourse import mybir as _mybir
    from concourse.bass_utils import run_bass_kernel_spmd as _run

    nc = _bacc.Bacc("TRN2", target_bir_lowering=False, num_devices=1)
    cst, lmask = shape_constants()
    arrays, args = {}, {}
    for name, a in [(n, _np.ascontiguousarray(inputs[n])) for n in _INS] + [("cst", cst), ("lmask", lmask)]:
        arrays[f"in_{name}_dram"] = a
        args[name] = nc.dram_tensor(f"in_{name}_dram", a.shape, _mybir.dt.from_np(a.dtype), kind="ExternalInput").ap()
    out = nc.dram_tensor("out_0_dram", (1, T, D), F32, kind="ExternalOutput").ap()
    hybrid_block(nc, args, out)
    r = _run(nc, [arrays], core_ids=[0])
    return r.results[0]["out_0_dram"]
```

```python
import concourse.bass as bass
from concourse import mybir
from contextlib import ExitStack

F32 = mybir.dt.float32
F32R = mybir.dt.float32r
I32 = mybir.dt.int32
ALU = mybir.AluOpType
ACT = mybir.ActivationFunctionType
AX = mybir.AxisListType

P = 128
T = 256
TT = T // P
D = 1024
KD = D // P
HEADS, DH = 8, 64
GH, GK = 4, 128
CHUNK = 64
E = 32
TOPK = 4
CAP = 64
ROUNDS = T // CAP
DE = 1024
LIMIT, ALPHA = 7.0, 1.702
EPS = 1e-6
NEG = -1e30
BANKS = 8
SLOTS = 8
SCALE = DH ** -0.5
GROUP = 512
RING = 3
QA, KA, VA, QB, FB, IB, GB, GA0, GA1, GB0, GB1 = range(11)
LEVELS = [6, 5, 4, 3, 2, 1, 0]
NMASK = 7
DIAG = 6

LOADS = [FB, QB, QA, KA, VA, IB, GB, GA0, GA1, GB0, GB1, "mu", "hu", "wo0", "wo1"]

GATES = [("g0", GB, 0), ("g1", GB, 1)] + [(f"ga{j}", GA0 + j // 2, j % 2) for j in range(4)] + \
    [(f"gb{j}", GB0 + j // 2, j % 2) for j in range(4)]
PIECES = [(QA, j, "dve", ("A", j), None) for j in range(2)] + [(KA, j, "pool", ("B", j), None) for j in range(2)] + \
    [(VA, j, "dve", ("A", j), "qa1") for j in range(2)] + [(IB, j, "pool", ("B", j), "ka1") for j in range(2)] + \
    [(what, j, "dve", ("A", j), "va1" if n < 2 else GATES[n - 2][0]) for n, (_, what, j) in enumerate(GATES)] + \
    [("mu", j, "dve", ("Q", j), f"gb{2 + j // 2}") for j in range(4)] + \
    [("hu", j, "dve", ("Q", j), f"mu{j}") for j in range(4)]
AT_PIECE = {(p[0], p[1]): n for n, p in enumerate(PIECES)}


def lo_done(what, j):
    n = AT_PIECE[what, j]
    who = PIECES[n][2]
    return who, sum(1 for p in PIECES[:n + 1] if p[2] == who)


def bank_units():
    u = [("rows", "dve")] + [(f"xT{tt}{j}", "dve") for tt in range(TT) for j in range(2)]
    u += [("f0", "act"), ("f1", "act"), ("q0", "dve"), ("q1", "dve")]
    u += [("qa0", "act"), ("qa1", "act"), ("ka0", "act"), ("ka1", "act")]
    u += [("D", "dve"), ("X", "dve"), ("L6", "dve"), ("va0", "act"), ("L5", "dve"), ("L4", "dve"), ("va1", "act")]
    u += [("L3", "dve"), ("L2", "dve"), ("ib0", "act"), ("L1", "dve"), ("L0", "dve"), ("ib1", "act")]
    u += [("qT0", "act"), ("qT1", "act"), ("kT0", "act"), ("kT1", "act")]
    fill = ["g0", "g1", "ga0", "ga1", "ga2", "ga3", "gb0", "gb1", "gb2", "gb3"]
    for h in range(HEADS):
        u += [(f"sc{h}", "dve"), (fill[h], "act")]
        if h >= 1:
            u += [(f"pT{h - 1}", "act")]
    u += [("o0", "act"), ("o1", "act"), (fill[8], "act"), ("pT7", "act"), ("ms0", "act"), ("ms1", "act")]
    u += [("ya0", "act"), ("ya1", "act"), (fill[9], "act")]
    u += [(f"mu{j}", "dve") for j in range(4)] + [(f"hu{j}", "dve") for j in range(4)]
    u += [(n, "dve") for n in ("wo00", "wo01", "wo10", "h2T00", "h2T01", "rt0", "wo11", "h2T10", "h2T11", "rt1", "rt", "pos", "all",
                              "wT")]
    return u


UNITS = bank_units()
AT_UNIT = {name: n for n, (name, _) in enumerate(UNITS)}


def drained(name):
    n = AT_UNIT[name]
    who = UNITS[n][1]
    return who, sum(1 for _, w in UNITS[:n + 1] if w == who)


class Steps:

    def __init__(self, eng, own):
        self.eng, self.own, self.count, self.last = eng, own, {}, None

    def did(self, ins, sem=None, by=1):
        sem = self.own if sem is None else sem
        key = sem.name
        self.count[key] = self.count.get(key, 0) + by
        ins.then_inc(sem, by)
        self.last = (sem, self.count[key])

    def settle(self):
        self.eng.wait_ge(*self.last)


def hybrid_block(nc, A, out):
    ctx = ExitStack()
    with ctx:
        def sb(name, shape, dt=F32):
            return ctx.enter_context(nc.sbuf_tensor(name, shape, dt))

        def sem(name):
            return ctx.enter_context(nc.semaphore(name))

        with ExitStack() as early:
            def over(name, pages, dt=F32R):
                return early.enter_context(nc.sbuf_tensor(name, [P, 1024 * pages], dt))[:]

            hT_hi = over("hT_hi", 2).rearrange("p (k t) -> p k t", k=KD)
            ya_hi = over("ya_hi", 1).rearrange("p (k t) -> p k t", k=4)
            ya_lo = over("ya_lo", 1).rearrange("p (k t) -> p k t", k=4)
            over("skip_m2", 2, F32)
            hT_lo = over("hT_lo", 2).rearrange("p (k t) -> p k t", k=KD)
            over("skip_m6", 2, F32)
            hi_b = over("hi_b", 4)
            over("skip_s0", 10, F32)
            o_lo = over("o_lo", 1).rearrange("p (k t) -> p k t", k=4)
            o_hi = over("o_hi", 1).rearrange("p (k t) -> p k t", k=4)
            over("skip_s12", 4, F32)
            hi_a = over("hi_a", 4)
            w_lo = [over(f"w_lo{s}", 4) for s in range(RING)]

        XN = sb("XN", [P, TT, D])
        M = sb("M", [P, 12 * 1024])
        S = sb("S", [P, SLOTS, 4096])
        X = sb("X", [P, TT, D])
        CST = sb("CST", [P, 1152])
        MSK = sb("MSK", [P, NMASK, CHUNK], I32)
        ROWS = sb("ROWS", [32, P])
        COLS = sb("COLS", [P, 32])
        SMALL = sb("SMALL", [P, 640])
        ident, ucum = CST[:, 0:128], CST[:, 128:256]
        iota = CST[:, 256:384]
        amask = CST[:, 384:768]
        rcos = CST[:, 768:832].rearrange("p (t c) -> p t c", t=TT)
        rsin = CST[:, 832:896].rearrange("p (t c) -> p t c", t=TT)
        ohtab = CST[0:E, 896:896 + E]
        ones = CST[:, 1024:1152]

        SF = S[:].rearrange("p s n -> p (s n)")
        wr8 = [S[:, SLOTS - RING + s, :].rearrange("p (k n) -> p k n", k=KD) for s in range(RING)]
        wr4 = [S[:, SLOTS - RING + s, :].rearrange("p (k n) -> p k n", k=4) for s in range(RING)]

        def page(n, c=1):
            return SF[:, 1024 * n:1024 * (n + c)]

        qraw, kraw, rt1, rt2 = page(0), page(1), page(2), page(3)
        qs, kf, bcum, sgq = page(4), page(5), page(6), page(7)
        PT = page(4, 3).rearrange("p (h c) -> p h c", h=HEADS)
        DD = [page(8), page(9)]
        KQ = [page(10), page(11)]
        KX = page(12)
        logf = page(13)
        AT = page(14).rearrange("p (b h t) -> p b h t", b=2, h=GH)
        CT = page(15)[:, 0:512].rearrange("p (h t) -> p h t", h=GH)
        gT, oT, sq, rms = page(9), page(12), page(13), page(8)


        def mpage(n, c=1):
            return M[:, 1024 * n:1024 * (n + c)]

        QKT = mpage(0, 2).rearrange("p (a j t) -> p a j t", a=2, j=4)
        qT, kT = QKT[:, 0], QKT[:, 1]
        VI = mpage(2, 2).rearrange("p (a t n) -> p a t n", a=2, t=TT)
        va, ib = VI[:, 0], VI[:, 1]
        mixT = mpage(2, 2).rearrange("p (k t) -> p k t", k=KD)
        HT = mpage(4, 2).rearrange("p (k t) -> p k t", k=KD)
        SM = mpage(6)[:, 0:768].rearrange("p (b c) -> p b c", b=2)
        reset = mpage(7)
        gaT, gbT = mpage(8, 2), mpage(10, 2)

        RW = mpage(6)[:, 0:KD * E].rearrange("p (k e) -> p k e", k=KD)
        RB = mpage(6)[:, 256:256 + E]
        lgT = mpage(6)[0:E, 512:512 + T]
        GU_B = mpage(8, 2)[0:E, :]
        DN_B = mpage(10)[0:E, :]
        FW = mpage(11)
        hTe = mpage(0).rearrange("p (k s) -> p k s", k=KD)
        Y = mpage(1)
        gate, up = mpage(2)[:, 0:512], mpage(2)[:, 512:1024]
        sg, act = mpage(3)[:, 0:512], mpage(3)[:, 512:1024]
        actT = mpage(4)[:, 0:512].rearrange("p (c s) -> p c s", c=4)
        selT = mpage(4)[:, 512:768]
        sel = mpage(7)[:, 0:256].rearrange("p (t s) -> p t s", t=TT)
        selw = mpage(7)[:, 256:512].rearrange("p (t s) -> p t s", t=TT)
        wT = mpage(7)[0:E, 512:768]
        onehot = mpage(7)[0:E, 768:896].rearrange("p (f s) -> p f s", f=2)

        def h3(ap):
            return ap.rearrange("p (h t) -> p h t", h=GH)

        n1w, n2w = COLS[:, 0:8], COLS[:, 8:16]
        lbrow0, lbrow1, hnw = COLS[:, 16:20], COLS[:, 20:24], COLS[:, 24:28]
        ss, rstd, eps = SMALL[:, 0:2], SMALL[:, 2:4], SMALL[:, 4:5]
        rroot = SMALL[:, 5:7]
        lb, oml, lbd = SMALL[:, 8:12], SMALL[:, 12:16], SMALL[:, 16:20]
        dec = SMALL[:, 20:28]
        mx = SMALL[:, 28:30]
        nmx, rsum, rinv = SMALL[:, 32:48], SMALL[:, 48:64], SMALL[:, 64:80]
        top8 = SMALL[:, 80:96].rearrange("p (t c) -> p t c", t=TT)
        cgt, need, nm4, wsum, wrec = (SMALL[:, 96 + 2 * j:98 + 2 * j] for j in range(5))
        CM = SMALL[:, 110:111]
        ssp = SMALL[:, 111:115].rearrange("p (t n) -> p t n", t=TT)
        ssb = SMALL[:, 115:117]
        lg = SMALL[:, 128:192].rearrange("p (t c) -> p t c", t=TT)
        gt = SMALL[:, 192:256].rearrange("p (t c) -> p t c", t=TT)
        eq = SMALL[:, 256:320].rearrange("p (t c) -> p t c", t=TT)
        cum = SMALL[:, 320:384].rearrange("p (t c) -> p t c", t=TT)
        mask = SMALL[:, 384:448].rearrange("p (t c) -> p t c", t=TT)
        posm = SMALL[:, 448:512].rearrange("p (t c) -> p t c", t=TT)
        wts = SMALL[:, 512:576].rearrange("p (t c) -> p t c", t=TT)
        CMI = sb("CMI", [1, 1], I32)

        def hi_part(where):
            buf, j = where
            if buf == "Q":
                return hi_a[:, 1024 * j:1024 * j + 1024].rearrange("p (k n) -> p k n", k=4)
            return (hi_a if buf == "A" else hi_b)[:, 2048 * j:2048 * j + 2048].rearrange("p (k n) -> p k n", k=KD)

        def raw_part(what, j, lo=False):
            s, kn = LOADS.index(what) % RING, 4 if what in ("mu", "hu") else KD
            whole = w_lo[s].rearrange("p (k n) -> p k n", k=kn) if lo else (wr4 if kn == 4 else wr8)[s]
            return whole[:, :, 256 * j:256 * j + 256]

        PS = [ctx.enter_context(nc.psum_tensor(f"PS{b}", [P, 512], F32)) for b in range(BANKS)]
        acc = [[PS[2 * t + n] for n in range(2)] for t in range(TT)]
        gu = [PS[4], PS[5]]
        gath, multi = PS[6], PS[7]

        def bank(name):
            return PS[AT_UNIT[name] % BANKS]

        x_loaded = [sem(f"x_loaded{tt}") for tt in range(TT)]
        small_loaded, lmask_loaded = sem("small_loaded"), sem("lmask_loaded")
        w_loaded = [sem(f"w_loaded{s}") for s in range(RING)]
        moe_small_loaded = sem("moe_small_loaded")
        bank_filled = sem("bank_filled")
        drained_by = {"act": sem("drained_by_act"), "dve": sem("drained_by_dve")}
        act_step, dve_step, pool_step = sem("act_step"), sem("dve_step"), sem("pool_step")
        pool_ready = sem("pool_ready")
        eps_ready, root_ready, xn_ready = sem("eps_ready"), sem("root_ready"), sem("xn_ready")
        f_ready, logf_ready, sgq_ready = sem("f_ready"), sem("logf_ready"), sem("sgq_ready")
        dec_in_ready, dec_ready = sem("dec_in_ready"), sem("dec_ready")
        lb_in_ready, lb_ready = sem("lb_in_ready"), sem("lb_ready")
        diff_ready, decay_ready, kq_ready, kx_ready, qk_ready = (
            sem(n) for n in ("diff_ready", "decay_ready", "kq_ready", "kx_ready", "qk_ready"))
        q_roped, k_roped = sem("q_roped"), sem("k_roped")
        dx_ready, dx_exp, mix_step = sem("dx_ready"), sem("dx_exp"), sem("mix_step")
        round_moved, fin_step = sem("round_moved"), sem("fin_step")
        smax_ready, exp_ready, prob_ready = sem("smax_ready"), sem("exp_ready"), sem("prob_ready")
        osq_ready, rms_ready, sig_ready, yb_ready, mix_ready = (
            sem(n) for n in ("osq_ready", "rms_ready", "sig_ready", "yb_ready", "mix_ready"))
        res_ready, root2_ready, xn2_ready = sem("res_ready"), sem("root2_ready"), sem("xn2_ready")
        lgmax_ready, lgexp_ready, mask_ready, wts_ready, rounds_ready = (
            sem(n) for n in ("lgmax_ready", "lgexp_ready", "mask_ready", "wts_ready", "rounds_ready"))
        ss3_ready, root3_ready, out_ready, out_stored = (
            sem(n) for n in ("ss3_ready", "root3_ready", "out_ready", "out_stored"))
        ident_loaded = sem("ident_loaded")
        hi_ready, lo_ready = sem("hi_ready"), {"dve": sem("lo_ready_dve"), "pool": sem("lo_ready_pool")}
        hT_hi_ready, hT_lo_ready = sem("hT_hi_ready"), sem("hT_lo_ready")
        ya_lo_ready, o_ready, o_hi_ready = sem("ya_lo_ready"), sem("o_ready"), sem("o_hi_ready")
        first_loaded, cst_loaded, router_loaded = sem("first_loaded"), sem("cst_loaded"), sem("router_loaded")
        slot_loaded = [sem(f"slot_loaded{s}") for s in range(SLOTS)]
        weights_used = sem("weights_used")
        selw_ready = sem("selw_ready")
        sel_ready, selT_filled, selT_drained = sem("sel_ready"), sem("selT_filled"), sem("selT_drained")
        gath_filled, hTe_ready = sem("gath_filled"), sem("hTe_ready")
        gu_filled, gu_drained = sem("gu_filled"), sem("gu_drained")
        gate_ready, sigm_ready, act_ready = sem("gate_ready"), sem("sigm_ready"), sem("act_ready")
        up_ready = sem("up_ready")
        actT_filled, actT_ready = sem("actT_filled"), sem("actT_ready")
        y_filled, y_ready, moe_done = sem("y_filled"), sem("y_ready"), sem("moe_done")

        def filled(eng, name):
            eng.wait_ge(bank_filled, AT_UNIT[name] + 1)

        def wait_drained(eng, name):
            who, n = drained(name)
            eng.wait_ge(drained_by[who], n)

        wi = A["w_in"].rearrange("l (k p) n -> p (l k) n", p=P)
        load_src = {"mu": A["moba_up"].rearrange("l (k p) n -> p (l k) n", p=P),
                    "hu": A["hgrn_up"].rearrange("l (k p) n -> p (l k) n", p=P)}
        wo = A["w_out"].rearrange("l (k p) n -> p (l k) n", p=P)
        load_src["wo0"], load_src["wo1"] = wo[:, :, 0:512], wo[:, :, 512:1024]
        for g in range(11):
            load_src[g] = wi[:, :, g * GROUP:(g + 1) * GROUP]
        last_unit = {FB: "f1", QB: "q1", QA: "qa1", KA: "ka1", VA: "va1", IB: "ib1", GB: "g1", GA0: "ga1",
                     GA1: "ga3", GB0: "gb1", GB1: "gb3", "mu": "mu3", "hu": "hu3", "wo0": "wo10", "wo1": "wo11"}

        wgu = A["w_gate_up"].rearrange("l e (k p) n -> (l e) p k n", p=P)
        wdn = A["w_down"].rearrange("l e (k p) n -> (l e) p k n", p=P)
        gu_slot = [S[:, s, :].rearrange("p (k n) -> p k n", k=2) for s in range(SLOTS)]
        dn_slot = [S[:, s, :].rearrange("p (k n) -> p k n", k=4) for s in range(SLOTS)]

        def form_lo(eng, tensor_tensor, what, j):
            n = AT_PIECE[what, j]
            eng.wait_ge(hi_ready, n + 1)
            tensor_tensor(raw_part(what, j, lo=True), raw_part(what, j), hi_part(PIECES[n][3]),
                          ALU.subtract).then_inc(lo_ready[PIECES[n][2]], 1)

        block = ctx.enter_context(nc.Block())

        @block.sync
        def _(sp):
            for tt in range(TT):
                sp.dma_start(X[:, tt, :], A["x"][0, tt * P:(tt + 1) * P, :]).then_inc(x_loaded[tt], 16)
            sp.dma_start(CST[:, 0:128], A["cst"][:, 0:128]).then_inc(ident_loaded, 16)
            for n, what in enumerate(LOADS):
                if n >= RING:
                    filled(sp, last_unit[LOADS[n - RING]])
                s = n % RING
                dst = wr4[s] if what in ("mu", "hu") else wr8[s]
                if n == 0:
                    sp.dma_start(dst[:, :, 0:256], load_src[what][:, :, 0:256]).then_inc(first_loaded, 16)
                    sp.dma_start(dst[:, :, 256:512], load_src[what][:, :, 256:512]).then_inc(w_loaded[s], 16)
                else:
                    sp.dma_start(dst, load_src[what]).then_inc(w_loaded[s], 16)
                if n == 1:
                    sp.dma_start(CST[:, 128:], A["cst"][:, 128:]).then_inc(cst_loaded, 16)
                    sp.dma_start(MSK[:], A["lmask"].rearrange("p (m t) -> p m t", t=CHUNK)).then_inc(lmask_loaded, 16)

            def load(e, m):
                e, s, slot = e + m // 6, m % 6, m % SLOTS
                src = wgu[e, :, 2 * s:2 * s + 2, :] if s < 4 else wdn[e, :, 4 * (s - 4):4 * (s - 4) + 4, :]
                if len(src.shape) == 4:
                    src = src[0]
                dst = gu_slot[slot] if s < 4 else dn_slot[slot]
                sp.dma_start(dst, src).then_inc(slot_loaded[slot], 16)

            filled(sp, "kT1")
            load(0, 0)
            filled(sp, "ya1")
            load(0, 1)
            filled(sp, "hu3")
            for m in (2, 3, 4, 5):
                load(0, m)
            filled(sp, "wo11")
            load(0, 6)
            load(0, 7)

            def load_four(q, e, start=0):
                for m in range(start, 24):
                    i, s = q * 4 + m // 6, m % 6
                    if s == 1:
                        sp.wait_ge(y_filled, i - 1)
                    else:
                        sp.wait_ge(weights_used, i * 5 + (s - 6 if s > 1 else -5))
                    load(e, m)

            load_four(0, 0, start=SLOTS)
            with sp.Fori(1, E // 4) as q:
                load_four(q, q * 4)
            sp.wait_ge(rounds_ready, 1)
            most = sp.value_load(CMI[0:1, 0:1], min_val=0, max_val=T)
            with sp.If(most > CAP):
                with sp.Fori(1, ROUNDS) as r:
                    with sp.If(most > r * CAP):
                        with sp.Fori(0, E // 4) as q:
                            load_four(r * (E // 4) + q, q * 4)

        @block.gpsimd
        def _(pool):
            st = Steps(pool, pool_step)
            st.did(nc.gpsimd.memset(reset, 1.0))
            st.settle()
            nc.gpsimd.memset(reset.rearrange("p (c t) -> p c t", t=CHUNK)[:, :, 0:1], 0.0).then_inc(pool_ready, 1)
            nc.gpsimd.memset(page(14), 0.0).then_inc(pool_ready, 1)

            pool.wait_ge(cst_loaded, 16)
            for raw, units, done in ((qraw, "qa", q_roped), (kraw, "ka", k_roped)):
                if units == "qa":
                    for j in range(2):
                        form_lo(pool, nc.gpsimd.tensor_tensor, KA, j)
                for tt in range(TT):
                    wait_drained(pool, f"{units}{tt}")
                    r4 = raw[:, 512 * tt:512 * tt + 512].rearrange("p (h f c) -> p h f c", h=HEADS, f=2)
                    t1 = rt1[:, 512 * tt:512 * tt + 512].rearrange("p (h f c) -> p h f c", h=HEADS, f=2)
                    t2 = rt2[:, 512 * tt:512 * tt + 512].rearrange("p (h f c) -> p h f c", h=HEADS, f=2)
                    cs = rcos[:, tt, :].unsqueeze(1).to_broadcast([P, HEADS, 32])
                    sn = rsin[:, tt, :].unsqueeze(1).to_broadcast([P, HEADS, 32])
                    st.settle()
                    for f in range(2):
                        nc.gpsimd.tensor_tensor(t1[:, :, f, :], r4[:, :, f, :], cs, ALU.mult)
                        ins = nc.gpsimd.tensor_tensor(t2[:, :, f, :], r4[:, :, 1 - f, :], sn, ALU.mult)
                    st.did(ins)
                    st.settle()
                    nc.gpsimd.tensor_tensor(r4[:, :, 0, :], t1[:, :, 0, :], t2[:, :, 0, :], ALU.subtract)
                    st.did(nc.gpsimd.tensor_tensor(r4[:, :, 1, :], t1[:, :, 1, :], t2[:, :, 1, :], ALU.add), done)
            for j in range(2):
                form_lo(pool, nc.gpsimd.tensor_tensor, IB, j)

        @block.scalar
        def _(se):
            st = Steps(se, act_step)
            for r0, n, name in ((0, 8, "norm1_w"), (8, 8, "norm2_w"), (16, 8, "hgrn_lb_logits"), (24, 4, "hgrn_norm_w")):
                se.dma_start(ROWS[r0:r0 + n, :], A[name].rearrange("a (r c) -> (a r) c", c=P)).then_inc(small_loaded, 16)

            def root(dst, src, scale):
                return nc.scalar.activation(dst, src, ACT.Sqrt, bias=eps, scale=scale)

            se.wait_ge(eps_ready, 1)
            st.did(nc.scalar.activation(ssb[:, 0:1], eps, ACT.Sqrt))
            for tt in range(TT):
                se.wait_ge(x_loaded[tt], 16)
                st.did(nc.scalar.activation(XN[:, tt, :], X[:, tt, :], ACT.Square, accum_out=ss[:, tt:tt + 1]))
                st.settle()
                st.did(root(rroot[:, tt:tt + 1], ss[:, tt:tt + 1], 1.0 / D), root_ready)

            se.wait_ge(lb_in_ready, 1)
            st.did(nc.scalar.activation(lbd, lbd, ACT.Exp), lb_ready)

            def copy_out(name, dst, src=None):
                filled(se, name)
                st.did(nc.scalar.copy(dst, bank(name)[:] if src is None else src), drained_by["act"])

            def round_hi(what, j):
                n = AT_PIECE[what, j]
                if PIECES[n][4]:
                    filled(se, PIECES[n][4])
                m = LOADS.index(what)
                se.wait_ge(w_loaded[m % RING], 16 * (m // RING + 1))
                st.did(nc.scalar.copy(hi_part(PIECES[n][3]), raw_part(what, j)), hi_ready)

            wait_drained(se, "xT11")
            st.did(nc.scalar.copy(hT_hi, HT), hT_hi_ready)
            filled(se, "f0")
            st.did(nc.scalar.activation(kf[:, 0:512], bank("f0")[:], ACT.Sigmoid), drained_by["act"])
            for j in range(2):
                round_hi(QA, j)
            filled(se, "f1")
            st.did(nc.scalar.activation(kf[:, 512:1024], bank("f1")[:], ACT.Sigmoid), drained_by["act"])
            for j in range(2):
                filled(se, f"q{j}")
                st.did(nc.scalar.activation(sgq[:, 512 * j:512 * j + 512], bank(f"q{j}")[:], ACT.Sigmoid), sgq_ready)
                if j == 0:
                    for i in range(2):
                        round_hi(KA, i)
            se.wait_ge(f_ready, 1)
            st.did(nc.scalar.activation(logf[:], bcum[:], ACT.Ln), logf_ready)

            def decays(n):
                lv = LEVELS[n]
                h = 1 << lv
                d4 = DD[n % 2].rearrange("p (b f t) -> p b f t", f=2, t=h)
                se.wait_ge(diff_ready, n + 1)
                nc.scalar.activation(d4[:, :, 0, :], d4[:, :, 0, :], ACT.Exp, scale=-1.0)
                st.did(nc.scalar.activation(d4[:, :, 1, :], d4[:, :, 1, :], ACT.Exp), decay_ready)

            se.wait_ge(dec_in_ready, 1)
            bl = h3(bcum)[:, :, CHUNK - 1:T:CHUNK]
            st.did(nc.scalar.activation(dec.rearrange("p (c h) -> p h c", c=2), bl[:, :, 1:3], ACT.Exp), dec_ready)
            decays(0)
            se.wait_ge(dx_ready, 1)
            dx = h3(KX)[:, :, CHUNK:3 * CHUNK]
            st.did(nc.scalar.activation(dx, dx, ACT.Exp), dx_exp)
            decays(1)
            copy_out("qa0", qraw[:, 0:512])
            copy_out("qa1", qraw[:, 512:1024])
            for j in range(2):
                round_hi(VA, j)
            copy_out("ka0", kraw[:, 0:512])
            copy_out("ka1", kraw[:, 512:1024])
            decays(2)
            for j in range(2):
                round_hi(IB, j)
            copy_out("va0", va[:, 0, :])
            decays(3)
            decays(4)
            copy_out("va1", va[:, 1, :])
            decays(5)
            decays(6)
            for j in range(2):
                round_hi(GB, j)
            copy_out("ib0", ib[:, 0, :])
            copy_out("ib1", ib[:, 1, :])
            for name, dst in (("qT0", qT), ("qT1", qT), ("kT0", kT), ("kT1", kT)):
                j = int(name[2])
                copy_out(name, dst[:, 2 * j:2 * j + 2, :].rearrange("p a t -> p (a t)"))

            gates = [("g0", gT, 0), ("g1", gT, 1)] + [(f"ga{j}", gaT, j) for j in range(4)] + \
                [(f"gb{j}", gbT, j) for j in range(4)]

            def gate_out(n):
                name, dst, j = gates[n]
                copy_out(name, dst[:, 512 * j:512 * j + 512])

            def exps(h):
                se.wait_ge(smax_ready, h + 1)
                s = SM[:, h % 2, :]
                nc.scalar.activation(s[:, 0:128], s[:, 0:128], ACT.Exp, bias=nmx[:, 2 * h:2 * h + 1], scale=SCALE,
                                     accum_out=rsum[:, 2 * h:2 * h + 1])
                st.did(nc.scalar.activation(s[:, 128:384], s[:, 128:384], ACT.Exp, bias=nmx[:, 2 * h + 1:2 * h + 2],
                                            scale=SCALE, accum_out=rsum[:, 2 * h + 1:2 * h + 2]), exp_ready)

            for h in range(HEADS):
                if h >= 1:
                    round_hi(*GATES[h + 1][1:])
                exps(h)
                gate_out(h)
                if h >= 1:
                    copy_out(f"pT{h - 1}", PT[:, h - 1, :], bank(f"pT{h - 1}")[:, 0:384])
            round_hi(*GATES[9][1:])
            for j in range(2):
                filled(se, f"o{j}")
                nc.scalar.activation(sq[:, 512 * j:512 * j + 512], bank(f"o{j}")[:], ACT.Square).then_inc(osq_ready, 1)
                st.did(nc.scalar.copy(oT[:, 512 * j:512 * j + 512], bank(f"o{j}")[:]), drained_by["act"])
            gate_out(8)
            copy_out("pT7", PT[:, 7, :], bank("pT7")[:, 0:384])
            filled(se, "pT7")
            for dst, src in ((RW, A["router_w"].rearrange("l (k p) e -> p (l k) e", p=P)),
                             (RB, A["router_b"].to_broadcast([P, E]))):
                se.dma_start(dst, src).then_inc(router_loaded, 16)
            for j in range(2):
                filled(se, f"ms{j}")
                st.did(root(rms[:, 512 * j:512 * j + 512], bank(f"ms{j}")[:], 1.0 / GK), drained_by["act"])
            for j in range(2):
                round_hi("mu", j)
            filled(se, "ms1")
            st.did(nc.scalar.activation(sq[:], gT[:], ACT.Sigmoid), sig_ready)
            for j in range(2):
                filled(se, f"ya{j}")
                st.did(nc.scalar.copy(ya_hi[:, 2 * j:2 * j + 2, :].rearrange("p a t -> p (a t)"), bank(f"ya{j}")[:]),
                       drained_by["act"])
            st.did(nc.scalar.activation(gaT[:], gaT[:], ACT.Sigmoid), sig_ready)
            gate_out(9)
            st.settle()
            for j in range(2, 4):
                round_hi("mu", j)
            st.did(nc.scalar.activation(gbT[:], gbT[:], ACT.Sigmoid), sig_ready)
            round_hi("hu", 0)
            se.wait_ge(o_ready, 1)
            st.did(nc.scalar.copy(o_hi.rearrange("p k t -> p (k t)"), oT), o_hi_ready)
            for j in range(1, 4):
                round_hi("hu", j)

            se.wait_ge(mix_ready, 1)
            for dst, src in ((GU_B, A["b_gate_up"][0]), (DN_B, A["b_down"][0]),
                             (FW, A["final_norm_w"].unsqueeze(0).to_broadcast([P, D]))):
                se.dma_start(dst, src).then_inc(moe_small_loaded, 16)

            for tt in range(TT):
                for n in range(2):
                    c = slice(512 * n, 512 * n + 512)
                    se.wait_ge(res_ready, 2 * tt + n + 1)
                    st.did(nc.scalar.activation(XN[:, tt, c], X[:, tt, c], ACT.Square, accum_out=ssp[:, tt, n:n + 1]))
                    st.settle()
                    if n == 0:
                        st.did(nc.scalar.activation(ssb[:, tt:tt + 1], ssp[:, tt, 0:1], ACT.Identity, bias=eps,
                                                    scale=1.0 / D))
                st.did(nc.scalar.activation(rroot[:, tt:tt + 1], ssp[:, tt, 1:2], ACT.Sqrt, bias=ssb[:, tt:tt + 1],
                                            scale=1.0 / D), root2_ready)
            se.wait_ge(lgmax_ready, 1)
            for tt in range(TT):
                st.did(nc.scalar.activation(cum[:, tt, :], lg[:, tt, :], ACT.Exp, bias=nm4[:, tt:tt + 1]), lgexp_ready)
            st.settle()
            nc.scalar.copy(nm4, nm4).then_inc(y_ready, 1)

            def expert(i, b):
                for half in range(2):
                    se.wait_ge(gate_ready, 2 * i + half + 1)
                    c = slice(256 * half, 256 * half + 256)
                    nc.scalar.activation(sg[:, c], gate[:, c], ACT.Sigmoid, scale=ALPHA).then_inc(sigm_ready, 1)

            def drain_y(i, b):
                se.wait_ge(y_filled, i + 1)
                rows = slice(64 * b, 64 * b + 64)
                nc.scalar.copy(Y[rows, 0:512], multi[0:64, :])
                nc.scalar.copy(Y[rows, 512:1024], multi[64:128, :]).then_inc(y_ready, 1)

            def pair(p):
                expert(p * 2, 0)
                drain_y(p * 2, 0)
                expert(p * 2 + 1, 1)
                se.wait_ge(selT_filled, p + 1)
                nc.scalar.copy(selT, multi[:, 0:T]).then_inc(selT_drained, 1)
                drain_y(p * 2 + 1, 1)

            se.wait_ge(rounds_ready, 1)
            most = se.value_load(CMI[0:1, 0:1], min_val=0, max_val=T)
            with se.Fori(0, E // 2) as p:
                pair(p)
            with se.If(most > CAP):
                with se.Fori(1, ROUNDS) as r:
                    with se.If(most > r * CAP):
                        with se.Fori(0, E // 2) as p:
                            pair(r * (E // 2) + p)
            nc.scalar.activation(ssb[:, 0:1], eps, ACT.Sqrt)

            done = st.count[act_step.name]
            for tt in range(TT):
                for n in range(2):
                    c = slice(512 * n, 512 * n + 512)
                    done += 1
                    se.wait_ge(ss3_ready, 2 * tt + n + 1)
                    nc.scalar.activation(XN[:, tt, c], X[:, tt, c], ACT.Square,
                                         accum_out=ssp[:, tt, n:n + 1]).then_inc(act_step, 1)
                    se.wait_ge(act_step, done)
                    if n == 0:
                        done += 1
                        nc.scalar.activation(ssb[:, tt:tt + 1], ssp[:, tt, 0:1], ACT.Identity, bias=eps,
                                             scale=1.0 / D).then_inc(act_step, 1)
                nc.scalar.activation(rroot[:, tt:tt + 1], ssp[:, tt, 1:2], ACT.Sqrt, bias=ssb[:, tt:tt + 1],
                                     scale=1.0 / D).then_inc(root3_ready, 1)
            for tt in range(TT):
                for n in range(2):
                    c = slice(512 * n, 512 * n + 512)
                    se.wait_ge(out_ready, 2 * tt + n + 1)
                    se.dma_start(out[0, tt * P:(tt + 1) * P, c], XN[:, tt, c]).then_inc(out_stored, 16)
            se.wait_ge(out_stored, 16 * 2 * TT)

        @block.vector
        def _(ve):
            st = Steps(ve, dve_step)
            v = nc.vector

            def drain(name, ins):
                st.did(ins, drained_by["dve"])

            st.did(v.memset(eps, EPS), eps_ready)
            filled(ve, "rows")
            drain("rows", v.tensor_copy(COLS[:, 0:28], bank("rows")[:, 0:28]))
            st.settle()
            lbm = SMALL[:, 600:604]
            e1 = SMALL[:, 604:608]
            st.did(v.tensor_tensor(lbm, lbrow0, lbrow1, ALU.max))
            st.settle()
            st.did(v.tensor_tensor(lbrow0, lbrow0, lbm, ALU.subtract))
            st.did(v.tensor_tensor(lbrow1, lbrow1, lbm, ALU.subtract))
            st.settle()
            st.did(v.tensor_tensor(lbd, lbrow1, lbrow0, ALU.subtract), lb_in_ready)

            def weighted_T(name, tt, j, w):
                filled(ve, name)
                drain(name, v.tensor_tensor(HT[:, 4 * j:4 * j + 4, P * tt:P * tt + P],
                                            bank(name)[:].rearrange("p (k t) -> p k t", k=4),
                                            w[:, 4 * j:4 * j + 4].unsqueeze(2).to_broadcast([P, 4, P]), ALU.mult))

            for tt in range(TT):
                ve.wait_ge(root_ready, tt + 1)
                st.did(v.reciprocal(rstd[:, tt:tt + 1], rroot[:, tt:tt + 1]))
                st.settle()
                st.did(v.tensor_scalar(XN[:, tt, :], X[:, tt, :], rstd[:, tt:tt + 1], None, ALU.mult), xn_ready)
            for tt in range(TT):
                for j in range(2):
                    weighted_T(f"xT{tt}{j}", tt, j, n1w)
            ve.wait_ge(lb_ready, 1)
            st.did(v.tensor_scalar(lbm, lbd, 1.0, None, ALU.add))
            st.settle()
            st.did(v.reciprocal(lb, lbm))
            st.settle()
            st.did(v.tensor_scalar(oml, lb, -1.0, 1.0, ALU.mult, ALU.add))
            st.settle()

            def lo(what, j):
                form_lo(ve, v.tensor_tensor, what, j)

            for j in range(2):
                lo(QA, j)
            wait_drained(ve, "f1")
            for h in range(GH):
                c = slice(T * h, T * h + T)
                st.did(v.tensor_scalar(bcum[:, c], kf[:, c], oml[:, h:h + 1], lb[:, h:h + 1], ALU.mult, ALU.add), f_ready if h == GH - 1 else None)
            st.settle()
            st.did(v.tensor_scalar(kf[:], bcum[:], -1.0, 1.0, ALU.mult, ALU.add))
            for j in range(2):
                if j == 1:
                    filled(ve, "q1")
                    ve.wait_ge(hT_hi_ready, 1)
                    st.did(v.tensor_tensor(hT_lo, HT, hT_hi, ALU.subtract), hT_lo_ready)
                ve.wait_ge(sgq_ready, j + 1)
                c = slice(512 * j, 512 * j + 512)
                drain(f"q{j}", v.tensor_tensor(qs[:, c], bank(f"q{j}")[:], sgq[:, c], ALU.mult))
            ve.wait_ge(drained_by["dve"], st.count[drained_by["dve"].name])
            st.did(v.tensor_scalar(SMALL[:, 608:609], eps, 1.0, None, ALU.mult), qk_ready)
            ve.wait_ge(logf_ready, 1)
            ve.wait_ge(pool_ready, 1)
            st.did(v.tensor_tensor_scan(bcum[:], reset, logf[:], 0.0, ALU.mult, ALU.add), dec_in_ready)
            st.settle()

            def differences(n):
                lv = LEVELS[n]
                h = 1 << lv
                if n >= 2:
                    ve.wait_ge(kq_ready, n - 1)
                if lv == 6:
                    d4 = DD[n % 2].rearrange("p (b f t) -> p b f t", f=2, t=h)
                    b4 = bcum.rearrange("p (b f t) -> p b f t", f=2, t=h)
                    v.tensor_tensor(d4[:, :, 0, :], b4[:, :, 0, :], b4[:, :, 0, h - 1:h].to_broadcast([P, 8, h]),
                                    ALU.subtract)
                    st.did(v.tensor_copy(d4[:, :, 1, :], b4[:, :, 1, :]), diff_ready)
                else:
                    n_b = 1024 // (2 * h)
                    d3 = DD[n % 2].rearrange("p (b t) -> p b t", t=2 * h)
                    b3 = bcum.rearrange("p (b t) -> p b t", t=2 * h)
                    st.did(v.tensor_tensor(d3, b3, b3[:, :, h - 1:h].to_broadcast([P, n_b, 2 * h]), ALU.subtract),
                           diff_ready)

            def factors(n):
                lv = LEVELS[n]
                h = 1 << lv
                ve.wait_ge(decay_ready, n + 1)
                if n >= 2:
                    filled(ve, f"L{LEVELS[n - 2]}")
                kq4, d4, k4, q4 = (a.rearrange("p (b f t) -> p b f t", f=2, t=h)
                                   for a in (KQ[n % 2], DD[n % 2], kf, qs))
                v.tensor_tensor(kq4[:, :, 0, :], k4[:, :, 0, :], d4[:, :, 0, :], ALU.mult)
                st.did(v.tensor_tensor(kq4[:, :, 1, :], q4[:, :, 1, :], d4[:, :, 1, :], ALU.mult), kq_ready)

            def cross_factors():
                kx, kq, b3, k3, q3 = (h3(a) for a in (KX, KQ[0], bcum, kf, qs))
                dx = h3(KX)
                C = CHUNK
                st.settle()
                v.tensor_tensor(dx[:, :, C:2 * C], b3[:, :, 2 * C - 1:2 * C].to_broadcast([P, GH, C]), b3[:, :, C:2 * C],
                                ALU.subtract)
                st.did(v.tensor_copy(dx[:, :, 2 * C:3 * C], b3[:, :, 2 * C:3 * C]), dx_ready)
                ve.wait_ge(dx_exp, 1)
                v.tensor_tensor(kx[:, :, C:2 * C], k3[:, :, C:2 * C], dx[:, :, C:2 * C], ALU.mult)
                v.tensor_tensor(kx[:, :, 2 * C:3 * C], q3[:, :, 2 * C:3 * C], dx[:, :, 2 * C:3 * C], ALU.mult)
                ve.wait_ge(dec_ready, 1)
                v.tensor_tensor(kx[:, :, 0:C], kq[:, :, 0:C], dec[:, 0:4].unsqueeze(2).to_broadcast([P, GH, C]), ALU.mult)
                st.did(v.tensor_tensor(kx[:, :, 3 * C:4 * C], kq[:, :, 3 * C:4 * C],
                                       dec[:, 4:8].unsqueeze(2).to_broadcast([P, GH, C]), ALU.mult), kx_ready)

            halves = AT.rearrange("p b h t -> p (b h) t")

            def take_level(name, m):
                filled(ve, name)
                for o in (0, CHUNK):
                    r = slice(o, o + CHUNK)
                    ins = v.copy_predicated(halves[r, :, r], MSK[r, m, :].unsqueeze(1).to_broadcast([CHUNK, 8, CHUNK]),
                                            bank(name)[r, :].rearrange("p (b t) -> p b t", t=CHUNK))
                drain(name, ins)
                st.settle()

            def take_level6():
                filled(ve, "L6")
                for b in range(2):
                    src = bank("L6")[CHUNK * b:CHUNK * b + CHUNK, 0:GH * CHUNK].rearrange("p (h t) -> p h t", h=GH)
                    ins = v.tensor_copy(AT[0:CHUNK, b, :, CHUNK:P], src)
                drain("L6", ins)
                st.settle()

            differences(0)
            differences(1)
            factors(0)
            cross_factors()
            ve.wait_ge(lmask_loaded, 16)
            ve.wait_ge(pool_ready, 2)
            factors(1)
            for j in range(2):
                lo(VA, j)
            take_level("D", DIAG)
            filled(ve, "X")
            drain("X", v.tensor_copy(CT.rearrange("p h t -> p (h t)"), bank("X")[:]))
            for n in range(len(LEVELS)):
                if n + 2 < len(LEVELS):
                    differences(n + 2)
                if LEVELS[n] == 6:
                    take_level6()
                else:
                    take_level(f"L{LEVELS[n]}", LEVELS[n])
                if n + 2 < len(LEVELS):
                    factors(n + 2)

            def softmax_max(h):
                filled(ve, f"sc{h}")
                if h >= 2:
                    filled(ve, f"pT{h - 2}")
                s = SM[:, h % 2, :]
                drain(f"sc{h}", v.tensor_tensor(s, bank(f"sc{h}")[:, 0:384], amask, ALU.add))
                st.settle()
                st.did(v.reduce_max(mx[:, 0:1], s[:, 0:128], AX.X))
                st.did(v.reduce_max(mx[:, 1:2], s[:, 128:384], AX.X))
                st.settle()
                st.did(v.tensor_scalar(nmx[:, 2 * h:2 * h + 2], mx, -SCALE, None, ALU.mult), smax_ready)

            def softmax_norm(h):
                ve.wait_ge(exp_ready, h + 1)
                s = SM[:, h % 2, :]
                st.did(v.reciprocal(rinv[:, 2 * h:2 * h + 2], rsum[:, 2 * h:2 * h + 2]))
                st.settle()
                v.tensor_scalar(s[:, 0:128], s[:, 0:128], rinv[:, 2 * h:2 * h + 1], None, ALU.mult)
                st.did(v.tensor_scalar(s[:, 128:384], s[:, 128:384], rinv[:, 2 * h + 1:2 * h + 2], None, ALU.mult),
                       prob_ready)

            lo(GB, 0)
            for h in range(HEADS):
                softmax_max(h)
                lo(*GATES[h + 1][1:])
                softmax_norm(h)
            lo(*GATES[9][1:])

            wait_drained(ve, "ms1")
            for j in range(2):
                lo("mu", j)
            st.did(v.reciprocal(rms[:], rms[:]))
            st.settle()
            for h in range(GH):
                c = slice(T * h, T * h + T)
                st.did(v.scalar_tensor_tensor(out=oT[:, c], in0=oT[:, c], scalar=hnw[:, h:h + 1], in1=rms[:, c],
                                              op0=ALU.mult, op1=ALU.mult))
            ve.wait_ge(sig_ready, 1)
            st.did(v.tensor_tensor(sq[:], sq[:], gT[:], ALU.mult))
            st.settle()
            st.did(v.tensor_tensor(oT[:], oT[:], sq[:], ALU.mult), o_ready)
            wait_drained(ve, "ya1")
            for j in range(2):
                st.did(v.tensor_tensor(ya_lo[:, 2 * j:2 * j + 2, :].rearrange("p a t -> p (a t)"), bank(f"ya{j}")[:],
                                       ya_hi[:, 2 * j:2 * j + 2, :].rearrange("p a t -> p (a t)"), ALU.subtract),
                       ya_lo_ready)
            for j in range(2, 4):
                lo("mu", j)

            flat = mixT.rearrange("p k t -> p (k t)")
            ve.wait_ge(sig_ready, 2)
            for j in range(4):
                c = slice(512 * j, 512 * j + 512)
                filled(ve, f"mu{j}")
                drain(f"mu{j}", v.tensor_tensor(flat[:, c], bank(f"mu{j}")[:], gaT[:, c], ALU.mult))
                if j == 0:
                    ve.wait_ge(o_hi_ready, 1)
                    st.did(v.tensor_tensor(o_lo.rearrange("p k t -> p (k t)"), oT, o_hi.rearrange("p k t -> p (k t)"),
                                           ALU.subtract), yb_ready)
                lo("hu", j)
            for j in range(4):
                c = slice(512 * j, 512 * j + 512)
                ve.wait_ge(sig_ready, 3)
                filled(ve, f"hu{j}")
                drain(f"hu{j}", v.tensor_tensor(gbT[:, c], bank(f"hu{j}")[:], gbT[:, c], ALU.mult))
                st.settle()
                st.did(v.tensor_tensor(flat[:, c], flat[:, c], gbT[:, c], ALU.add), mix_step)
            st.settle()
            st.did(v.tensor_scalar(SMALL[:, 609:610], eps, 1.0, None, ALU.mult), mix_ready)
            def residual(tt, n):
                name = f"wo{tt}{n}"
                filled(ve, name)
                xs = X[:, tt, 512 * n:512 * n + 512]
                drain(name, v.tensor_tensor(xs, bank(name)[:], xs, ALU.add))
                st.settle()
                st.did(v.tensor_copy(SMALL[:, 610:611], eps), res_ready)

            def normalise(tt):
                ve.wait_ge(root2_ready, tt + 1)
                st.did(v.reciprocal(rstd[:, tt:tt + 1], rroot[:, tt:tt + 1]))
                st.settle()
                for n in range(2):
                    c = slice(512 * n, 512 * n + 512)
                    st.did(v.tensor_scalar(XN[:, tt, c], X[:, tt, c], rstd[:, tt:tt + 1], None, ALU.mult), xn2_ready)

            def drain_logits(tt):
                filled(ve, f"rt{tt}")
                drain(f"rt{tt}", v.tensor_copy(lgT[:, P * tt:P * tt + P], bank(f"rt{tt}")[0:E, 0:P]))

            residual(0, 0)
            residual(0, 1)
            normalise(0)
            residual(1, 0)
            weighted_T("h2T00", 0, 0, n2w)
            weighted_T("h2T01", 0, 1, n2w)
            drain_logits(0)
            residual(1, 1)
            normalise(1)
            weighted_T("h2T10", 1, 0, n2w)
            weighted_T("h2T11", 1, 1, n2w)

            drain_logits(1)
            ve.wait_ge(router_loaded, 32)
            filled(ve, "rt")
            drain("rt", v.tensor_tensor(lg, bank("rt")[:, 0:64].rearrange("p (t e) -> p t e", t=TT),
                                        RB.unsqueeze(1).to_broadcast([P, TT, E]), ALU.add))
            st.settle()
            for tt in range(TT):
                st.did(v.max(top8[:, tt, :], lg[:, tt, :]))
            st.settle()
            st.did(v.tensor_scalar(nm4, top8[:, :, 0], -1.0, None, ALU.mult), lgmax_ready)
            v4 = top8[:, :, TOPK - 1:TOPK].to_broadcast([P, TT, E])
            v.tensor_tensor(gt, lg, v4, ALU.is_gt)
            st.did(v.tensor_tensor(eq, lg, v4, ALU.is_equal))
            st.settle()
            st.did(v.reduce_sum(cgt, gt, AX.X))
            st.settle()
            st.did(v.tensor_scalar(need, cgt, -1.0, float(TOPK), ALU.mult, ALU.add))
            for tt in range(TT):
                st.did(v.tensor_tensor_scan(mask[:, tt, :], eq[:, tt, :], eq[:, tt, :], 0.0, ALU.add, ALU.bypass))
            st.settle()
            for tt in range(TT):
                st.did(v.scalar_tensor_tensor(out=eq[:, tt, :], in0=mask[:, tt, :], scalar=need[:, tt:tt + 1],
                                              in1=eq[:, tt, :], op0=ALU.is_le, op1=ALU.mult))
            st.settle()
            st.did(v.tensor_tensor(mask, gt, eq, ALU.add), mask_ready)
            st.settle()
            ve.wait_ge(lgexp_ready, TT)
            st.did(v.tensor_tensor(cum, cum, mask, ALU.mult))
            st.settle()
            st.did(v.reduce_sum(wsum, cum, AX.X))
            st.settle()
            st.did(v.reciprocal(wrec, wsum))
            st.settle()
            st.did(v.tensor_tensor(wts, cum, wrec.unsqueeze(2).to_broadcast([P, TT, E]), ALU.mult), wts_ready)
            st.settle()
            filled(ve, "pos")
            pp = bank("pos")[:, 0:64].rearrange("p (t e) -> p t e", t=TT)
            drain("pos", v.scalar_tensor_tensor(out=posm, in0=pp, scalar=1.0, in1=mask, op0=ALU.add, op1=ALU.mult))
            st.settle()

            def select(e):
                slots = iota[:, 0:CAP].unsqueeze(1).unsqueeze(1).to_broadcast([P, TT, 2, CAP])
                taken = posm[:, :, bass.ds(e, 2)].unsqueeze(3).to_broadcast([P, TT, 2, CAP])
                v.tensor_tensor(sel.rearrange("p t (f s) -> p t f s", f=2), slots, taken,
                                ALU.is_equal).then_inc(sel_ready, 1)

            def select_weighted(e):
                for tt in range(TT):
                    for f in range(2):
                        ins = v.tensor_scalar(selw[:, tt, CAP * f:CAP * f + CAP], iota[:, 0:CAP],
                                              posm[:, tt, bass.ds(e + f, 1)], wts[:, tt, bass.ds(e + f, 1)],
                                              ALU.is_equal, ALU.mult)
                ins.then_inc(selw_ready, 1)

            def bias_selector(e):
                for f in range(2):
                    v.tensor_copy(onehot[:, f, :], ohtab[:, bass.ds(e + f, 1)].to_broadcast([E, CAP]))

            def drain_gathered(p):
                for part, src in enumerate((gath, gu[0])):
                    ve.wait_ge(gath_filled, p * 2 + part + 1)
                    v.tensor_tensor(hTe[:, 4 * part:4 * part + 4, :], src[:].rearrange("p (k s) -> p k s", k=4),
                                    n2w[:, 4 * part:4 * part + 4].unsqueeze(2).to_broadcast([P, 4, P]),
                                    ALU.mult).then_inc(hTe_ready, 1)

            def activate(i, half):
                c = slice(256 * half, 256 * half + 256)
                ve.wait_ge(gu_filled, i * 2 + half + 1)
                g2 = gu[half][:].rearrange("p (n f) -> p n f", f=2)
                v.tensor_scalar(gate[:, c], g2[:, :, 0], LIMIT, None, ALU.min).then_inc(gate_ready, 1)
                v.tensor_scalar(up[:, c], g2[:, :, 1], LIMIT, -LIMIT, ALU.min, ALU.max).then_inc(gu_drained, 1)
                ve.wait_ge(gu_drained, i * 2 + half + 3)
                v.scalar_tensor_tensor(out=up[:, c], in0=up[:, c], scalar=1.0, in1=gate[:, c],
                                       op0=ALU.add, op1=ALU.mult).then_inc(up_ready, 1)
                ve.wait_ge(up_ready, i * 2 + half + 1)
                ve.wait_ge(sigm_ready, i * 2 + half + 1)
                v.tensor_tensor(act[:, c], up[:, c], sg[:, c], ALU.mult).then_inc(act_ready, 1)

            def drain_actT(i):
                ve.wait_ge(actT_filled, i + 1)
                v.tensor_copy(actT, multi[:].rearrange("p (c s) -> p c s", c=4)).then_inc(actT_ready, 1)

            def pair(p, e, last=False):
                activate(p * 2, 0)
                select_weighted(e)
                if not last:
                    select(e + 2)
                activate(p * 2, 1)
                drain_actT(p * 2)
                activate(p * 2 + 1, 0)
                activate(p * 2 + 1, 1)
                if not last:
                    bias_selector(e + 2)
                    drain_gathered(p + 1)
                drain_actT(p * 2 + 1)

            select(0)
            bias_selector(0)
            filled(ve, "all")
            drain("all", v.reduce_max(CM, bank("all")[:, 0:E], AX.X))
            st.settle()
            st.did(v.tensor_copy(CMI[0:1, 0:1], CM[0:1, 0:1]), rounds_ready)
            filled(ve, "wT")
            drain("wT", v.tensor_copy(wT, bank("wT")[0:E, 0:T]))
            st.settle()
            st.did(v.tensor_copy(SMALL[:, 611:612], eps), gu_drained)
            st.did(v.tensor_copy(SMALL[:, 612:613], eps), gu_drained)
            st.settle()
            most = ve.value_load(CMI[0:1, 0:1], min_val=0, max_val=T)
            drain_gathered(0)
            with ve.Fori(0, E // 2 - 1) as p:
                pair(p, p * 2)
            pair(E // 2 - 1, E - 2, last=True)
            with ve.If(most > CAP):
                with ve.Fori(1, ROUNDS) as r:
                    with ve.If(most > r * CAP):
                        v.tensor_scalar(posm, posm, -float(CAP), None, ALU.add).then_inc(round_moved, 1)
                        bias_selector(0)
                        ve.wait_ge(round_moved, r)
                        select(0)
                        drain_gathered(r * (E // 2))
                        with ve.Fori(0, E // 2 - 1) as p:
                            pair(r * (E // 2) + p, p * 2)
                        pair(r * (E // 2) + (E // 2 - 1), E - 2, last=True)

            f = Steps(ve, fin_step)
            for tt in range(TT):
                ve.wait_ge(moe_done, tt + 1)
                for n in range(2):
                    xs = X[:, tt, 512 * n:512 * n + 512]
                    f.did(v.tensor_tensor(xs, acc[tt][n][:], xs, ALU.add), ss3_ready)
            for tt in range(TT):
                ve.wait_ge(root3_ready, tt + 1)
                f.did(v.reciprocal(rstd[:, tt:tt + 1], rroot[:, tt:tt + 1]))
                f.settle()
                for n in range(2):
                    c = slice(512 * n, 512 * n + 512)
                    f.did(v.scalar_tensor_tensor(out=XN[:, tt, c], in0=X[:, tt, c], scalar=rstd[:, tt:tt + 1],
                                                 in1=FW[:, c], op0=ALU.mult, op1=ALU.mult), out_ready)

        @block.tensor
        def _(pe):
            mm, tr = nc.tensor.matmul, nc.tensor.transpose
            n_unit = [0]

            def begin(name):
                assert UNITS[n_unit[0]][0] == name, (name, UNITS[n_unit[0]])
                if n_unit[0] >= BANKS:
                    wait_drained(pe, UNITS[n_unit[0] - BANKS][0])
                return bank(name)

            def end(ins):
                ins.then_inc(bank_filled, 1)
                n_unit[0] += 1

            def weights(what, name):
                n = LOADS.index(what)
                if name == "f0":
                    pe.wait_ge(first_loaded, 16)
                else:
                    pe.wait_ge(w_loaded[n % RING], 16 * (n // RING + 1))
                return wr4[n % RING] if what in ("mu", "hu") else wr8[n % RING]

            def proj_T(name, what, j, src=HT, kn=KD):
                ps, w = begin(name), weights(what, name)
                for a in range(2):
                    for k in range(kn):
                        c = P * (2 * j + a)
                        ins = mm(ps[:, T * a:T * a + T], w[:, k, c:c + P], src[:, k, :], start=(k == 0), stop=(k == kn - 1))
                end(ins)

            def proj(name, what, tt, src=HT):
                ps, w = begin(name), weights(what, name)
                for k in range(KD):
                    ins = mm(ps[:], src[:, k, P * tt:P * tt + P], w[:, k, :], start=(k == 0), stop=(k == KD - 1))
                end(ins)

            def transposed(name, tt, j):
                ps = begin(name)
                for a in range(4):
                    k = 4 * j + a
                    ins = tr(ps[:, P * a:P * a + P], XN[:, tt, P * k:P * k + P], ident)
                end(ins)

            pe.wait_ge(ident_loaded, 16)
            pe.wait_ge(small_loaded, 64)
            end(tr(begin("rows")[:, 0:28], ROWS[0:28, :], ident[0:28, 0:28]))
            for tt in range(TT):
                pe.wait_ge(xn_ready, tt + 1)
                for j in range(2):
                    transposed(f"xT{tt}{j}", tt, j)
            wait_drained(pe, "xT11")
            for name in ("f0", "f1"):
                proj_T(name, FB, int(name[1]))
            for name in ("q0", "q1"):
                proj_T(name, QB, int(name[1]))
            def wait_lo(what, j):
                who, n = lo_done(what, j)
                pe.wait_ge(lo_ready[who], n)

            def split_T(name, what, j, hi=hT_hi, lo=hT_lo, kn=KD):
                ps = begin(name)
                n = AT_PIECE[what, j]
                w_h, w_l = hi_part(PIECES[n][3]), raw_part(what, j, lo=True)
                pe.wait_ge(hi_ready, n + 1)
                for a in range(2):
                    for w, x in ((w_h, hi), (w_h, lo), (w_l, hi)):
                        if a == 0 and w is w_l:
                            wait_lo(what, j)
                        for k in range(kn):
                            ins = mm(ps[:, T * a:T * a + T], w[:, k, P * a:P * a + P], x[:, k, :],
                                     start=(k == 0 and w is w_h and x is hi), stop=(k == kn - 1 and w is w_l))
                end(ins)

            def split(name, what, tt):
                ps = begin(name)
                n, s = AT_PIECE[what, 1], LOADS.index(what) % RING
                w_h = (hi_a if PIECES[n][3][0] == "A" else hi_b).rearrange("p (j k n) -> p k j n", j=2, k=KD)
                w_l = w_lo[s].rearrange("p (k n) -> p k n", k=KD)
                rows = slice(P * tt, P * tt + P)
                pe.wait_ge(hi_ready, n + 1)
                for k in range(KD):
                    mm(ps[:].rearrange("p (j n) -> p j n", j=2), hT_hi[:, k, rows], w_h[:, k], start=(k == 0), stop=False)
                wait_lo(what, 1)
                for k in range(KD):
                    mm(ps[:], hT_hi[:, k, rows], w_l[:, k, :], start=False, stop=False)
                pe.wait_ge(hT_lo_ready, 1)
                for k in range(KD):
                    ins = mm(ps[:].rearrange("p (j n) -> p j n", j=2), hT_lo[:, k, rows], w_h[:, k], start=False,
                             stop=(k == KD - 1))
                end(ins)

            for tt in range(TT):
                split(f"qa{tt}", QA, tt)
            for tt in range(TT):
                split(f"ka{tt}", KA, tt)

            def level(name):
                if name == "D":
                    pe.wait_ge(qk_ready, 1)
                    lhs, rhs = h3(kf), h3(qs)
                elif name == "X":
                    pe.wait_ge(kx_ready, 1)
                    lhs = rhs = h3(KX)
                else:
                    n = LEVELS.index(int(name[1]))
                    pe.wait_ge(kq_ready, n + 1)
                    lhs = rhs = h3(KQ[n % 2])
                ps = begin(name)
                C = CHUNK
                for h in range(GH):
                    if name == "X":
                        ins = mm(ps[:, P * h:P * h + P], lhs[:, h, 0:P], rhs[:, h, P:T], start=True, stop=True)
                    elif name == "L6":
                        for b in range(2):
                            ins = mm(ps[C * b:C * b + C, C * h:C * h + C], lhs[:, h, P * b:P * b + C],
                                     rhs[:, h, P * b + C:P * b + P], start=True, stop=True)
                    else:
                        for b in range(2):
                            for o in (0, C):
                                c = slice(P * b + o, P * b + o + C)
                                ins = mm(ps[o:o + C, C * (GH * b + h):C * (GH * b + h) + C], lhs[:, h, c], rhs[:, h, c],
                                         start=True, stop=True)
                end(ins)

            for name in ("D", "X", "L6"):
                level(name)
            split("va0", VA, 0)
            level("L5")
            level("L4")
            split("va1", VA, 1)
            level("L3")
            level("L2")
            split("ib0", IB, 0)
            level("L1")
            level("L0")
            split("ib1", IB, 1)

            for raw, u, roped in ((qraw, "qT", q_roped), (kraw, "kT", k_roped)):
                pe.wait_ge(roped, TT)
                for j in range(2):
                    ps = begin(f"{u}{j}")
                    for a in range(2):
                        for tt in range(TT):
                            c = 512 * tt + P * (2 * j + a)
                            ins = tr(ps[:, T * a + P * tt:T * a + P * tt + P], raw[:, c:c + P], ident)
                    end(ins)

            def probs_T(h):
                ps = begin(f"pT{h}")
                pe.wait_ge(prob_ready, h + 1)
                for a in range(3):
                    ins = tr(ps[:, P * a:P * a + P], SM[:, h % 2, P * a:P * a + P], ident)
                end(ins)

            wait_drained(pe, "kT1")
            for h in range(HEADS):
                ps = begin(f"sc{h}")
                r = slice(64 * (h % 2), 64 * (h % 2) + 64)
                for c, q, k in ((0, 0, 0), (128, 1, 1), (256, 1, 0)):
                    ins = mm(ps[:, c:c + P], qT[r, h // 2, P * q:P * q + P], kT[r, h // 2, P * k:P * k + P],
                             start=True, stop=True)
                end(ins)
                split_T(*GATES[h])
                if h >= 1:
                    probs_T(h - 1)

            wait_drained(pe, "ib1")
            wait_drained(pe, "L0")
            wait_drained(pe, "X")
            for j in range(2):
                ps = begin(f"o{j}")
                for a in range(2):
                    h = 2 * j + a
                    c = slice(P * h, P * h + P)
                    mm(ps[:, T * a:T * a + P], ib[:, 0, c], AT[:, 0, h, :], start=True, stop=True)
                    mm(ps[:, T * a + P:T * a + T], ib[:, 1, c], AT[:, 1, h, :], start=True, stop=False)
                    ins = mm(ps[:, T * a + P:T * a + T], ib[:, 0, c], CT[:, h, :], start=False, stop=True)
                end(ins)
            split_T(*GATES[8])
            probs_T(7)
            for j in range(2):
                ps = begin(f"ms{j}")
                pe.wait_ge(osq_ready, j + 1)
                end(mm(ps[:], ones, sq[:, 512 * j:512 * j + 512], start=True, stop=True))
            wait_drained(pe, "pT7")
            for j in range(2):
                ps = begin(f"ya{j}")
                for a in range(2):
                    for q, k, c in ((0, 0, 0), (1, 1, 128), (1, 0, 256)):
                        for f in range(2):
                            h = 4 * j + 2 * a + f
                            ins = mm(ps[64 * f:64 * f + 64, T * a + P * q:T * a + P * q + P],
                                     va[:, k, 64 * h:64 * h + 64], PT[:, h, c:c + P], start=(c < 256), stop=(c != 128))
                end(ins)
            split_T(*GATES[9])
            wait_drained(pe, "ya1")
            pe.wait_ge(ya_lo_ready, 2)
            for j in range(4):
                split_T(f"mu{j}", "mu", j, ya_hi, ya_lo, kn=4)
            pe.wait_ge(yb_ready, 1)
            for j in range(4):
                split_T(f"hu{j}", "hu", j, o_hi, o_lo, kn=4)
            pe.wait_ge(mix_ready, 1)
            for name in ("wo00", "wo01", "wo10"):
                proj(name, f"wo{name[3]}", int(name[2]), src=mixT)
            pe.wait_ge(xn2_ready, 2)
            transposed("h2T00", 0, 0)
            transposed("h2T01", 0, 1)

            def keep_clock(n, free_bank):
                for _ in range(n):
                    mm(free_bank[:], ident, CST[:, 0:512], start=True, stop=True)

            def logits_T(tt):
                ps = begin(f"rt{tt}")
                wait_drained(pe, f"h2T{tt}1")
                pe.wait_ge(router_loaded, 32)
                for k in range(KD):
                    ins = mm(ps[0:E, 0:P], RW[:, k, :], HT[:, k, P * tt:P * tt + P], start=(k == 0), stop=(k == KD - 1))
                end(ins)

            logits_T(0)
            proj("wo11", "wo1", 1, src=mixT)
            wait_drained(pe, "rt0")
            keep_clock(3, bank("rt0"))
            for j in range(2):
                pe.wait_ge(xn2_ready, 3 + j)
                transposed(f"h2T1{j}", 1, j)
            logits_T(1)

            ps = begin("rt")
            for tt in range(TT):
                wait_drained(pe, f"rt{tt}")
                ins = tr(ps[:, E * tt:E * tt + E], lgT[:, P * tt:P * tt + P], ident[0:E, 0:E])
            end(ins)
            keep_clock(2, bank("rt0"))
            ps = begin("pos")
            pe.wait_ge(mask_ready, 1)
            mm(ps[:, 0:2 * E], ucum, mask.rearrange("p t e -> p (t e)"), start=True, stop=False)
            end(mm(ps[:, E:2 * E], ones, mask[:, 0, :], start=False, stop=True))
            ps = begin("all")
            for tt in range(TT):
                ins = mm(ps[:, 0:E], ones, mask[:, tt, :], start=(tt == 0), stop=(tt == TT - 1))
            end(ins)
            ps = begin("wT")
            pe.wait_ge(wts_ready, 1)
            for tt in range(TT):
                ins = tr(ps[0:E, P * tt:P * tt + P], wts[:, tt, 0:E], ident)
            end(ins)

            def gather(p):
                pe.wait_ge(sel_ready, p + 1)
                for part, dst in enumerate((gath, gu[0])):
                    for a in range(4):
                        k = 4 * part + a
                        for tt in range(TT):
                            ins = mm(dst[:, P * a:P * a + P], XN[:, tt, P * k:P * k + P], sel[:, tt, :],
                                     start=(tt == 0), stop=(tt == TT - 1))
                    ins.then_inc(gath_filled, 1)

            def combine():
                for tt in range(TT):
                    for n in range(2):
                        mm(acc[tt][n][:], selT[:, P * tt:P * tt + P], Y[:, 512 * n:512 * n + 512],
                           start=False, stop=True, skip_group_check=True)

            def gate_up(q, i, m, b):
                tok = slice(CAP * b, CAP * b + CAP)

                def one(half, k, slot, kk, start):
                    for g in range(2):
                        c = 1024 * g + 512 * half
                        ins = mm(gu[half][64 * g:64 * g + 64, :], hTe[:, k, tok], gu_slot[slot][:, kk, c:c + 512],
                                 start=start, stop=False)
                    return ins

                for s in range(4):
                    slot = (m + s) % SLOTS
                    pe.wait_ge(slot_loaded[slot], (q * 3 + (m + s) // SLOTS) * 16 + 16)
                    if s < 3:
                        for kk in range(2):
                            for half in range(2):
                                if s == 0 and kk == 0:
                                    pe.wait_ge(gu_drained, i * 2 + half + 1)
                                ins = one(half, 2 * s + kk, slot, kk, s == 0 and kk == 0)
                        ins.then_inc(weights_used, 1)
                    else:
                        for half in range(2):
                            for kk in range(2):
                                ins = one(half, 6 + kk, slot, kk, False)
                            if half == 1:
                                ins.then_inc(weights_used, 1)
                            for g in range(2):
                                c = 1024 * g + 512 * half
                                ins = mm(gu[half][64 * g:64 * g + 64, :], onehot[:, b, :], GU_B[:, c:c + 512],
                                         start=False, stop=True)
                            ins.then_inc(gu_filled, 1)

            def down(q, i, m):
                pe.wait_ge(act_ready, i * 2 + 2)
                pe.wait_ge(y_ready, i + 1)
                for c in range(4):
                    ins = tr(multi[:, P * c:P * c + P], act[:, P * c:P * c + P], ident)
                ins.then_inc(actT_filled, 1)
                pe.wait_ge(actT_ready, i + 1)
                for kh in range(2):
                    slot = (m + kh) % SLOTS
                    pe.wait_ge(slot_loaded[slot], (q * 3 + (m + kh) // SLOTS) * 16 + 16)
                    for k in range(4):
                        for n in range(2):
                            ins = mm(multi[64 * n:64 * n + 64, :], actT[:, k, 64 * kh:64 * kh + 64],
                                     dn_slot[slot][:, k, 512 * n:512 * n + 512], start=(kh == 0 and k == 0),
                                     stop=(kh == 1 and k == 3))
                    ins.then_inc(y_filled if kh else weights_used, 1)

            def four(q, first=None):
                for h in range(2):
                    p, i, m = q * 2 + h, q * 4 + 2 * h, 12 * h
                    pe.wait_ge(hTe_ready, p * 2 + 2)
                    gate_up(q, i, m, 0)
                    if h == 1 or first != "biases":
                        pe.wait_ge(y_ready, i + 1)
                        combine()
                    else:
                        for tt in range(TT):
                            for n in range(2):
                                mm(acc[tt][n][:], wT[:, P * tt:P * tt + P], DN_B[:, 512 * n:512 * n + 512],
                                   start=True, stop=True, skip_group_check=True)
                    down(q, i, m + 4)
                    gate_up(q, i + 1, m + 6, 1)
                    pe.wait_ge(selw_ready, p + 1)
                    pe.wait_ge(y_ready, i + 2)
                    for tt in range(TT):
                        ins = tr(multi[:, P * tt:P * tt + P], selw[:, tt, :], ident)
                    ins.then_inc(selT_filled, 1)
                    if h == 0 or first != "last":
                        pe.wait_ge(gu_drained, i * 2 + 5)
                        gather(p + 1)
                    else:
                        keep_clock(2, gath)
                    pe.wait_ge(selT_drained, p + 1)
                    down(q, i + 1, m + 10)

            keep_clock(1, bank("wo11"))
            gather(0)
            wait_drained(pe, "wT")
            pe.wait_ge(moe_small_loaded, 48)
            pe.wait_ge(rounds_ready, 1)
            most = pe.value_load(CMI[0:1, 0:1], min_val=0, max_val=T)
            four(0, "biases")
            with pe.Fori(1, E // 4 - 1) as q:
                four(q)
            four(E // 4 - 1, "last")
            keep_clock(1, gath)
            pe.wait_ge(y_ready, E + 1)
            with pe.If(most > CAP):
                with pe.Fori(1, ROUNDS) as r:
                    with pe.If(most > r * CAP):
                        pe.wait_ge(gu_drained, r * (2 * E) + 2)
                        gather(r * (E // 2))
                        with pe.Fori(0, E // 4 - 1) as q:
                            four(r * (E // 4) + q)
                        four(r * (E // 4) + (E // 4 - 1), "last")
                        pe.wait_ge(y_ready, (r + 1) * E + 1)
            for tt in range(TT):
                for n in range(2):
                    ins = mm(acc[tt][n][:], selT[:, P * tt:P * tt + P], Y[:, 512 * n:512 * n + 512],
                             start=False, stop=True, skip_group_check=True)
                ins.then_inc(moe_done, 1)


_INS = ['x', 'norm1_w', 'w_in', 'moba_up', 'hgrn_lb_logits', 'hgrn_norm_w', 'hgrn_up', 'w_out', 'norm2_w', 'router_w',
        'router_b', 'w_gate_up', 'b_gate_up', 'w_down', 'b_down', 'final_norm_w']


def shape_constants():
    import numpy as np
    c = np.zeros((P, 1152), np.float32)
    r = np.arange(P)
    c[:, 0:128] = np.eye(P)
    c[:, 128:256] = r[:, None] < r[None, :]
    c[:, 256:384] = 1 + r[None, :] % CAP
    own = np.where(r[None, :] <= r[:, None], 0.0, NEG)
    c[:, 384:512] = own
    c[:, 512:640] = own
    inv = (np.float32(10000.0) ** (-(np.arange(32, dtype=np.float32) * np.float32(2.0) / np.float32(DH)))).astype(np.float32)
    ang = (np.arange(T, dtype=np.float32)[:, None] * inv[None, :]).astype(np.float32)
    for t in range(TT):
        c[:, 768 + 32 * t:800 + 32 * t] = np.cos(ang[P * t:P * t + P])
        c[:, 832 + 32 * t:864 + 32 * t] = np.sin(ang[P * t:P * t + P])
    c[0:E, 896:896 + E] = np.eye(E)
    c[:, 1024:1152] = 1.0
    m = np.zeros((P, NMASK, CHUNK), np.int32)
    step, other = r[:, None] % CHUNK, r[None, 0:CHUNK]
    for lv in range(6):
        m[:, lv] = (((step ^ other) >> lv) == 1) & (step < other)
    m[:, DIAG] = step == other
    return c, m.reshape(P, NMASK * CHUNK)


def kernel(**inputs):
    import numpy as _np
    import concourse.bacc as _bacc
    from concourse import mybir as _mybir
    from concourse.bass_utils import run_bass_kernel_spmd as _run

    nc = _bacc.Bacc("TRN2", target_bir_lowering=False, num_devices=1)
    cst, lmask = shape_constants()
    arrays, args = {}, {}
    for name, a in [(n, _np.ascontiguousarray(inputs[n])) for n in _INS] + [("cst", cst), ("lmask", lmask)]:
        arrays[f"in_{name}_dram"] = a
        args[name] = nc.dram_tensor(f"in_{name}_dram", a.shape, _mybir.dt.from_np(a.dtype), kind="ExternalInput").ap()
    out = nc.dram_tensor("out_0_dram", (1, T, D), F32, kind="ExternalOutput").ap()
    hybrid_block(nc, args, out)
    r = _run(nc, [arrays], core_ids=[0])
    return r.results[0]["out_0_dram"]
```

```python
import concourse.bass as bass
from concourse import mybir
from contextlib import ExitStack

F32 = mybir.dt.float32
F32R = mybir.dt.float32r
I32 = mybir.dt.int32
ALU = mybir.AluOpType
ACT = mybir.ActivationFunctionType
AX = mybir.AxisListType

P = 128
T = 256
TT = T // P
D = 1024
KD = D // P
HEADS, DH = 8, 64
GH, GK = 4, 128
CHUNK = 64
E = 32
TOPK = 4
CAP = 64
ROUNDS = T // CAP
DE = 1024
LIMIT, ALPHA = 7.0, 1.702
EPS = 1e-6
NEG = -1e30
BANKS = 8
SLOTS = 8
SCALE = DH ** -0.5
GROUP = 512
RING = 3
QA, KA, VA, QB, FB, IB, GB, GA0, GA1, GB0, GB1 = range(11)
LEVELS = [6, 5, 4, 3, 2, 1, 0]
NMASK = 7
DIAG = 6

LOADS = [FB, QB, QA, KA, VA, IB, GB, GA0, GA1, GB0, GB1, "mu", "hu", "wo0", "wo1"]

GATES = [("g0", GB, 0), ("g1", GB, 1)] + [(f"ga{j}", GA0 + j // 2, j % 2) for j in range(4)] + \
    [(f"gb{j}", GB0 + j // 2, j % 2) for j in range(4)]
PIECES = [(FB, 1, "dve", ("C", 0), None), (QB, 0, "dve", ("C", 1), None), (QB, 1, "dve", ("C", 0), "f1")] + \
    [(QA, j, "dve", ("A", j), None) for j in range(2)] + [(KA, j, "pool", ("B", j), None) for j in range(2)] + \
    [(VA, j, "dve", ("A", j), "qa1") for j in range(2)] + [(IB, j, "pool", ("B", j), "ka1") for j in range(2)] + \
    [(what, j, "dve", ("A", j), "va1" if n < 2 else GATES[n - 2][0]) for n, (_, what, j) in enumerate(GATES)] + \
    [("mu", j, "pool", ("Q", j), f"gb{2 + j // 2}") for j in range(4)] + \
    [("hu", j, "dve", ("Q", j), f"mu{j}") for j in range(4)] + \
    [("wo1", j, "dve", ("A", j), f"hu{2 * j + 1}") for j in range(2)]
AT_PIECE = {(p[0], p[1]): n for n, p in enumerate(PIECES)}


def lo_done(what, j):
    n = AT_PIECE[what, j]
    who = PIECES[n][2]
    return who, sum(1 for p in PIECES[:n + 1] if p[2] == who)


def bank_units():
    u = [("rows", "dve")] + [(f"xT{tt}{j}", "dve") for tt in range(TT) for j in range(2)]
    u += [("f0", "act"), ("f1", "act"), ("q0", "dve"), ("q1", "dve")]
    u += [("qa0", "act"), ("qa1", "act"), ("ka0", "act"), ("ka1", "act")]
    u += [("D", "dve"), ("X", "dve"), ("L6", "dve"), ("va0", "act"), ("L5", "dve"), ("L4", "dve"), ("va1", "act")]
    u += [("L3", "dve"), ("L2", "dve"), ("ib0", "act"), ("L1", "dve"), ("L0", "dve"), ("ib1", "act")]
    u += [("qT0", "act"), ("qT1", "act"), ("kT0", "act"), ("kT1", "act")]
    fill = ["g0", "g1", "ga0", "ga1", "ga2", "ga3", "gb0", "gb1", "gb2", "gb3"]
    for h in range(HEADS):
        u += [(f"sc{h}", "dve"), (fill[h], "act")] if h else [(fill[0], "act"), ("sc0", "dve")]
        if h >= 1:
            u += [(f"pT{h - 1}", "act")]
    u += [("o0", "act"), ("o1", "act"), (fill[8], "act"), ("pT7", "act"), ("ms0", "act"), ("ms1", "act")]
    u += [("ya0", "act"), ("ya1", "act"), (fill[9], "act")]
    u += [(f"mu{j}", "dve") for j in range(4)] + [(f"hu{j}", "dve") for j in range(4)]
    u += [(n, "dve") for n in ("wo00", "wo10", "wo01", "wo11", "h2T00", "h2T01", "rt0", "h2T10", "h2T11", "rt1", "rt", "pos", "all",
                              "wT")]
    return u


UNITS = bank_units()
AT_UNIT = {name: n for n, (name, _) in enumerate(UNITS)}


def drained(name):
    n = AT_UNIT[name]
    who = UNITS[n][1]
    return who, sum(1 for _, w in UNITS[:n + 1] if w == who)


class Steps:

    def __init__(self, eng, own):
        self.eng, self.own, self.count, self.last = eng, own, {}, None

    def did(self, ins, sem=None, by=1):
        sem = self.own if sem is None else sem
        key = sem.name
        self.count[key] = self.count.get(key, 0) + by
        ins.then_inc(sem, by)
        self.last = (sem, self.count[key])

    def settle(self):
        self.eng.wait_ge(*self.last)


def hybrid_block(nc, A, out):
    ctx = ExitStack()
    with ctx:
        def sb(name, shape, dt=F32):
            return ctx.enter_context(nc.sbuf_tensor(name, shape, dt))

        def sem(name):
            return ctx.enter_context(nc.semaphore(name))

        with ExitStack() as early:
            def over(name, pages, dt=F32R):
                return early.enter_context(nc.sbuf_tensor(name, [P, 1024 * pages], dt))[:]

            hT_hi = over("hT_hi", 2).rearrange("p (k t) -> p k t", k=KD)
            mix_hi = over("mix_hi", 2)
            ya_hi, ya_lo = (mix_hi[:, 1024 * n:1024 * n + 1024].rearrange("p (k t) -> p k t", k=4) for n in range(2))
            mix_hi = mix_hi.rearrange("p (k t) -> p k t", k=KD)
            mix_lo = over("mix_lo", 2).rearrange("p (k t) -> p k t", k=KD)
            hT_lo = over("hT_lo", 2).rearrange("p (k t) -> p k t", k=KD)
            over("skip_m6", 2, F32)
            hi_b = over("hi_b", 4)
            over("skip_s0", 10, F32)
            hi_c = over("hi_c", 4)
            o_lo, o_hi = (hi_c[:, 1024 * n:1024 * n + 1024].rearrange("p (k t) -> p k t", k=4) for n in range(2))
            over("skip_s14", 2, F32)
            hi_a = over("hi_a", 4)
            w_lo = [over(f"w_lo{s}", 4) for s in range(RING)]

        XN = sb("XN", [P, TT, D])
        M = sb("M", [P, 12 * 1024])
        S = sb("S", [P, SLOTS, 4096])
        X = sb("X", [P, TT, D])
        CST = sb("CST", [P, 1152])
        MSK = sb("MSK", [P, NMASK, CHUNK], I32)
        ROWS = sb("ROWS", [32, P])
        COLS = sb("COLS", [P, 32])
        SMALL = sb("SMALL", [P, 640])
        ident, ucum = CST[:, 0:128], CST[:, 128:256]
        iota = CST[:, 256:384]
        amask = CST[:, 384:768]
        rcos = CST[:, 768:832].rearrange("p (t c) -> p t c", t=TT)
        rsin = CST[:, 832:896].rearrange("p (t c) -> p t c", t=TT)
        ohtab = CST[0:E, 896:896 + E]
        ones = CST[:, 1024:1152]

        SF = S[:].rearrange("p s n -> p (s n)")
        wr8 = [S[:, SLOTS - RING + s, :].rearrange("p (k n) -> p k n", k=KD) for s in range(RING)]
        wr4 = [S[:, SLOTS - RING + s, :].rearrange("p (k n) -> p k n", k=4) for s in range(RING)]

        def page(n, c=1):
            return SF[:, 1024 * n:1024 * (n + c)]

        qraw, kraw, rt1, rt2 = page(0), page(1), page(2), page(3)
        qs, kf, bcum, sgq = page(4), page(5), page(6), page(7)
        PT = page(4, 3).rearrange("p (h c) -> p h c", h=HEADS)
        DD = [page(8), page(9)]
        KQ = [page(10), page(11)]
        KX = page(12)
        logf = page(13)
        AT = page(14).rearrange("p (b h t) -> p b h t", b=2, h=GH)
        CT = page(15)[:, 0:512].rearrange("p (h t) -> p h t", h=GH)
        gT, oT, sq, rms = page(9), page(12), page(13), page(8)


        def mpage(n, c=1):
            return M[:, 1024 * n:1024 * (n + c)]

        QKT = mpage(0, 2).rearrange("p (a j t) -> p a j t", a=2, j=4)
        qT, kT = QKT[:, 0], QKT[:, 1]
        VI = mpage(2, 2).rearrange("p (a t n) -> p a t n", a=2, t=TT)
        va, ib = VI[:, 0], VI[:, 1]
        mixT = mpage(2, 2).rearrange("p (k t) -> p k t", k=KD)
        HT = mpage(4, 2).rearrange("p (k t) -> p k t", k=KD)
        HT1 = mpage(8, 2).rearrange("p (k t) -> p k t", k=KD)
        SM = mpage(6)[:, 0:768].rearrange("p (b c) -> p b c", b=2)
        reset = mpage(7)
        gaT, gbT = mpage(8, 2), mpage(10, 2)

        RW = mpage(6)[:, 0:KD * E].rearrange("p (k e) -> p k e", k=KD)
        RB = mpage(6)[:, 256:256 + E]
        lgT = mpage(6)[0:E, 512:512 + T]
        GU_B = mpage(8, 2)[0:E, :]
        DN_B = mpage(8)[E:2 * E, :]
        FW = mpage(11)
        hTe = mpage(0).rearrange("p (k s) -> p k s", k=KD)
        Y = mpage(1)
        gate, up = mpage(2)[:, 0:512], mpage(2)[:, 512:1024]
        sg, act = mpage(3)[:, 0:512], mpage(3)[:, 512:1024]
        actT = mpage(4)[:, 0:512].rearrange("p (c s) -> p c s", c=4)
        selT = mpage(4)[:, 512:768]
        sel = mpage(7)[:, 0:256].rearrange("p (t s) -> p t s", t=TT)
        selw = mpage(7)[:, 256:512].rearrange("p (t s) -> p t s", t=TT)
        wT = mpage(7)[E:2 * E, 512:768]
        onehot = mpage(7)[0:E, 768:896].rearrange("p (f s) -> p f s", f=2)

        KEPT = sb("KEPT", [P, D])
        kept = [KEPT[:], mpage(10), mpage(5), mpage(6)]

        def h3(ap):
            return ap.rearrange("p (h t) -> p h t", h=GH)

        n1w, n2w = COLS[:, 0:8], COLS[:, 8:16]
        lbrow0, lbrow1, hnw = COLS[:, 16:20], COLS[:, 20:24], COLS[:, 24:28]
        ss, rstd, eps = SMALL[:, 0:2], SMALL[:, 2:4], SMALL[:, 4:5]
        rroot = SMALL[:, 5:7]
        lb, oml, lbd = SMALL[:, 8:12], SMALL[:, 12:16], SMALL[:, 16:20]
        dec = SMALL[:, 20:28]
        mx = SMALL[:, 28:30]
        nmx, rsum, rinv = SMALL[:, 32:48], SMALL[:, 48:64], SMALL[:, 64:80]
        top8 = SMALL[:, 80:96].rearrange("p (t c) -> p t c", t=TT)
        cgt, need, nm4, wsum, wrec = (SMALL[:, 96 + 2 * j:98 + 2 * j] for j in range(5))
        CM = SMALL[:, 110:111]
        ssp = SMALL[:, 111:115].rearrange("p (t n) -> p t n", t=TT)
        ssb = SMALL[:, 115:117]
        lg = SMALL[:, 128:192].rearrange("p (t c) -> p t c", t=TT)
        gt = SMALL[:, 192:256].rearrange("p (t c) -> p t c", t=TT)
        eq = SMALL[:, 256:320].rearrange("p (t c) -> p t c", t=TT)
        cum = SMALL[:, 320:384].rearrange("p (t c) -> p t c", t=TT)
        mask = SMALL[:, 384:448].rearrange("p (t c) -> p t c", t=TT)
        posm = SMALL[:, 448:512].rearrange("p (t c) -> p t c", t=TT)
        wts = SMALL[:, 512:576].rearrange("p (t c) -> p t c", t=TT)
        CMI = sb("CMI", [1, 1], I32)

        def hi_part(where):
            buf, j = where
            if buf == "Q":
                return hi_a[:, 1024 * j:1024 * j + 1024].rearrange("p (k n) -> p k n", k=4)
            return {"A": hi_a, "B": hi_b, "C": hi_c}[buf][:, 2048 * j:2048 * j + 2048].rearrange("p (k n) -> p k n", k=KD)

        def raw_part(what, j, lo=False):
            s, kn = LOADS.index(what) % RING, 4 if what in ("mu", "hu") else KD
            whole = w_lo[s].rearrange("p (k n) -> p k n", k=kn) if lo else (wr4 if kn == 4 else wr8)[s]
            return whole[:, :, 256 * j:256 * j + 256]

        PS = [ctx.enter_context(nc.psum_tensor(f"PS{b}", [P, 512], F32)) for b in range(BANKS)]
        acc = [[PS[2 * t + n] for n in range(2)] for t in range(TT)]
        gu = [PS[4], PS[5]]
        gath, multi = PS[6], PS[7]

        def bank(name):
            return PS[AT_UNIT[name] % BANKS]

        x_loaded = [sem(f"x_loaded{tt}") for tt in range(TT)]
        small_loaded, lmask_loaded = sem("small_loaded"), sem("lmask_loaded")
        w_loaded = [sem(f"w_loaded{s}") for s in range(RING)]
        moe_small_loaded = sem("moe_small_loaded")
        bank_filled = sem("bank_filled")
        drained_by = {"act": sem("drained_by_act"), "dve": sem("drained_by_dve")}
        act_step, dve_step, pool_step = sem("act_step"), sem("dve_step"), sem("pool_step")
        pool_ready = sem("pool_ready")
        eps_ready, root_ready, xn_ready = sem("eps_ready"), sem("root_ready"), sem("xn_ready")
        f_ready, logf_ready, sgq_ready = sem("f_ready"), sem("logf_ready"), sem("sgq_ready")
        dec_in_ready, dec_ready = sem("dec_in_ready"), sem("dec_ready")
        lb_in_ready, lb_ready = sem("lb_in_ready"), sem("lb_ready")
        diff_ready, decay_ready, kq_ready, kx_ready, qk_ready = (
            sem(n) for n in ("diff_ready", "decay_ready", "kq_ready", "kx_ready", "qk_ready"))
        q_roped, k_roped = sem("q_roped"), sem("k_roped")
        dx_ready, dx_exp, mix_step = sem("dx_ready"), sem("dx_exp"), sem("mix_step")
        round_moved, fin_step = sem("round_moved"), sem("fin_step")
        smax_ready, exp_ready, prob_ready = sem("smax_ready"), sem("exp_ready"), sem("prob_ready")
        osq_ready, rms_ready, sig_ready, yb_ready, mix_ready = (
            sem(n) for n in ("osq_ready", "rms_ready", "sig_ready", "yb_ready", "mix_ready"))
        res_ready, root2_ready, xn2_ready = sem("res_ready"), sem("root2_ready"), sem("xn2_ready")
        lgmax_ready, lgexp_ready, mask_ready, wts_ready, rounds_ready = (
            sem(n) for n in ("lgmax_ready", "lgexp_ready", "mask_ready", "wts_ready", "rounds_ready"))
        ss3_ready, root3_ready, out_ready, out_stored = (
            sem(n) for n in ("ss3_ready", "root3_ready", "out_ready", "out_stored"))
        ident_loaded = sem("ident_loaded")
        hi_ready, lo_ready = sem("hi_ready"), {"dve": sem("lo_ready_dve"), "pool": sem("lo_ready_pool")}
        hT_hi_ready, hT_lo_ready = sem("hT_hi_ready"), sem("hT_lo_ready")
        mix_hi_ready, mix_lo_ready = sem("mix_hi_ready"), sem("mix_lo_ready")
        ya_lo_ready, o_ready, o_hi_ready = sem("ya_lo_ready"), sem("o_ready"), sem("o_hi_ready")
        first_loaded, cst_loaded, router_loaded = sem("first_loaded"), sem("cst_loaded"), sem("router_loaded")
        slot_loaded = [sem(f"slot_loaded{s}") for s in range(SLOTS)]
        kept_loaded, last_loaded = sem("kept_loaded"), sem("last_loaded")
        weights_used = sem("weights_used")
        selw_ready = sem("selw_ready")
        sel_ready, selT_filled, selT_drained = sem("sel_ready"), sem("selT_filled"), sem("selT_drained")
        gath_filled, hTe_ready = sem("gath_filled"), sem("hTe_ready")
        gu_filled, gu_drained = sem("gu_filled"), sem("gu_drained")
        gate_ready, sigm_ready, act_ready = sem("gate_ready"), sem("sigm_ready"), sem("act_ready")
        up_ready = sem("up_ready")
        actT_filled, actT_ready = sem("actT_filled"), sem("actT_ready")
        y_filled, y_ready, moe_done = sem("y_filled"), sem("y_ready"), sem("moe_done")

        def filled(eng, name):
            eng.wait_ge(bank_filled, AT_UNIT[name] + 1)

        def wait_drained(eng, name):
            who, n = drained(name)
            eng.wait_ge(drained_by[who], n)

        wi = A["w_in"].rearrange("l (k p) n -> p (l k) n", p=P)
        load_src = {"mu": A["moba_up"].rearrange("l (k p) n -> p (l k) n", p=P),
                    "hu": A["hgrn_up"].rearrange("l (k p) n -> p (l k) n", p=P)}
        wo = A["w_out"].rearrange("l (k p) n -> p (l k) n", p=P)
        load_src["wo0"], load_src["wo1"] = wo[:, :, 0:512], wo[:, :, 512:1024]
        for g in range(11):
            load_src[g] = wi[:, :, g * GROUP:(g + 1) * GROUP]
        last_unit = {FB: "f1", QB: "q1", QA: "qa1", KA: "ka1", VA: "va1", IB: "ib1", GB: "g1", GA0: "ga1",
                     GA1: "ga3", GB0: "gb1", GB1: "gb3", "mu": "mu3", "hu": "hu3", "wo0": "wo10", "wo1": "wo11"}

        wgu = A["w_gate_up"].rearrange("l e (k p) n -> (l e) p k n", p=P)
        wdn = A["w_down"].rearrange("l e (k p) n -> (l e) p k n", p=P)
        gu_slot = [S[:, s, :].rearrange("p (k n) -> p k n", k=2) for s in range(SLOTS)]
        dn_slot = [S[:, s, :].rearrange("p (k n) -> p k n", k=4) for s in range(SLOTS)]

        def form_lo(eng, tensor_tensor, what, j):
            n = AT_PIECE[what, j]
            eng.wait_ge(hi_ready, n + 1)
            tensor_tensor(raw_part(what, j, lo=True), raw_part(what, j), hi_part(PIECES[n][3]),
                          ALU.subtract).then_inc(lo_ready[PIECES[n][2]], 1)

        block = ctx.enter_context(nc.Block())

        @block.sync
        def _(sp):
            for tt in range(TT):
                sp.dma_start(X[:, tt, :], A["x"][0, tt * P:(tt + 1) * P, :]).then_inc(x_loaded[tt], 16)
            sp.dma_start(CST[:, 0:128], A["cst"][:, 0:128]).then_inc(ident_loaded, 16)
            def load(e, m, slot=None):
                e, s, slot = e + m // 6, m % 6, (m - 1) % SLOTS if slot is None else slot
                src = wgu[e, :, 2 * s:2 * s + 2, :] if s < 4 else wdn[e, :, 4 * (s - 4):4 * (s - 4) + 4, :]
                if len(src.shape) == 4:
                    src = src[0]
                dst = gu_slot[slot] if s < 4 else dn_slot[slot]
                sp.dma_start(dst, src).then_inc(slot_loaded[slot], 16)

            def keep(k):
                sp.dma_start(kept[k], wgu[1, :, 4 + k // 2, 1024 * (k % 2):1024 * (k % 2) + 1024]).then_inc(kept_loaded, 16)

            for n, what in enumerate(LOADS):
                if what == "mu":
                    keep(0)
                    filled(sp, "kT1")
                    load(0, 0, slot=0)
                if what == "wo0":
                    filled(sp, "ya1")
                    load(0, 1, slot=1)
                if n >= RING:
                    filled(sp, last_unit[LOADS[n - RING]])
                s = n % RING
                dst = wr4[s] if what in ("mu", "hu") else wr8[s]
                if n == 0:
                    sp.dma_start(dst[:, :, 0:256], load_src[what][:, :, 0:256]).then_inc(first_loaded, 16)
                    sp.dma_start(dst[:, :, 256:512], load_src[what][:, :, 256:512]).then_inc(w_loaded[s], 16)
                else:
                    sp.dma_start(dst, load_src[what]).then_inc(w_loaded[s], 16)
                if n == 1:
                    sp.dma_start(CST[:, 128:], A["cst"][:, 128:]).then_inc(cst_loaded, 16)
                    sp.dma_start(MSK[:], A["lmask"].rearrange("p (m t) -> p m t", t=CHUNK)).then_inc(lmask_loaded, 16)

            filled(sp, "hu3")
            for m in (2, 3, 5):
                load(0, m, slot=m)
            sp.wait_ge(mix_ready, 1)
            keep(1)
            filled(sp, "wo11")
            for m in (4, 6, 7):
                load(0, m, slot=m)
            wait_drained(sp, "rt")
            keep(2)
            keep(3)

            def used(q, m):
                i, s = q * 4 + m // 6, m % 6
                if s == 5:
                    sp.wait_ge(y_filled, i + 1)
                elif s == 3:
                    sp.wait_ge(gu_filled, i * 2 + 2)
                else:
                    sp.wait_ge(weights_used, i * 4 + min(s, 3) + 1)

            def load_four(q, e, stop=24):
                for m in range(stop):
                    used(q, m - SLOTS)
                    load(e, m)

            for m in range(SLOTS + 1, 24):
                used(0, m - SLOTS if m > 2 * SLOTS else m - SLOTS - 1)
                load(0, m)
            with sp.Fori(1, E // 4 - 1) as q:
                load_four(q, q * 4)
            load_four(E // 4 - 1, E - 4, stop=23)
            used(E // 4 - 1, 23 - SLOTS)
            last_slot = 22 % SLOTS
            for part, done in ((0, slot_loaded[last_slot]), (1, last_loaded)):
                sp.dma_start(dn_slot[last_slot][:, 2 * part:2 * part + 2, :],
                             wdn[E - 1, :, 4 + 2 * part:6 + 2 * part, :]).then_inc(done, 16)
            sp.wait_ge(rounds_ready, 1)
            most = sp.value_load(CMI[0:1, 0:1], min_val=0, max_val=T)
            with sp.If(most > CAP):
                with sp.Fori(1, ROUNDS) as r:
                    with sp.If(most > r * CAP):
                        with sp.Fori(0, E // 4) as q:
                            load_four(r * (E // 4) + q, q * 4)

        @block.gpsimd
        def _(pool):
            st = Steps(pool, pool_step)
            st.did(nc.gpsimd.memset(reset, 1.0))
            st.settle()
            nc.gpsimd.memset(reset.rearrange("p (c t) -> p c t", t=CHUNK)[:, :, 0:1], 0.0).then_inc(pool_ready, 1)
            nc.gpsimd.memset(page(14), 0.0).then_inc(pool_ready, 1)

            pool.wait_ge(cst_loaded, 16)
            for raw, units, done in ((qraw, "qa", q_roped), (kraw, "ka", k_roped)):
                if units == "qa":
                    for j in range(2):
                        form_lo(pool, nc.gpsimd.tensor_tensor, KA, j)
                for tt in range(TT):
                    wait_drained(pool, f"{units}{tt}")
                    r4 = raw[:, 512 * tt:512 * tt + 512].rearrange("p (h f c) -> p h f c", h=HEADS, f=2)
                    t1 = rt1[:, 512 * tt:512 * tt + 512].rearrange("p (h f c) -> p h f c", h=HEADS, f=2)
                    t2 = rt2[:, 512 * tt:512 * tt + 512].rearrange("p (h f c) -> p h f c", h=HEADS, f=2)
                    cs = rcos[:, tt, :].unsqueeze(1).to_broadcast([P, HEADS, 32])
                    sn = rsin[:, tt, :].unsqueeze(1).to_broadcast([P, HEADS, 32])
                    st.settle()
                    for f in range(2):
                        nc.gpsimd.tensor_tensor(t1[:, :, f, :], r4[:, :, f, :], cs, ALU.mult)
                        ins = nc.gpsimd.tensor_tensor(t2[:, :, f, :], r4[:, :, 1 - f, :], sn, ALU.mult)
                    st.did(ins)
                    st.settle()
                    nc.gpsimd.tensor_tensor(r4[:, :, 0, :], t1[:, :, 0, :], t2[:, :, 0, :], ALU.subtract)
                    st.did(nc.gpsimd.tensor_tensor(r4[:, :, 1, :], t1[:, :, 1, :], t2[:, :, 1, :], ALU.add), done)
            for what, j in ((IB, 0), (IB, 1), ("mu", 0), ("mu", 1), ("mu", 2), ("mu", 3)):
                form_lo(pool, nc.gpsimd.tensor_tensor, what, j)

        @block.scalar
        def _(se):
            st = Steps(se, act_step)
            for r0, n, name in ((0, 8, "norm1_w"), (8, 8, "norm2_w"), (16, 8, "hgrn_lb_logits"), (24, 4, "hgrn_norm_w")):
                se.dma_start(ROWS[r0:r0 + n, :], A[name].rearrange("a (r c) -> (a r) c", c=P)).then_inc(small_loaded, 16)

            def root(dst, src, scale):
                return nc.scalar.activation(dst, src, ACT.Sqrt, bias=eps, scale=scale)

            se.wait_ge(eps_ready, 1)
            st.did(nc.scalar.activation(ssb[:, 0:1], eps, ACT.Sqrt))
            for tt in range(TT):
                se.wait_ge(x_loaded[tt], 16)
                st.did(nc.scalar.activation(XN[:, tt, :], X[:, tt, :], ACT.Square, accum_out=ss[:, tt:tt + 1]))
                st.settle()
                st.did(root(rroot[:, tt:tt + 1], ss[:, tt:tt + 1], 1.0 / D), root_ready)

            se.wait_ge(lb_in_ready, 1)
            st.did(nc.scalar.activation(lbd, lbd, ACT.Exp), lb_ready)

            def copy_out(name, dst, src=None):
                filled(se, name)
                st.did(nc.scalar.copy(dst, bank(name)[:] if src is None else src), drained_by["act"])

            def round_hi(what, j):
                n = AT_PIECE[what, j]
                if PIECES[n][4]:
                    filled(se, PIECES[n][4])
                m = LOADS.index(what)
                se.wait_ge(w_loaded[m % RING], 16 * (m // RING + 1))
                st.did(nc.scalar.copy(hi_part(PIECES[n][3]), raw_part(what, j)), hi_ready)

            wait_drained(se, "xT11")
            st.did(nc.scalar.copy(hT_hi, HT1), hT_hi_ready)
            round_hi(FB, 1)
            filled(se, "f0")
            st.did(nc.scalar.activation(kf[:, 0:512], bank("f0")[:], ACT.Sigmoid), drained_by["act"])
            round_hi(QB, 0)
            filled(se, "f1")
            st.did(nc.scalar.activation(kf[:, 512:1024], bank("f1")[:], ACT.Sigmoid), drained_by["act"])
            round_hi(QB, 1)
            for j in range(2):
                round_hi(QA, j)
            for j in range(2):
                filled(se, f"q{j}")
                st.did(nc.scalar.activation(sgq[:, 512 * j:512 * j + 512], bank(f"q{j}")[:], ACT.Sigmoid), sgq_ready)
                if j == 0:
                    for i in range(2):
                        round_hi(KA, i)
            se.wait_ge(f_ready, 1)
            st.did(nc.scalar.activation(logf[:], bcum[:], ACT.Ln), logf_ready)

            def decays(n):
                lv = LEVELS[n]
                h = 1 << lv
                d4 = DD[n % 2].rearrange("p (b f t) -> p b f t", f=2, t=h)
                se.wait_ge(diff_ready, n + 1)
                nc.scalar.activation(d4[:, :, 0, :], d4[:, :, 0, :], ACT.Exp, scale=-1.0)
                st.did(nc.scalar.activation(d4[:, :, 1, :], d4[:, :, 1, :], ACT.Exp), decay_ready)

            se.wait_ge(dec_in_ready, 1)
            bl = h3(bcum)[:, :, CHUNK - 1:T:CHUNK]
            st.did(nc.scalar.activation(dec.rearrange("p (c h) -> p h c", c=2), bl[:, :, 1:3], ACT.Exp), dec_ready)
            decays(0)
            se.wait_ge(dx_ready, 1)
            dx = h3(KX)[:, :, CHUNK:3 * CHUNK]
            st.did(nc.scalar.activation(dx, dx, ACT.Exp), dx_exp)
            decays(1)
            copy_out("qa0", qraw[:, 0:512])
            copy_out("qa1", qraw[:, 512:1024])
            for j in range(2):
                round_hi(VA, j)
            copy_out("ka0", kraw[:, 0:512])
            copy_out("ka1", kraw[:, 512:1024])
            decays(2)
            for j in range(2):
                round_hi(IB, j)
            copy_out("va0", va[:, 0, :])
            decays(3)
            decays(4)
            copy_out("va1", va[:, 1, :])
            decays(5)
            decays(6)
            for j in range(2):
                round_hi(GB, j)
            copy_out("ib0", ib[:, 0, :])
            copy_out("ib1", ib[:, 1, :])
            for name, dst in (("qT0", qT), ("qT1", qT), ("kT0", kT), ("kT1", kT)):
                j = int(name[2])
                copy_out(name, dst[:, 2 * j:2 * j + 2, :].rearrange("p a t -> p (a t)"))

            gates = [("g0", gT, 0), ("g1", gT, 1)] + [(f"ga{j}", gaT, j) for j in range(4)] + \
                [(f"gb{j}", gbT, j) for j in range(4)]

            def gate_out(n):
                name, dst, j = gates[n]
                copy_out(name, dst[:, 512 * j:512 * j + 512])

            def exps(h):
                se.wait_ge(smax_ready, h + 1)
                s = SM[:, h % 2, :]
                nc.scalar.activation(s[:, 0:128], s[:, 0:128], ACT.Exp, bias=nmx[:, 2 * h:2 * h + 1], scale=SCALE,
                                     accum_out=rsum[:, 2 * h:2 * h + 1])
                st.did(nc.scalar.activation(s[:, 128:384], s[:, 128:384], ACT.Exp, bias=nmx[:, 2 * h + 1:2 * h + 2],
                                            scale=SCALE, accum_out=rsum[:, 2 * h + 1:2 * h + 2]), exp_ready)

            for h in range(HEADS):
                if h >= 1:
                    round_hi(*GATES[h + 1][1:])
                exps(h)
                gate_out(h)
                if h >= 1:
                    copy_out(f"pT{h - 1}", PT[:, h - 1, :], bank(f"pT{h - 1}")[:, 0:384])
            round_hi(*GATES[9][1:])
            for j in range(2):
                filled(se, f"o{j}")
                nc.scalar.activation(sq[:, 512 * j:512 * j + 512], bank(f"o{j}")[:], ACT.Square).then_inc(osq_ready, 1)
                st.did(nc.scalar.copy(oT[:, 512 * j:512 * j + 512], bank(f"o{j}")[:]), drained_by["act"])
            gate_out(8)
            copy_out("pT7", PT[:, 7, :], bank("pT7")[:, 0:384])
            filled(se, "pT7")
            for dst, src in ((RW, A["router_w"].rearrange("l (k p) e -> p (l k) e", p=P)),
                             (RB, A["router_b"].to_broadcast([P, E]))):
                se.dma_start(dst, src).then_inc(router_loaded, 16)
            for j in range(2):
                filled(se, f"ms{j}")
                st.did(root(rms[:, 512 * j:512 * j + 512], bank(f"ms{j}")[:], 1.0 / GK), drained_by["act"])
            for j in range(2):
                round_hi("mu", j)
            filled(se, "ms1")
            st.did(nc.scalar.activation(sq[:], gT[:], ACT.Sigmoid), sig_ready)
            for j in range(2):
                filled(se, f"ya{j}")
                st.did(nc.scalar.copy(ya_hi[:, 2 * j:2 * j + 2, :].rearrange("p a t -> p (a t)"), bank(f"ya{j}")[:]),
                       drained_by["act"])
            st.did(nc.scalar.activation(gaT[:], gaT[:], ACT.Sigmoid), sig_ready)
            gate_out(9)
            st.settle()
            for j in range(2, 4):
                round_hi("mu", j)
            st.did(nc.scalar.activation(gbT[:], gbT[:], ACT.Sigmoid), sig_ready)
            round_hi("hu", 0)
            se.wait_ge(o_ready, 1)
            st.did(nc.scalar.copy(o_hi.rearrange("p k t -> p (k t)"), oT), o_hi_ready)
            for j in range(1, 4):
                round_hi("hu", j)
            round_hi("wo1", 0)
            filled(se, "mu3")
            for j in range(4):
                if j == 3:
                    round_hi("wo1", 1)
                se.wait_ge(mix_step, j + 1)
                st.did(nc.scalar.copy(mix_hi[:, 2 * j:2 * j + 2, :], mixT[:, 2 * j:2 * j + 2, :]), mix_hi_ready)

            se.wait_ge(mix_ready, 1)
            for dst, src in ((GU_B, A["b_gate_up"][0]), (DN_B, A["b_down"][0]),
                             (FW, A["final_norm_w"].unsqueeze(0).to_broadcast([P, D]))):
                se.dma_start(dst, src).then_inc(moe_small_loaded, 16)

            for n in range(2):
                for tt in range(TT):
                    c = slice(512 * n, 512 * n + 512)
                    se.wait_ge(res_ready, 2 * n + tt + 1)
                    st.did(nc.scalar.activation(XN[:, tt, c], X[:, tt, c], ACT.Square, accum_out=ssp[:, tt, n:n + 1]))
                    st.settle()
                    if n == 0:
                        st.did(nc.scalar.activation(ssb[:, tt:tt + 1], ssp[:, tt, 0:1], ACT.Identity, bias=eps,
                                                    scale=1.0 / D))
                    else:
                        st.did(nc.scalar.activation(rroot[:, tt:tt + 1], ssp[:, tt, 1:2], ACT.Sqrt,
                                                    bias=ssb[:, tt:tt + 1], scale=1.0 / D), root2_ready)
            se.wait_ge(lgmax_ready, 1)
            for tt in range(TT):
                st.did(nc.scalar.activation(cum[:, tt, :], lg[:, tt, :], ACT.Exp, bias=nm4[:, tt:tt + 1]), lgexp_ready)
            st.settle()
            nc.scalar.copy(nm4, nm4).then_inc(y_ready, 1)

            def expert(i, b):
                for half in range(2):
                    se.wait_ge(gate_ready, 2 * i + half + 1)
                    c = slice(256 * half, 256 * half + 256)
                    nc.scalar.activation(sg[:, c], gate[:, c], ACT.Sigmoid, scale=ALPHA).then_inc(sigm_ready, 1)

            def drain_y(i, b):
                se.wait_ge(y_filled, i + 1)
                rows = slice(64 * b, 64 * b + 64)
                nc.scalar.copy(Y[rows, 0:512], multi[0:64, :])
                nc.scalar.copy(Y[rows, 512:1024], multi[64:128, :]).then_inc(y_ready, 1)

            def pair(p):
                expert(p * 2, 0)
                drain_y(p * 2, 0)
                expert(p * 2 + 1, 1)
                se.wait_ge(selT_filled, p + 1)
                nc.scalar.copy(selT, multi[:, 0:T]).then_inc(selT_drained, 1)
                drain_y(p * 2 + 1, 1)

            se.wait_ge(rounds_ready, 1)
            most = se.value_load(CMI[0:1, 0:1], min_val=0, max_val=T)
            with se.Fori(0, E // 2) as p:
                pair(p)
            with se.If(most > CAP):
                with se.Fori(1, ROUNDS) as r:
                    with se.If(most > r * CAP):
                        with se.Fori(0, E // 2) as p:
                            pair(r * (E // 2) + p)
            nc.scalar.activation(ssb[:, 0:1], eps, ACT.Sqrt)

            done = st.count[act_step.name]
            for tt in range(TT):
                for n in range(2):
                    c = slice(512 * n, 512 * n + 512)
                    done += 1
                    se.wait_ge(ss3_ready, 2 * tt + n + 1)
                    nc.scalar.activation(XN[:, tt, c], X[:, tt, c], ACT.Square,
                                         accum_out=ssp[:, tt, n:n + 1]).then_inc(act_step, 1)
                    se.wait_ge(act_step, done)
                    if n == 0:
                        done += 1
                        nc.scalar.activation(ssb[:, tt:tt + 1], ssp[:, tt, 0:1], ACT.Identity, bias=eps,
                                             scale=1.0 / D).then_inc(act_step, 1)
                nc.scalar.activation(rroot[:, tt:tt + 1], ssp[:, tt, 1:2], ACT.Sqrt, bias=ssb[:, tt:tt + 1],
                                     scale=1.0 / D).then_inc(root3_ready, 1)
            for tt in range(TT):
                for n in range(2):
                    c = slice(512 * n, 512 * n + 512)
                    se.wait_ge(out_ready, 2 * tt + n + 1)
                    se.dma_start(out[0, tt * P:(tt + 1) * P, c], XN[:, tt, c]).then_inc(out_stored, 16)
            se.wait_ge(out_stored, 16 * 2 * TT)

        @block.vector
        def _(ve):
            st = Steps(ve, dve_step)
            v = nc.vector

            def drain(name, ins):
                st.did(ins, drained_by["dve"])

            st.did(v.memset(eps, EPS), eps_ready)
            filled(ve, "rows")
            drain("rows", v.tensor_copy(COLS[:, 0:28], bank("rows")[:, 0:28]))
            st.settle()
            lbm = SMALL[:, 600:604]
            e1 = SMALL[:, 604:608]
            st.did(v.tensor_tensor(lbm, lbrow0, lbrow1, ALU.max))
            st.settle()
            st.did(v.tensor_tensor(lbrow0, lbrow0, lbm, ALU.subtract))
            st.did(v.tensor_tensor(lbrow1, lbrow1, lbm, ALU.subtract))
            st.settle()
            st.did(v.tensor_tensor(lbd, lbrow1, lbrow0, ALU.subtract), lb_in_ready)

            def weighted_T(name, tt, j, w, dst):
                filled(ve, name)
                drain(name, v.tensor_tensor(dst[:, 4 * j:4 * j + 4, P * tt:P * tt + P],
                                            bank(name)[:].rearrange("p (k t) -> p k t", k=4),
                                            w[:, 4 * j:4 * j + 4].unsqueeze(2).to_broadcast([P, 4, P]), ALU.mult))

            for tt in range(TT):
                ve.wait_ge(root_ready, tt + 1)
                st.did(v.reciprocal(rstd[:, tt:tt + 1], rroot[:, tt:tt + 1]))
                st.settle()
                st.did(v.tensor_scalar(XN[:, tt, :], X[:, tt, :], rstd[:, tt:tt + 1], None, ALU.mult), xn_ready)
            for tt in range(TT):
                for j in range(2):
                    weighted_T(f"xT{tt}{j}", tt, j, n1w, HT1)
            def lo(what, j):
                form_lo(ve, v.tensor_tensor, what, j)

            ve.wait_ge(hT_hi_ready, 1)
            st.did(v.tensor_tensor(hT_lo, HT1, hT_hi, ALU.subtract), hT_lo_ready)
            ve.wait_ge(lb_ready, 1)
            st.did(v.tensor_scalar(lbm, lbd, 1.0, None, ALU.add))
            st.settle()
            st.did(v.reciprocal(lb, lbm))
            st.settle()
            st.did(v.tensor_scalar(oml, lb, -1.0, 1.0, ALU.mult, ALU.add))
            st.settle()

            lo(FB, 1)
            lo(QB, 0)
            wait_drained(ve, "f1")
            for h in range(GH):
                c = slice(T * h, T * h + T)
                st.did(v.tensor_scalar(bcum[:, c], kf[:, c], oml[:, h:h + 1], lb[:, h:h + 1], ALU.mult, ALU.add), f_ready if h == GH - 1 else None)
            st.settle()
            st.did(v.tensor_scalar(kf[:], bcum[:], -1.0, 1.0, ALU.mult, ALU.add))
            lo(QB, 1)
            for j in range(2):
                lo(QA, j)
            for j in range(2):
                ve.wait_ge(sgq_ready, j + 1)
                c = slice(512 * j, 512 * j + 512)
                drain(f"q{j}", v.tensor_tensor(qs[:, c], bank(f"q{j}")[:], sgq[:, c], ALU.mult))
            ve.wait_ge(drained_by["dve"], st.count[drained_by["dve"].name])
            st.did(v.tensor_scalar(SMALL[:, 608:609], eps, 1.0, None, ALU.mult), qk_ready)
            ve.wait_ge(logf_ready, 1)
            ve.wait_ge(pool_ready, 1)
            st.did(v.tensor_tensor_scan(bcum[:], reset, logf[:], 0.0, ALU.mult, ALU.add), dec_in_ready)
            st.settle()

            def differences(n):
                lv = LEVELS[n]
                h = 1 << lv
                if n >= 2:
                    ve.wait_ge(kq_ready, n - 1)
                if lv == 6:
                    d4 = DD[n % 2].rearrange("p (b f t) -> p b f t", f=2, t=h)
                    b4 = bcum.rearrange("p (b f t) -> p b f t", f=2, t=h)
                    v.tensor_tensor(d4[:, :, 0, :], b4[:, :, 0, :], b4[:, :, 0, h - 1:h].to_broadcast([P, 8, h]),
                                    ALU.subtract)
                    st.did(v.tensor_copy(d4[:, :, 1, :], b4[:, :, 1, :]), diff_ready)
                else:
                    n_b = 1024 // (2 * h)
                    d3 = DD[n % 2].rearrange("p (b t) -> p b t", t=2 * h)
                    b3 = bcum.rearrange("p (b t) -> p b t", t=2 * h)
                    st.did(v.tensor_tensor(d3, b3, b3[:, :, h - 1:h].to_broadcast([P, n_b, 2 * h]), ALU.subtract),
                           diff_ready)

            def factors(n):
                lv = LEVELS[n]
                h = 1 << lv
                ve.wait_ge(decay_ready, n + 1)
                if n >= 2:
                    filled(ve, f"L{LEVELS[n - 2]}")
                kq4, d4, k4, q4 = (a.rearrange("p (b f t) -> p b f t", f=2, t=h)
                                   for a in (KQ[n % 2], DD[n % 2], kf, qs))
                v.tensor_tensor(kq4[:, :, 0, :], k4[:, :, 0, :], d4[:, :, 0, :], ALU.mult)
                st.did(v.tensor_tensor(kq4[:, :, 1, :], q4[:, :, 1, :], d4[:, :, 1, :], ALU.mult), kq_ready)

            def cross_factors():
                kx, kq, b3, k3, q3 = (h3(a) for a in (KX, KQ[0], bcum, kf, qs))
                dx = h3(KX)
                C = CHUNK
                st.settle()
                v.tensor_tensor(dx[:, :, C:2 * C], b3[:, :, 2 * C - 1:2 * C].to_broadcast([P, GH, C]), b3[:, :, C:2 * C],
                                ALU.subtract)
                st.did(v.tensor_copy(dx[:, :, 2 * C:3 * C], b3[:, :, 2 * C:3 * C]), dx_ready)
                ve.wait_ge(dx_exp, 1)
                v.tensor_tensor(kx[:, :, C:2 * C], k3[:, :, C:2 * C], dx[:, :, C:2 * C], ALU.mult)
                v.tensor_tensor(kx[:, :, 2 * C:3 * C], q3[:, :, 2 * C:3 * C], dx[:, :, 2 * C:3 * C], ALU.mult)
                ve.wait_ge(dec_ready, 1)
                v.tensor_tensor(kx[:, :, 0:C], kq[:, :, 0:C], dec[:, 0:4].unsqueeze(2).to_broadcast([P, GH, C]), ALU.mult)
                st.did(v.tensor_tensor(kx[:, :, 3 * C:4 * C], kq[:, :, 3 * C:4 * C],
                                       dec[:, 4:8].unsqueeze(2).to_broadcast([P, GH, C]), ALU.mult), kx_ready)

            halves = AT.rearrange("p b h t -> p (b h) t")

            def take_level(name, m):
                filled(ve, name)
                for o in (0, CHUNK):
                    r = slice(o, o + CHUNK)
                    ins = v.copy_predicated(halves[r, :, r], MSK[r, m, :].unsqueeze(1).to_broadcast([CHUNK, 8, CHUNK]),
                                            bank(name)[r, :].rearrange("p (b t) -> p b t", t=CHUNK))
                drain(name, ins)
                st.settle()

            def take_level6():
                filled(ve, "L6")
                for b in range(2):
                    src = bank("L6")[CHUNK * b:CHUNK * b + CHUNK, 0:GH * CHUNK].rearrange("p (h t) -> p h t", h=GH)
                    ins = v.tensor_copy(AT[0:CHUNK, b, :, CHUNK:P], src)
                drain("L6", ins)
                st.settle()

            differences(0)
            differences(1)
            factors(0)
            cross_factors()
            ve.wait_ge(lmask_loaded, 16)
            ve.wait_ge(pool_ready, 2)
            factors(1)
            for j in range(2):
                lo(VA, j)
            take_level("D", DIAG)
            filled(ve, "X")
            drain("X", v.tensor_copy(CT.rearrange("p h t -> p (h t)"), bank("X")[:]))
            for n in range(len(LEVELS)):
                if n + 2 < len(LEVELS):
                    differences(n + 2)
                if LEVELS[n] == 6:
                    take_level6()
                else:
                    take_level(f"L{LEVELS[n]}", LEVELS[n])
                if n + 2 < len(LEVELS):
                    factors(n + 2)

            def softmax_max(h):
                filled(ve, f"sc{h}")
                if h >= 2:
                    filled(ve, f"pT{h - 2}")
                s = SM[:, h % 2, :]
                drain(f"sc{h}", v.tensor_tensor(s, bank(f"sc{h}")[:, 0:384], amask, ALU.add))
                st.settle()
                st.did(v.reduce_max(mx[:, 0:1], s[:, 0:128], AX.X))
                st.did(v.reduce_max(mx[:, 1:2], s[:, 128:384], AX.X))
                st.settle()
                st.did(v.tensor_scalar(nmx[:, 2 * h:2 * h + 2], mx, -SCALE, None, ALU.mult), smax_ready)

            def softmax_norm(h):
                ve.wait_ge(exp_ready, h + 1)
                s = SM[:, h % 2, :]
                st.did(v.reciprocal(rinv[:, 2 * h:2 * h + 2], rsum[:, 2 * h:2 * h + 2]))
                st.settle()
                v.tensor_scalar(s[:, 0:128], s[:, 0:128], rinv[:, 2 * h:2 * h + 1], None, ALU.mult)
                st.did(v.tensor_scalar(s[:, 128:384], s[:, 128:384], rinv[:, 2 * h + 1:2 * h + 2], None, ALU.mult),
                       prob_ready)

            lo(GB, 0)
            lo(GB, 1)
            for h in range(HEADS):
                softmax_max(h)
                if h >= 1:
                    lo(*GATES[h + 1][1:])
                softmax_norm(h)
            lo(*GATES[9][1:])

            for j in range(2):
                wait_drained(ve, f"ms{j}")
                c = slice(512 * j, 512 * j + 512)
                st.did(v.reciprocal(rms[:, c], rms[:, c]))
            wait_drained(ve, "ya1")
            for j in range(2):
                st.did(v.tensor_tensor(ya_lo[:, 2 * j:2 * j + 2, :].rearrange("p a t -> p (a t)"), bank(f"ya{j}")[:],
                                       ya_hi[:, 2 * j:2 * j + 2, :].rearrange("p a t -> p (a t)"), ALU.subtract),
                       ya_lo_ready)
            ve.wait_ge(dve_step, st.count[dve_step.name])
            for h in range(GH):
                c = slice(T * h, T * h + T)
                st.did(v.scalar_tensor_tensor(out=oT[:, c], in0=oT[:, c], scalar=hnw[:, h:h + 1], in1=rms[:, c],
                                              op0=ALU.mult, op1=ALU.mult))
            ve.wait_ge(sig_ready, 1)
            st.did(v.tensor_tensor(sq[:], sq[:], gT[:], ALU.mult))
            st.settle()
            st.did(v.tensor_tensor(oT[:], oT[:], sq[:], ALU.mult), o_ready)

            flat = mixT.rearrange("p k t -> p (k t)")
            ve.wait_ge(sig_ready, 2)
            for j in range(4):
                c = slice(512 * j, 512 * j + 512)
                filled(ve, f"mu{j}")
                drain(f"mu{j}", v.tensor_tensor(flat[:, c], bank(f"mu{j}")[:], gaT[:, c], ALU.mult))
                if j == 0:
                    ve.wait_ge(o_hi_ready, 1)
                    st.did(v.tensor_tensor(o_lo.rearrange("p k t -> p (k t)"), oT, o_hi.rearrange("p k t -> p (k t)"),
                                           ALU.subtract), yb_ready)
                lo("hu", j)
            for j in range(4):
                c = slice(512 * j, 512 * j + 512)
                ve.wait_ge(sig_ready, 3)
                filled(ve, f"hu{j}")
                drain(f"hu{j}", v.tensor_tensor(gbT[:, c], bank(f"hu{j}")[:], gbT[:, c], ALU.mult))
                st.settle()
                st.did(v.tensor_tensor(flat[:, c], flat[:, c], gbT[:, c], ALU.add), mix_step)
            st.settle()
            st.did(v.tensor_scalar(SMALL[:, 609:610], eps, 1.0, None, ALU.mult), mix_ready)
            def residual(tt, n):
                name = f"wo{tt}{n}"
                filled(ve, name)
                xs = X[:, tt, 512 * n:512 * n + 512]
                drain(name, v.tensor_tensor(xs, bank(name)[:], xs, ALU.add))
                st.settle()
                st.did(v.tensor_copy(SMALL[:, 610:611], eps), res_ready)

            def normalise(tt):
                ve.wait_ge(root2_ready, tt + 1)
                st.did(v.reciprocal(rstd[:, tt:tt + 1], rroot[:, tt:tt + 1]))
                st.settle()
                for n in range(2):
                    c = slice(512 * n, 512 * n + 512)
                    st.did(v.tensor_scalar(XN[:, tt, c], X[:, tt, c], rstd[:, tt:tt + 1], None, ALU.mult), xn2_ready)

            def drain_logits(tt):
                filled(ve, f"rt{tt}")
                drain(f"rt{tt}", v.tensor_copy(lgT[:, P * tt:P * tt + P], bank(f"rt{tt}")[0:E, 0:P]))

            lo("wo1", 0)
            lo("wo1", 1)
            residual(0, 0)
            residual(1, 0)
            ve.wait_ge(mix_hi_ready, 4)
            st.did(v.tensor_tensor(mix_lo, mixT, mix_hi, ALU.subtract), mix_lo_ready)
            residual(0, 1)
            normalise(0)
            residual(1, 1)
            weighted_T("h2T00", 0, 0, n2w, HT)
            weighted_T("h2T01", 0, 1, n2w, HT)
            normalise(1)
            drain_logits(0)
            weighted_T("h2T10", 1, 0, n2w, HT)
            weighted_T("h2T11", 1, 1, n2w, HT)

            drain_logits(1)
            ve.wait_ge(router_loaded, 32)
            filled(ve, "rt")
            drain("rt", v.tensor_tensor(lg, bank("rt")[:, 0:64].rearrange("p (t e) -> p t e", t=TT),
                                        RB.unsqueeze(1).to_broadcast([P, TT, E]), ALU.add))
            st.settle()
            for tt in range(TT):
                st.did(v.max(top8[:, tt, :], lg[:, tt, :]))
            st.settle()
            st.did(v.tensor_scalar(nm4, top8[:, :, 0], -1.0, None, ALU.mult), lgmax_ready)
            v4 = top8[:, :, TOPK - 1:TOPK].to_broadcast([P, TT, E])
            v.tensor_tensor(gt, lg, v4, ALU.is_gt)
            st.did(v.tensor_tensor(eq, lg, v4, ALU.is_equal))
            st.settle()
            st.did(v.reduce_sum(cgt, gt, AX.X))
            st.settle()
            st.did(v.tensor_scalar(need, cgt, -1.0, float(TOPK), ALU.mult, ALU.add))
            for tt in range(TT):
                st.did(v.tensor_tensor_scan(mask[:, tt, :], eq[:, tt, :], eq[:, tt, :], 0.0, ALU.add, ALU.bypass))
            st.settle()
            for tt in range(TT):
                st.did(v.scalar_tensor_tensor(out=eq[:, tt, :], in0=mask[:, tt, :], scalar=need[:, tt:tt + 1],
                                              in1=eq[:, tt, :], op0=ALU.is_le, op1=ALU.mult))
            st.settle()
            st.did(v.tensor_tensor(mask, gt, eq, ALU.add), mask_ready)
            st.settle()
            ve.wait_ge(lgexp_ready, TT)
            st.did(v.tensor_tensor(cum, cum, mask, ALU.mult))
            st.settle()
            st.did(v.reduce_sum(wsum, cum, AX.X))
            st.settle()
            st.did(v.reciprocal(wrec, wsum))
            st.settle()
            st.did(v.tensor_tensor(wts, cum, wrec.unsqueeze(2).to_broadcast([P, TT, E]), ALU.mult), wts_ready)
            st.settle()
            filled(ve, "pos")
            pp = bank("pos")[:, 0:64].rearrange("p (t e) -> p t e", t=TT)
            drain("pos", v.scalar_tensor_tensor(out=posm, in0=pp, scalar=1.0, in1=mask, op0=ALU.add, op1=ALU.mult))
            st.settle()

            def select(e):
                slots = iota[:, 0:CAP].unsqueeze(1).unsqueeze(1).to_broadcast([P, TT, 2, CAP])
                taken = posm[:, :, bass.ds(e, 2)].unsqueeze(3).to_broadcast([P, TT, 2, CAP])
                v.tensor_tensor(sel.rearrange("p t (f s) -> p t f s", f=2), slots, taken,
                                ALU.is_equal).then_inc(sel_ready, 1)

            def select_weighted(e):
                for tt in range(TT):
                    for f in range(2):
                        ins = v.tensor_scalar(selw[:, tt, CAP * f:CAP * f + CAP], iota[:, 0:CAP],
                                              posm[:, tt, bass.ds(e + f, 1)], wts[:, tt, bass.ds(e + f, 1)],
                                              ALU.is_equal, ALU.mult)
                ins.then_inc(selw_ready, 1)

            def bias_selector(e):
                for f in range(2):
                    v.tensor_copy(onehot[:, f, :], ohtab[:, bass.ds(e + f, 1)].to_broadcast([E, CAP]))

            def drain_gathered(p):
                for part, src in enumerate((gath, multi if isinstance(p, int) and p == 0 else gu[0])):
                    ve.wait_ge(gath_filled, p * 2 + part + 1)
                    v.tensor_tensor(hTe[:, 4 * part:4 * part + 4, :], src[:].rearrange("p (k s) -> p k s", k=4),
                                    n2w[:, 4 * part:4 * part + 4].unsqueeze(2).to_broadcast([P, 4, P]),
                                    ALU.mult).then_inc(hTe_ready, 1)

            def activate(i, half):
                c = slice(256 * half, 256 * half + 256)
                ve.wait_ge(gu_filled, i * 2 + half + 1)
                g2 = gu[half][:].rearrange("p (n f) -> p n f", f=2)
                v.tensor_scalar(gate[:, c], g2[:, :, 0], LIMIT, None, ALU.min).then_inc(gate_ready, 1)
                v.tensor_scalar(up[:, c], g2[:, :, 1], LIMIT, -LIMIT, ALU.min, ALU.max).then_inc(gu_drained, 1)
                ve.wait_ge(gu_drained, i * 2 + half + 3)
                v.scalar_tensor_tensor(out=up[:, c], in0=up[:, c], scalar=1.0, in1=gate[:, c],
                                       op0=ALU.add, op1=ALU.mult).then_inc(up_ready, 1)
                ve.wait_ge(up_ready, i * 2 + half + 1)
                ve.wait_ge(sigm_ready, i * 2 + half + 1)
                v.tensor_tensor(act[:, c], up[:, c], sg[:, c], ALU.mult).then_inc(act_ready, 1)

            def drain_actT(i):
                ve.wait_ge(actT_filled, i + 1)
                v.tensor_copy(actT, multi[:].rearrange("p (c s) -> p c s", c=4)).then_inc(actT_ready, 1)

            def pair(p, e, last=False):
                activate(p * 2, 0)
                select_weighted(e)
                if not last:
                    select(e + 2)
                activate(p * 2, 1)
                drain_actT(p * 2)
                activate(p * 2 + 1, 0)
                activate(p * 2 + 1, 1)
                if not last:
                    bias_selector(e + 2)
                    drain_gathered(p + 1)
                drain_actT(p * 2 + 1)

            select(0)
            bias_selector(0)
            filled(ve, "all")
            drain("all", v.reduce_max(CM, bank("all")[:, 0:E], AX.X))
            st.settle()
            st.did(v.tensor_copy(CMI[0:1, 0:1], CM[0:1, 0:1]), rounds_ready)
            filled(ve, "wT")
            drain("wT", v.tensor_copy(wT, bank("wT")[0:E, 0:T]))
            st.settle()
            st.did(v.tensor_copy(SMALL[:, 611:612], eps), gu_drained)
            st.did(v.tensor_copy(SMALL[:, 612:613], eps), gu_drained)
            st.settle()
            most = ve.value_load(CMI[0:1, 0:1], min_val=0, max_val=T)
            drain_gathered(0)
            with ve.Fori(0, E // 2 - 1) as p:
                pair(p, p * 2)
            pair(E // 2 - 1, E - 2, last=True)
            with ve.If(most > CAP):
                with ve.Fori(1, ROUNDS) as r:
                    with ve.If(most > r * CAP):
                        v.tensor_scalar(posm, posm, -float(CAP), None, ALU.add).then_inc(round_moved, 1)
                        bias_selector(0)
                        ve.wait_ge(round_moved, r)
                        select(0)
                        drain_gathered(r * (E // 2))
                        with ve.Fori(0, E // 2 - 1) as p:
                            pair(r * (E // 2) + p, p * 2)
                        pair(r * (E // 2) + (E // 2 - 1), E - 2, last=True)

            f = Steps(ve, fin_step)
            for tt in range(TT):
                ve.wait_ge(moe_done, tt + 1)
                for n in range(2):
                    xs = X[:, tt, 512 * n:512 * n + 512]
                    f.did(v.tensor_tensor(xs, acc[tt][n][:], xs, ALU.add), ss3_ready)
            for tt in range(TT):
                ve.wait_ge(root3_ready, tt + 1)
                f.did(v.reciprocal(rstd[:, tt:tt + 1], rroot[:, tt:tt + 1]))
                f.settle()
                for n in range(2):
                    c = slice(512 * n, 512 * n + 512)
                    f.did(v.scalar_tensor_tensor(out=XN[:, tt, c], in0=X[:, tt, c], scalar=rstd[:, tt:tt + 1],
                                                 in1=FW[:, c], op0=ALU.mult, op1=ALU.mult), out_ready)

        @block.tensor
        def _(pe):
            mm, tr = nc.tensor.matmul, nc.tensor.transpose
            n_unit = [0]

            def begin(name):
                assert UNITS[n_unit[0]][0] == name, (name, UNITS[n_unit[0]])
                if n_unit[0] >= BANKS:
                    wait_drained(pe, UNITS[n_unit[0] - BANKS][0])
                return bank(name)

            def end(ins):
                ins.then_inc(bank_filled, 1)
                n_unit[0] += 1

            def weights(what, name):
                n = LOADS.index(what)
                if name == "f0":
                    pe.wait_ge(first_loaded, 16)
                else:
                    pe.wait_ge(w_loaded[n % RING], 16 * (n // RING + 1))
                return wr4[n % RING] if what in ("mu", "hu") else wr8[n % RING]

            def proj_T(name, what, j, src, kn=KD):
                ps, w = begin(name), weights(what, name)
                for a in range(2):
                    for k in range(kn):
                        c = P * (2 * j + a)
                        ins = mm(ps[:, T * a:T * a + T], w[:, k, c:c + P], src[:, k, :], start=(k == 0), stop=(k == kn - 1))
                end(ins)

            def proj(name, what, tt, src):
                ps, w = begin(name), weights(what, name)
                for k in range(KD):
                    if name == "wo00" and k % 2 == 0:
                        pe.wait_ge(mix_step, k // 2 + 1)
                    ins = mm(ps[:], src[:, k, P * tt:P * tt + P], w[:, k, :], start=(k == 0), stop=(k == KD - 1))
                end(ins)

            def transposed(name, tt, j):
                ps = begin(name)
                for a in range(4):
                    k = 4 * j + a
                    ins = tr(ps[:, P * a:P * a + P], XN[:, tt, P * k:P * k + P], ident)
                end(ins)

            pe.wait_ge(ident_loaded, 16)
            pe.wait_ge(small_loaded, 64)
            end(tr(begin("rows")[:, 0:28], ROWS[0:28, :], ident[0:28, 0:28]))
            for tt in range(TT):
                pe.wait_ge(xn_ready, tt + 1)
                for j in range(2):
                    transposed(f"xT{tt}{j}", tt, j)
            wait_drained(pe, "xT11")
            proj_T("f0", FB, 0, HT1)
            def wait_lo(what, j):
                who, n = lo_done(what, j)
                pe.wait_ge(lo_ready[who], n)

            def split_T(name, what, j, hi=hT_hi, lo=hT_lo, lo_there=(hT_lo_ready, 1), kn=KD):
                ps = begin(name)
                n = AT_PIECE[what, j]
                w_h, w_l = hi_part(PIECES[n][3]), raw_part(what, j, lo=True)
                pe.wait_ge(hi_ready, n + 1)
                for a in range(2):
                    for w, x in ((w_h, hi), (w_l, hi), (w_h, lo)):
                        if a == 0 and w is w_l:
                            wait_lo(what, j)
                        if a == 0 and x is lo:
                            pe.wait_ge(*lo_there)
                        for k in range(kn):
                            ins = mm(ps[:, T * a:T * a + T], w[:, k, P * a:P * a + P], x[:, k, :],
                                     start=(k == 0 and w is w_h and x is hi), stop=(k == kn - 1 and x is lo))
                end(ins)

            def split(name, what, tt, hi=hT_hi, lo=hT_lo, lo_there=(hT_lo_ready, 1)):
                ps = begin(name)
                n, s = AT_PIECE[what, 1], LOADS.index(what) % RING
                w_h = (hi_a if PIECES[n][3][0] == "A" else hi_b).rearrange("p (j k n) -> p k j n", j=2, k=KD)
                w_l = w_lo[s].rearrange("p (k n) -> p k n", k=KD)
                rows = slice(P * tt, P * tt + P)
                pe.wait_ge(hi_ready, n + 1)
                for k in range(KD):
                    mm(ps[:].rearrange("p (j n) -> p j n", j=2), hi[:, k, rows], w_h[:, k], start=(k == 0), stop=False)
                wait_lo(what, 1)
                for k in range(KD):
                    mm(ps[:], hi[:, k, rows], w_l[:, k, :], start=False, stop=False)
                pe.wait_ge(*lo_there)
                for k in range(KD):
                    ins = mm(ps[:].rearrange("p (j n) -> p j n", j=2), lo[:, k, rows], w_h[:, k], start=False,
                             stop=(k == KD - 1))
                end(ins)

            split_T("f1", FB, 1)
            for j in range(2):
                split_T(f"q{j}", QB, j)
            for tt in range(TT):
                split(f"qa{tt}", QA, tt)
            for tt in range(TT):
                split(f"ka{tt}", KA, tt)

            def level(name):
                if name == "D":
                    pe.wait_ge(qk_ready, 1)
                    lhs, rhs = h3(kf), h3(qs)
                elif name == "X":
                    pe.wait_ge(kx_ready, 1)
                    lhs = rhs = h3(KX)
                else:
                    n = LEVELS.index(int(name[1]))
                    pe.wait_ge(kq_ready, n + 1)
                    lhs = rhs = h3(KQ[n % 2])
                ps = begin(name)
                C = CHUNK
                for h in range(GH):
                    if name == "X":
                        ins = mm(ps[:, P * h:P * h + P], lhs[:, h, 0:P], rhs[:, h, P:T], start=True, stop=True)
                    elif name == "L6":
                        for b in range(2):
                            ins = mm(ps[C * b:C * b + C, C * h:C * h + C], lhs[:, h, P * b:P * b + C],
                                     rhs[:, h, P * b + C:P * b + P], start=True, stop=True)
                    else:
                        for b in range(2):
                            for o in (0, C):
                                c = slice(P * b + o, P * b + o + C)
                                ins = mm(ps[o:o + C, C * (GH * b + h):C * (GH * b + h) + C], lhs[:, h, c], rhs[:, h, c],
                                         start=True, stop=True)
                end(ins)

            for name in ("D", "X", "L6"):
                level(name)
            split("va0", VA, 0)
            level("L5")
            level("L4")
            split("va1", VA, 1)
            level("L3")
            level("L2")
            split("ib0", IB, 0)
            level("L1")
            level("L0")
            split("ib1", IB, 1)

            for raw, u, roped in ((qraw, "qT", q_roped), (kraw, "kT", k_roped)):
                pe.wait_ge(roped, TT)
                for j in range(2):
                    ps = begin(f"{u}{j}")
                    for a in range(2):
                        for tt in range(TT):
                            c = 512 * tt + P * (2 * j + a)
                            ins = tr(ps[:, T * a + P * tt:T * a + P * tt + P], raw[:, c:c + P], ident)
                    end(ins)

            def probs_T(h):
                ps = begin(f"pT{h}")
                pe.wait_ge(prob_ready, h + 1)
                for a in range(3):
                    ins = tr(ps[:, P * a:P * a + P], SM[:, h % 2, P * a:P * a + P], ident)
                end(ins)

            split_T(*GATES[0])
            wait_drained(pe, "kT1")
            for h in range(HEADS):
                ps = begin(f"sc{h}")
                r = slice(64 * (h % 2), 64 * (h % 2) + 64)
                for c, q, k in ((0, 0, 0), (128, 1, 1), (256, 1, 0)):
                    ins = mm(ps[:, c:c + P], qT[r, h // 2, P * q:P * q + P], kT[r, h // 2, P * k:P * k + P],
                             start=True, stop=True)
                end(ins)
                if h >= 1:
                    split_T(*GATES[h])
                if h >= 1:
                    probs_T(h - 1)

            wait_drained(pe, "ib1")
            wait_drained(pe, "L0")
            wait_drained(pe, "X")
            for j in range(2):
                ps = begin(f"o{j}")
                for a in range(2):
                    h = 2 * j + a
                    c = slice(P * h, P * h + P)
                    mm(ps[:, T * a:T * a + P], ib[:, 0, c], AT[:, 0, h, :], start=True, stop=True)
                    mm(ps[:, T * a + P:T * a + T], ib[:, 1, c], AT[:, 1, h, :], start=True, stop=False)
                    ins = mm(ps[:, T * a + P:T * a + T], ib[:, 0, c], CT[:, h, :], start=False, stop=True)
                end(ins)
            split_T(*GATES[8])
            probs_T(7)
            for j in range(2):
                ps = begin(f"ms{j}")
                pe.wait_ge(osq_ready, j + 1)
                end(mm(ps[:], ones, sq[:, 512 * j:512 * j + 512], start=True, stop=True))
            wait_drained(pe, "pT7")
            for j in range(2):
                ps = begin(f"ya{j}")
                for a in range(2):
                    for q, k, c in ((0, 0, 0), (1, 1, 128), (1, 0, 256)):
                        for f in range(2):
                            h = 4 * j + 2 * a + f
                            ins = mm(ps[64 * f:64 * f + 64, T * a + P * q:T * a + P * q + P],
                                     va[:, k, 64 * h:64 * h + 64], PT[:, h, c:c + P], start=(c < 256), stop=(c != 128))
                end(ins)
            split_T(*GATES[9])
            wait_drained(pe, "ya1")
            for j in range(4):
                split_T(f"mu{j}", "mu", j, ya_hi, ya_lo, (ya_lo_ready, 2), kn=4)
            pe.wait_ge(o_hi_ready, 1)
            for j in range(4):
                split_T(f"hu{j}", "hu", j, o_hi, o_lo, (yb_ready, 1), kn=4)
            for name in ("wo00", "wo10"):
                proj(name, "wo0", int(name[2]), src=mixT)
            pe.wait_ge(mix_hi_ready, 4)
            for name in ("wo01", "wo11"):
                split(name, "wo1", int(name[2]), mix_hi, mix_lo, (mix_lo_ready, 1))
            pe.wait_ge(xn2_ready, 2)
            transposed("h2T00", 0, 0)
            transposed("h2T01", 0, 1)

            def keep_clock(n, free_bank):
                for _ in range(n):
                    mm(free_bank[:], ident, CST[:, 0:512], start=True, stop=True)

            def logits_T(tt):
                ps = begin(f"rt{tt}")
                pe.wait_ge(router_loaded, 32)
                for k in range(KD):
                    if k % 4 == 0:
                        wait_drained(pe, f"h2T{tt}{k // 4}")
                    ins = mm(ps[0:E, 0:P], RW[:, k, :], HT[:, k, P * tt:P * tt + P], start=(k == 0), stop=(k == KD - 1))
                end(ins)

            logits_T(0)
            keep_clock(1, bank("h2T10"))
            for j in range(2):
                pe.wait_ge(xn2_ready, 3 + j)
                transposed(f"h2T1{j}", 1, j)
            logits_T(1)

            ps = begin("rt")
            for tt in range(TT):
                wait_drained(pe, f"rt{tt}")
                ins = tr(ps[:, E * tt:E * tt + E], lgT[:, P * tt:P * tt + P], ident[0:E, 0:E])
            end(ins)
            wait_drained(pe, "h2T10")
            keep_clock(2, bank("h2T10"))
            ps = begin("pos")
            pe.wait_ge(mask_ready, 1)
            mm(ps[:, 0:2 * E], ucum, mask.rearrange("p t e -> p (t e)"), start=True, stop=False)
            end(mm(ps[:, E:2 * E], ones, mask[:, 0, :], start=False, stop=True))
            ps = begin("all")
            for tt in range(TT):
                ins = mm(ps[:, 0:E], ones, mask[:, tt, :], start=(tt == 0), stop=(tt == TT - 1))
            end(ins)
            ps = begin("wT")
            pe.wait_ge(wts_ready, 1)
            for tt in range(TT):
                ins = tr(ps[0:E, P * tt:P * tt + P], wts[:, tt, 0:E], ident)
            end(ins)

            def gather(p):
                pe.wait_ge(sel_ready, p + 1)
                for part, dst in enumerate((gath, multi if isinstance(p, int) and p == 0 else gu[0])):
                    for a in range(4):
                        k = 4 * part + a
                        for tt in range(TT):
                            ins = mm(dst[:, P * a:P * a + P], XN[:, tt, P * k:P * k + P], sel[:, tt, :],
                                     start=(tt == 0), stop=(tt == TT - 1))
                    ins.then_inc(gath_filled, 1)

            def combine():
                for tt in range(TT):
                    for n in range(2):
                        mm(acc[tt][n][:], selT[:, P * tt:P * tt + P], Y[:, 512 * n:512 * n + 512],
                           start=False, stop=True, skip_group_check=True)

            def arrived(q, m, opening):
                if opening and m == SLOTS:
                    pe.wait_ge(kept_loaded, 64)
                    return None
                slot, before = (m, 0) if opening and m < SLOTS else ((m - 1) % SLOTS, q * 3 + (m - 1) // SLOTS)
                pe.wait_ge(slot_loaded[slot], before * 16 + 16)
                return slot

            def gate_up(q, i, m, b, opening, final=False):
                tok = slice(CAP * b, CAP * b + CAP)

                def one(half, k, slot, kk):
                    for g in range(2):
                        c = 1024 * g + 512 * half
                        w = kept[2 * kk + g][:, c - 1024 * g:c - 1024 * g + 512] if slot is None else \
                            gu_slot[slot][:, kk, c:c + 512]
                        ins = mm(gu[half][64 * g:64 * g + 64, :], hTe[:, k, tok], w, start=(k == 0), stop=(k == KD - 1))
                    return ins

                for s in range(4):
                    if opening and m == 0 and s == 2:
                        pe.wait_ge(hTe_ready, 2)
                    slot = arrived(q, m + s, opening)
                    if s < 3:
                        for kk in range(2):
                            for half in range(2):
                                if s == 0 and kk == 0:
                                    pe.wait_ge(gu_drained, i * 2 + half + 1)
                                ins = one(half, 2 * s + kk, slot, kk)
                        ins.then_inc(weights_used, 1)
                        if s == 1 and final:
                            keep_clock(2, gath)
                        if s == 2:
                            for half in range(2):
                                for g in range(2):
                                    c = 1024 * g + 512 * half
                                    mm(gu[half][64 * g:64 * g + 64, :], onehot[:, b, :], GU_B[:, c:c + 512],
                                       start=False, stop=False)
                    else:
                        for half in range(2):
                            for kk in range(2):
                                ins = one(half, 6 + kk, slot, kk)
                            ins.then_inc(gu_filled, 1)

            def down(q, i, m, opening, final=False):
                pe.wait_ge(act_ready, i * 2 + 2)
                pe.wait_ge(y_ready, i + 1)
                for c in range(4):
                    ins = tr(multi[:, P * c:P * c + P], act[:, P * c:P * c + P], ident)
                ins.then_inc(actT_filled, 1)
                pe.wait_ge(actT_ready, i + 1)
                for kh in range(2):
                    slot = arrived(q, m + kh, opening)
                    for k in range(4):
                        if final and kh == 1 and k == 2:
                            pe.wait_ge(last_loaded, 16)
                        for n in range(2):
                            ins = mm(multi[64 * n:64 * n + 64, :], actT[:, k, 64 * kh:64 * kh + 64],
                                     dn_slot[slot][:, k, 512 * n:512 * n + 512], start=(kh == 0 and k == 0),
                                     stop=(kh == 1 and k == 3))
                    ins.then_inc(y_filled if kh else weights_used, 1)

            def four(q, first=None):
                for h in range(2):
                    p, i, m = q * 2 + h, q * 4 + 2 * h, 12 * h
                    opening = first == "biases"
                    pe.wait_ge(hTe_ready, 1 if opening and h == 0 else p * 2 + 2)
                    gate_up(q, i, m, 0, opening)
                    if h == 1 or first != "biases":
                        pe.wait_ge(y_ready, i + 1)
                        combine()
                    else:
                        for tt in range(TT):
                            for n in range(2):
                                mm(acc[tt][n][:], wT[:, P * tt:P * tt + P], DN_B[:, 512 * n:512 * n + 512],
                                   start=True, stop=True, skip_group_check=True)
                    down(q, i, m + 4, opening)
                    gate_up(q, i + 1, m + 6, 1, opening, final=(h == 1 and first == "final"))
                    pe.wait_ge(selw_ready, p + 1)
                    pe.wait_ge(y_ready, i + 2)
                    for tt in range(TT):
                        ins = tr(multi[:, P * tt:P * tt + P], selw[:, tt, :], ident)
                    ins.then_inc(selT_filled, 1)
                    if h == 0 or first not in ("last", "final"):
                        pe.wait_ge(gu_drained, i * 2 + 5)
                        gather(p + 1)
                    else:
                        keep_clock(2, gath)
                    pe.wait_ge(selT_drained, p + 1)
                    down(q, i + 1, m + 10, opening, final=(h == 1 and first == "final"))

            keep_clock(1, bank("rt0"))
            gather(0)
            wait_drained(pe, "wT")
            pe.wait_ge(moe_small_loaded, 48)
            pe.wait_ge(rounds_ready, 1)
            most = pe.value_load(CMI[0:1, 0:1], min_val=0, max_val=T)
            four(0, "biases")
            with pe.Fori(1, E // 4 - 1) as q:
                four(q)
            four(E // 4 - 1, "final")
            keep_clock(1, gath)
            pe.wait_ge(y_ready, E + 1)
            with pe.If(most > CAP):
                with pe.Fori(1, ROUNDS) as r:
                    with pe.If(most > r * CAP):
                        pe.wait_ge(gu_drained, r * (2 * E) + 2)
                        gather(r * (E // 2))
                        with pe.Fori(0, E // 4 - 1) as q:
                            four(r * (E // 4) + q)
                        four(r * (E // 4) + (E // 4 - 1), "last")
                        pe.wait_ge(y_ready, (r + 1) * E + 1)
            for tt in range(TT):
                for n in range(2):
                    ins = mm(acc[tt][n][:], selT[:, P * tt:P * tt + P], Y[:, 512 * n:512 * n + 512],
                             start=False, stop=True, skip_group_check=True)
                ins.then_inc(moe_done, 1)


_INS = ['x', 'norm1_w', 'w_in', 'moba_up', 'hgrn_lb_logits', 'hgrn_norm_w', 'hgrn_up', 'w_out', 'norm2_w', 'router_w',
        'router_b', 'w_gate_up', 'b_gate_up', 'w_down', 'b_down', 'final_norm_w']


def shape_constants():
    import numpy as np
    c = np.zeros((P, 1152), np.float32)
    r = np.arange(P)
    c[:, 0:128] = np.eye(P)
    c[:, 128:256] = r[:, None] < r[None, :]
    c[:, 256:384] = 1 + r[None, :] % CAP
    own = np.where(r[None, :] <= r[:, None], 0.0, NEG)
    c[:, 384:512] = own
    c[:, 512:640] = own
    inv = (np.float32(10000.0) ** (-(np.arange(32, dtype=np.float32) * np.float32(2.0) / np.float32(DH)))).astype(np.float32)
    ang = (np.arange(T, dtype=np.float32)[:, None] * inv[None, :]).astype(np.float32)
    for t in range(TT):
        c[:, 768 + 32 * t:800 + 32 * t] = np.cos(ang[P * t:P * t + P])
        c[:, 832 + 32 * t:864 + 32 * t] = np.sin(ang[P * t:P * t + P])
    c[0:E, 896:896 + E] = np.eye(E)
    c[:, 1024:1152] = 1.0
    m = np.zeros((P, NMASK, CHUNK), np.int32)
    step, other = r[:, None] % CHUNK, r[None, 0:CHUNK]
    for lv in range(6):
        m[:, lv] = (((step ^ other) >> lv) == 1) & (step < other)
    m[:, DIAG] = step == other
    return c, m.reshape(P, NMASK * CHUNK)


def kernel(**inputs):
    import numpy as _np
    import concourse.bacc as _bacc
    from concourse import mybir as _mybir
    from concourse.bass_utils import run_bass_kernel_spmd as _run

    nc = _bacc.Bacc("TRN2", target_bir_lowering=False, num_devices=1)
    cst, lmask = shape_constants()
    arrays, args = {}, {}
    for name, a in [(n, _np.ascontiguousarray(inputs[n])) for n in _INS] + [("cst", cst), ("lmask", lmask)]:
        arrays[f"in_{name}_dram"] = a
        args[name] = nc.dram_tensor(f"in_{name}_dram", a.shape, _mybir.dt.from_np(a.dtype), kind="ExternalInput").ap()
    out = nc.dram_tensor("out_0_dram", (1, T, D), F32, kind="ExternalOutput").ap()
    hybrid_block(nc, args, out)
    r = _run(nc, [arrays], core_ids=[0])
    return r.results[0]["out_0_dram"]
```
